# Optimizing a Trainium2 kernel written in Bass

```python
import math
import jax, jax.numpy as jnp
from jax import lax
import numpy as np

D_MODEL = 1024
BATCH = 1
SEQ = 512
DEPTH = 1

HEAD_DIM = 64
D_MIX = D_MODEL
A_HEADS = D_MIX // 2 // HEAD_DIM
A_KV = A_HEADS // 4
B_HEADS = D_MIX // 2 // HEAD_DIM
B_KV = B_HEADS // 4
D_A = A_HEADS * HEAD_DIM
D_B = B_HEADS * HEAD_DIM
KV_A = A_KV * HEAD_DIM
KV_B = B_KV * HEAD_DIM
N_HEADS_TOTAL = A_HEADS + B_HEADS
SWA_WINDOW = 128
ATTN_BLOCK = 128
CMP_LEN = 32
CMP_STRIDE = 16
CMP_HIDDEN = 256
SEL_LEN = 64
SEL_TOPK = 16
NSA_WINDOW = 512
NSA_Q_CHUNK = 32
N_NSA_BRANCHES = 3
N_BUCKETS = 32
MAX_DISTANCE = 128
FORCE_BONUS = 1e4
EPS = 1e-6
PROJ_SIZES = (D_A, KV_A, KV_A, D_A,
              D_B, KV_B, KV_B, KV_B, KV_B, KV_B, KV_B, D_B, B_HEADS * N_NSA_BRANCHES)
D_PROJ = sum(PROJ_SIZES)


def _split_points():
    pts, acc = [], 0
    for s in PROJ_SIZES[:-1]:
        acc += s
        pts.append(acc)
    return pts

def rms_norm(x, gain):
    xf = x.astype(jnp.float32)
    y = xf * lax.rsqrt(jnp.mean(xf * xf, -1, keepdims=True) + EPS)
    return (y * gain.astype(jnp.float32)).astype(x.dtype)

def qk_norm(t, gain):
    tf = t.astype(jnp.float32)
    return tf * lax.rsqrt(jnp.mean(tf * tf, -1, keepdims=True) + EPS) * gain.astype(jnp.float32)

def t5_bucket(dist):
    n = jnp.maximum(dist, 0)
    max_exact = N_BUCKETS // 2
    nf = jnp.maximum(n, 1).astype(jnp.float32)
    large = max_exact + (jnp.log(nf / max_exact) / math.log(MAX_DISTANCE / max_exact)
                         * (N_BUCKETS - max_exact)).astype(jnp.int32)
    large = jnp.minimum(large, N_BUCKETS - 1)
    return jnp.where(n < max_exact, n, large)

def masked_softmax(logits, mask, sink=None):
    z = jnp.where(mask, logits, -jnp.inf)
    m = jnp.max(z, -1, keepdims=True)
    if sink is not None:
        m = jnp.maximum(m, sink)
    m = jnp.where(jnp.isfinite(m), m, 0.0)
    e = jnp.where(mask, jnp.exp(z - m), 0.0)
    denom = jnp.sum(e, -1, keepdims=True)
    if sink is not None:
        denom = denom + jnp.exp(sink - m)
    return e / jnp.maximum(denom, 1e-30)

def banded_gqa(q, k, v, window, head_bias, sinks):
    Bn, S, H, D = q.shape
    G = k.shape[2]
    R = H // G
    nblk = S // ATTN_BLOCK
    span = window + ATTN_BLOCK
    kp = jnp.pad(k.astype(jnp.float32), ((0, 0), (window, 0), (0, 0), (0, 0)))
    vp = jnp.pad(v.astype(jnp.float32), ((0, 0), (window, 0), (0, 0), (0, 0)))
    qb = q.reshape(Bn, nblk, ATTN_BLOCK, G, R, D).transpose(1, 0, 2, 3, 4, 5)
    hb = head_bias.astype(jnp.float32)
    sink = None if sinks is None else sinks.astype(jnp.float32).reshape(G, R, 1, 1)
    q_off = jnp.arange(ATTN_BLOCK)
    k_off = jnp.arange(span)

    def block(args):
        qi, i = args
        start = i * ATTN_BLOCK
        kb = lax.dynamic_slice_in_dim(kp, start, span, axis=1)
        vb = lax.dynamic_slice_in_dim(vp, start, span, axis=1)
        t = start + q_off
        s = start - window + k_off
        dist = t[:, None] - s[None, :]
        mask = (dist >= 0) & (dist < window) & (s[None, :] >= 0)
        bias = hb[t5_bucket(dist)].reshape(ATTN_BLOCK, span, G, R).transpose(2, 3, 0, 1)
        logits = jnp.einsum('btgrd,bsgd->bgrts', qi, kb) + bias
        p = masked_softmax(logits, mask, sink)
        return jnp.einsum('bgrts,bsgd->btgrd', p, vb)

    out = lax.map(block, (qb, jnp.arange(nblk)))
    return out.transpose(1, 0, 2, 3, 4, 5).reshape(Bn, S, H, D)

def compress_blocks(t, pos, w1, w2):
    Bn, S, G, D = t.shape
    nc = (S - CMP_LEN) // CMP_STRIDE + 1
    idx = jnp.arange(nc)[:, None] * CMP_STRIDE + jnp.arange(CMP_LEN)[None, :]
    blocks = t[:, idx] + pos[None, None, :, None, :]
    flat = blocks.transpose(0, 1, 3, 2, 4).reshape(Bn, nc, G, CMP_LEN * D)
    return jax.nn.silu(flat @ w1) @ w2

def nsa_cmp_sel(q, k_cmp, v_cmp, k_sel, v_sel, head_bias):
    Bn, S, H, D = q.shape
    G = k_sel.shape[2]
    R = H // G
    nc = k_cmp.shape[1]
    ns = S // SEL_LEN
    topk = min(SEL_TOPK, ns)
    qc_len = NSA_Q_CHUNK
    nch = S // qc_len
    kc = k_cmp.astype(jnp.float32)
    vc = v_cmp.astype(jnp.float32)
    ks_b = k_sel.astype(jnp.float32).reshape(Bn, ns, SEL_LEN, G, D).transpose(0, 3, 1, 2, 4)
    vs_b = v_sel.astype(jnp.float32).reshape(Bn, ns, SEL_LEN, G, D).transpose(0, 3, 1, 2, 4)
    c_lo = jnp.arange(nc) * CMP_STRIDE
    c_end = c_lo + CMP_LEN - 1
    s_lo = jnp.arange(ns) * SEL_LEN
    overlap = jnp.clip(jnp.minimum(c_lo[:, None] + CMP_LEN, s_lo[None, :] + SEL_LEN)
                       - jnp.maximum(c_lo[:, None], s_lo[None, :]), 0, None).astype(jnp.float32) / CMP_LEN
    tbl = head_bias.astype(jnp.float32).reshape(N_BUCKETS, G, R).transpose(1, 0, 2)
    g_idx = jnp.arange(G)[None, :, None, None]
    blk = jnp.arange(ns)
    gather = jax.vmap(jax.vmap(lambda kb, ix: kb[ix]))
    qch = q.reshape(Bn, nch, qc_len, G, R, D).transpose(1, 0, 2, 3, 4, 5)

    def chunk(args):
        qi, i = args
        t = i * qc_len + jnp.arange(qc_len)
        logits_c = jnp.einsum('btgrd,bngd->bgrtn', qi, kc)
        p_c = masked_softmax(logits_c, c_end[None, :] <= t[:, None])
        o_cmp = jnp.einsum('bgrtn,bngd->btgrd', p_c, vc)
        imp = jnp.einsum('bgrtn,nj->bgtj', p_c, overlap)
        cur = t // SEL_LEN
        valid = blk[None, :] <= cur[:, None]
        forced = (blk[None, :] == 0) | (blk[None, :] == cur[:, None]) | (blk[None, :] == cur[:, None] - 1)
        score = jnp.where(valid, imp + jnp.where(forced, FORCE_BONUS, 0.0), -jnp.inf)
        _, sel = lax.top_k(score, topk)
        kg = gather(ks_b, sel).reshape(Bn, G, qc_len, topk * SEL_LEN, D)
        vg = gather(vs_b, sel).reshape(Bn, G, qc_len, topk * SEL_LEN, D)
        spos = (sel[..., None] * SEL_LEN + jnp.arange(SEL_LEN)).reshape(Bn, G, qc_len, topk * SEL_LEN)
        dist = t[None, None, :, None] - spos
        bias = tbl[g_idx, t5_bucket(dist)].transpose(0, 1, 4, 2, 3)
        logits_s = jnp.einsum('btgrd,bgtld->bgrtl', qi, kg) + bias
        p_s = masked_softmax(logits_s, (dist >= 0)[:, :, None])
        o_sel = jnp.einsum('bgrtl,bgtld->btgrd', p_s, vg)
        return o_cmp, o_sel

    o_cmp, o_sel = lax.map(chunk, (qch, jnp.arange(nch)))
    o_cmp = o_cmp.transpose(1, 0, 2, 3, 4, 5).reshape(Bn, S, H, D)
    o_sel = o_sel.transpose(1, 0, 2, 3, 4, 5).reshape(Bn, S, H, D)
    return o_cmp, o_sel

def hybrid_layer(x, c, w_ada, b_ada, norm_gain, w_in, b_nsa_gate, q_gain_a, k_gain_a, sinks,
                 q_gain_b, k_gain_cmp, k_gain_sel, k_gain_win, cmp_pos_k, cmp_pos_v,
                 w_cmp_k1, w_cmp_k2, w_cmp_v1, w_cmp_v2, w_out, rel_bias):
    Bn, S, _ = x.shape
    qscale = HEAD_DIM ** -0.5
    mod = jax.nn.silu(c) @ w_ada + b_ada
    shift, scale, gate = jnp.split(mod, 3, axis=-1)
    h = rms_norm(x, norm_gain) * (1 + scale[:, None, :]) + shift[:, None, :]
    proj = h @ w_in
    (q_a, k_a, v_a, z_a, q_b, kc, vc, ks, vs, kw, vw, z_b, g_b) = jnp.split(proj, _split_points(), axis=-1)
    heads = lambda t, n: t.reshape(Bn, S, n, HEAD_DIM)

    qa = qk_norm(heads(q_a, A_HEADS), q_gain_a) * qscale
    ka = qk_norm(heads(k_a, A_KV), k_gain_a)
    o_a = banded_gqa(qa, ka, heads(v_a, A_KV), SWA_WINDOW, rel_bias[:, :A_HEADS], sinks)

    bias_b = rel_bias[:, A_HEADS:]
    qb = qk_norm(heads(q_b, B_HEADS), q_gain_b) * qscale
    k_cmp = qk_norm(compress_blocks(heads(kc, B_KV), cmp_pos_k, w_cmp_k1, w_cmp_k2), k_gain_cmp)
    v_cmp = compress_blocks(heads(vc, B_KV), cmp_pos_v, w_cmp_v1, w_cmp_v2)
    k_sel = qk_norm(heads(ks, B_KV), k_gain_sel)
    k_win = qk_norm(heads(kw, B_KV), k_gain_win)
    o_cmp, o_sel = nsa_cmp_sel(qb, k_cmp, v_cmp, k_sel, heads(vs, B_KV), bias_b)
    o_win = banded_gqa(qb, k_win, heads(vw, B_KV), NSA_WINDOW, bias_b, None)
    gb = jax.nn.sigmoid((g_b + b_nsa_gate).astype(jnp.float32)).reshape(Bn, S, B_HEADS, N_NSA_BRANCHES, 1)
    o_b = gb[..., 0, :] * o_cmp + gb[..., 1, :] * o_sel + gb[..., 2, :] * o_win

    y = jnp.concatenate([o_a.reshape(Bn, S, D_A) * jax.nn.silu(z_a.astype(jnp.float32)),
                         o_b.reshape(Bn, S, D_B) * jax.nn.silu(z_b.astype(jnp.float32))], axis=-1)
    out = y.astype(x.dtype) @ w_out
    return x + gate[:, None, :] * out

def first_inputs(seed: int = 0) -> dict:
    key = jax.random.key(seed)
    ks = jax.random.split(key, 24)
    nrm = lambda k, shape, s: jax.random.normal(k, shape, jnp.float32) * s
    gain = lambda k, shape: 1.0 + 0.1 * jax.random.normal(k, shape, jnp.float32)
    L = DEPTH
    return {
        "x": nrm(ks[0], (BATCH, SEQ, D_MODEL), 1.0),
        "c": nrm(ks[1], (BATCH, D_MODEL), 1.0),
        "w_ada": nrm(ks[2], (L, D_MODEL, 3 * D_MODEL), 0.5 * D_MODEL ** -0.5),
        "b_ada": nrm(ks[3], (L, 3 * D_MODEL), 0.01),
        "norm_gain": gain(ks[4], (L, D_MODEL)),
        "w_in": nrm(ks[5], (L, D_MODEL, D_PROJ), D_MODEL ** -0.5),
        "b_nsa_gate": nrm(ks[6], (L, B_HEADS * N_NSA_BRANCHES), 0.1),
        "q_gain_a": gain(ks[7], (L, HEAD_DIM)),
        "k_gain_a": gain(ks[8], (L, HEAD_DIM)),
        "sinks": nrm(ks[9], (L, A_HEADS), 1.0),
        "q_gain_b": gain(ks[10], (L, HEAD_DIM)),
        "k_gain_cmp": gain(ks[11], (L, HEAD_DIM)),
        "k_gain_sel": gain(ks[12], (L, HEAD_DIM)),
        "k_gain_win": gain(ks[13], (L, HEAD_DIM)),
        "cmp_pos_k": nrm(ks[14], (L, CMP_LEN, HEAD_DIM), 0.5),
        "cmp_pos_v": nrm(ks[15], (L, CMP_LEN, HEAD_DIM), 0.5),
        "w_cmp_k1": nrm(ks[16], (L, CMP_LEN * HEAD_DIM, CMP_HIDDEN), (CMP_LEN * HEAD_DIM) ** -0.5),
        "w_cmp_k2": nrm(ks[17], (L, CMP_HIDDEN, HEAD_DIM), CMP_HIDDEN ** -0.5),
        "w_cmp_v1": nrm(ks[18], (L, CMP_LEN * HEAD_DIM, CMP_HIDDEN), (CMP_LEN * HEAD_DIM) ** -0.5),
        "w_cmp_v2": nrm(ks[19], (L, CMP_HIDDEN, HEAD_DIM), CMP_HIDDEN ** -0.5),
        "w_out": nrm(ks[20], (L, D_MIX, D_MODEL), D_MIX ** -0.5),
        "rel_bias": nrm(ks[21], (N_BUCKETS, N_HEADS_TOTAL), 0.5),
    }

def first_block(x, c, w_ada, b_ada, norm_gain, w_in, b_nsa_gate, q_gain_a, k_gain_a, sinks,
              q_gain_b, k_gain_cmp, k_gain_sel, k_gain_win, cmp_pos_k, cmp_pos_v,
              w_cmp_k1, w_cmp_k2, w_cmp_v1, w_cmp_v2, w_out, rel_bias):
    for l in range(DEPTH):
        x = hybrid_layer(x, c, w_ada[l], b_ada[l], norm_gain[l], w_in[l], b_nsa_gate[l],
                         q_gain_a[l], k_gain_a[l], sinks[l], q_gain_b[l], k_gain_cmp[l],
                         k_gain_sel[l], k_gain_win[l], cmp_pos_k[l], cmp_pos_v[l],
                         w_cmp_k1[l], w_cmp_k2[l], w_cmp_v1[l], w_cmp_v2[l], w_out[l], rel_bias)
    return x


CONV_WIDTH = D_MODEL
CONV_K = 3
RET_HEADS = 4
RET_QK_DIM = D_MODEL // RET_HEADS
RET_V_DIM = 2 * RET_QK_DIM
RET_QK = RET_HEADS * RET_QK_DIM
RET_V = RET_HEADS * RET_V_DIM
CHUNK = 128
ROPE_BASE = 10000.0
D_FF = -(-8 * D_MODEL // (3 * 256)) * 256
IN_SIZES = (CONV_WIDTH, CONV_WIDTH, CONV_WIDTH, RET_QK, RET_QK, RET_V, RET_V, D_MODEL, D_MODEL)
N_IN = sum(IN_SIZES)


def rmsnorm(x, g):
    xf = x.astype(jnp.float32)
    y = xf * lax.rsqrt(jnp.mean(xf * xf, axis=-1, keepdims=True) + EPS)
    return (y * g.astype(jnp.float32)).astype(x.dtype)

def rotary(t):
    s, d = t.shape[1], t.shape[-1]
    pos = jnp.arange(s, dtype=jnp.float32)
    freqs = ROPE_BASE ** (-jnp.arange(0, d, 2, dtype=jnp.float32) / d)
    ang = pos[:, None] * freqs[None, :]
    cos = jnp.cos(ang)[None, :, None, :]
    sin = jnp.sin(ang)[None, :, None, :]
    t1, t2 = t[..., : d // 2], t[..., d // 2:]
    return jnp.concatenate([t1 * cos - t2 * sin, t1 * sin + t2 * cos], axis=-1)

def retention_chunkwise(q, k, v, log_gamma, strict):
    b, h, s, dk = q.shape
    dv = v.shape[-1]
    n_chunks = s // CHUNK

    def chunks(t):
        return jnp.moveaxis(t.reshape(b, h, n_chunks, CHUNK, t.shape[-1]), 2, 0)

    idx = jnp.arange(CHUNK, dtype=jnp.float32)
    diff = idx[:, None] - idx[None, :]
    mask = (diff > 0) if strict else (diff >= 0)
    lg = log_gamma[:, None, None]
    intra_decay = jnp.where(mask[None], jnp.exp(jnp.maximum(diff, 0.0)[None] * lg), 0.0)
    xi = jnp.exp((idx + 1.0)[None, :] * log_gamma[:, None])[..., None]
    zeta = jnp.exp((CHUNK - 1.0 - idx)[None, :] * log_gamma[:, None])[..., None]
    chunk_decay = jnp.exp(CHUNK * log_gamma)[:, None, None]

    def step(state, qkv):
        qc, kc, vc = qkv
        scores = jnp.einsum('bhcd,bhmd->bhcm', qc, kc) * intra_decay
        inner = jnp.einsum('bhcm,bhme->bhce', scores, vc)
        cross = jnp.einsum('bhcd,bhde->bhce', qc, state) * xi
        state = chunk_decay * state + jnp.einsum('bhcd,bhce->bhde', kc * zeta, vc)
        return state, inner + cross

    state0 = jnp.zeros((b, h, dk, dv), jnp.float32)
    _, out = lax.scan(step, state0, (chunks(q), chunks(k), chunks(v)))
    return jnp.moveaxis(out, 0, 2).reshape(b, h, s, dv)

def second_inputs(seed: int = 0) -> dict:
    key = jax.random.key(seed)
    ks = jax.random.split(key, 16)
    f32 = jnp.float32

    def normal(k, shape, scale):
        return jax.random.normal(k, shape, f32) * scale

    def gain(k, shape):
        return 1.0 + 0.05 * jax.random.normal(k, shape, f32)

    base_logit = jnp.log(2.0 ** (5.0 + jnp.arange(RET_HEADS, dtype=f32)) - 1.0)
    return {
        "x": jax.random.normal(ks[0], (BATCH, SEQ, D_MODEL), f32),
        "g_mix": gain(ks[1], (DEPTH, D_MODEL)),
        "w_in": normal(ks[2], (DEPTH, D_MODEL, N_IN), D_MODEL ** -0.5),
        "w_conv": normal(ks[3], (DEPTH, CONV_K, CONV_WIDTH), CONV_K ** -0.5),
        "dec_f": base_logit[None] + 0.01 * jax.random.normal(ks[4], (DEPTH, RET_HEADS), f32),
        "dec_b": base_logit[None] + 0.01 * jax.random.normal(ks[5], (DEPTH, RET_HEADS), f32),
        "g_ret": gain(ks[6], (DEPTH, RET_V)),
        "w_a_out": normal(ks[7], (DEPTH, CONV_WIDTH, D_MODEL), CONV_WIDTH ** -0.5),
        "w_r_out": normal(ks[8], (DEPTH, RET_V, D_MODEL), RET_V ** -0.5),
        "w_o": normal(ks[9], (DEPTH, D_MODEL, D_MODEL), D_MODEL ** -0.5),
        "g_ffn": gain(ks[10], (DEPTH, D_MODEL)),
        "w_ff_gate": normal(ks[11], (DEPTH, D_MODEL, D_FF), D_MODEL ** -0.5),
        "w_ff_up": normal(ks[12], (DEPTH, D_MODEL, D_FF), D_MODEL ** -0.5),
        "w_ff_down": normal(ks[13], (DEPTH, D_FF, D_MODEL), D_FF ** -0.5),
        "g_final": gain(ks[14], (D_MODEL,)),
    }

def second_block(x, g_mix, w_in, w_conv, dec_f, dec_b, g_ret, w_a_out, w_r_out, w_o,
              g_ffn, w_ff_gate, w_ff_up, w_ff_down, g_final):
    b, s, _ = x.shape
    dt = x.dtype
    split_points = [int(p) for p in np.cumsum(IN_SIZES)[:-1]]
    for l in range(DEPTH):
        h = rmsnorm(x, g_mix[l])
        proj = h @ w_in[l]
        xc, gb, gc, q, k, v, g_sw, gate_a, gate_r = jnp.split(proj, split_points, axis=-1)

        u = gc * xc
        u_pad = jnp.pad(u, ((0, 0), (CONV_K // 2, CONV_K // 2), (0, 0)))
        conv = u_pad[:, 0:s] * w_conv[l, 0]
        for tap in range(1, CONV_K):
            conv = conv + u_pad[:, tap:tap + s] * w_conv[l, tap]
        y_a = (gb * conv) @ w_a_out[l]

        qf = rotary(q.reshape(b, s, RET_HEADS, RET_QK_DIM).astype(jnp.float32)) * (RET_QK_DIM ** -0.5)
        kf = rotary(k.reshape(b, s, RET_HEADS, RET_QK_DIM).astype(jnp.float32))
        vf = v.reshape(b, s, RET_HEADS, RET_V_DIM).astype(jnp.float32)
        qf, kf, vf = (jnp.transpose(t, (0, 2, 1, 3)) for t in (qf, kf, vf))
        lg_f = jax.nn.log_sigmoid(dec_f[l].astype(jnp.float32))
        lg_b = jax.nn.log_sigmoid(dec_b[l].astype(jnp.float32))
        ret_f = retention_chunkwise(qf, kf, vf, lg_f, strict=False)
        ret_b = jnp.flip(retention_chunkwise(jnp.flip(qf, 2), jnp.flip(kf, 2), jnp.flip(vf, 2),
                                             lg_b, strict=True), 2)
        ret = ret_f + ret_b
        mu = jnp.mean(ret, axis=-1, keepdims=True)
        var = jnp.mean(jnp.square(ret - mu), axis=-1, keepdims=True)
        ret = (ret - mu) * lax.rsqrt(var + EPS)
        ret = jnp.transpose(ret, (0, 2, 1, 3)).reshape(b, s, RET_V) * g_ret[l].astype(jnp.float32)
        y_r = (ret.astype(dt) * jax.nn.silu(g_sw)) @ w_r_out[l]

        merged = jax.nn.sigmoid(gate_a) * y_a + jax.nn.sigmoid(gate_r) * y_r
        x = x + merged @ w_o[l]

        h2 = rmsnorm(x, g_ffn[l])
        x = x + (jax.nn.silu(h2 @ w_ff_gate[l]) * (h2 @ w_ff_up[l])) @ w_ff_down[l]
    return rmsnorm(x, g_final)


def setup_inputs(seed=0):
    out = dict(first_inputs(seed))
    for name, value in second_inputs(seed + 1).items():
        if name != "x":
            out[name + "_2"] = value
    return out


def reference(
    x, c, w_ada, b_ada, norm_gain, w_in, b_nsa_gate, q_gain_a, k_gain_a, sinks, q_gain_b,
    k_gain_cmp, k_gain_sel, k_gain_win, cmp_pos_k, cmp_pos_v, w_cmp_k1, w_cmp_k2, w_cmp_v1,
    w_cmp_v2, w_out, rel_bias, g_mix_2, w_in_2, w_conv_2, dec_f_2, dec_b_2, g_ret_2, w_a_out_2,
    w_r_out_2, w_o_2, g_ffn_2, w_ff_gate_2, w_ff_up_2, w_ff_down_2, g_final_2,
):
    x = first_block(
        x, c, w_ada, b_ada, norm_gain, w_in, b_nsa_gate, q_gain_a, k_gain_a, sinks, q_gain_b,
        k_gain_cmp, k_gain_sel, k_gain_win, cmp_pos_k, cmp_pos_v, w_cmp_k1, w_cmp_k2, w_cmp_v1,
        w_cmp_v2, w_out, rel_bias,
    )
    return second_block(
        x, g_mix_2, w_in_2, w_conv_2, dec_f_2, dec_b_2, g_ret_2, w_a_out_2, w_r_out_2, w_o_2,
        g_ffn_2, w_ff_gate_2, w_ff_up_2, w_ff_down_2, g_final_2,
    )


_drawn_inputs = setup_inputs


def setup_inputs(seed=0):
    import zlib

    import numpy as np

    out = dict(_drawn_inputs(seed))
    spreads = {}
    factors = {'b_ada': 8.0,
     'norm_gain': 3.95,
     'b_nsa_gate': 8.0,
     'q_gain_a': 8.0,
     'k_gain_a': 8.0,
     'sinks': 32.564,
     'q_gain_b': 8.0,
     'k_gain_cmp': 8.0,
     'k_gain_sel': 8.0,
     'k_gain_win': 8.0,
     'cmp_pos_k': 8.0,
     'w_cmp_k1': 3.727,
     'w_cmp_k2': 3.877,
     'rel_bias': 2.795,
     'g_ret_2': 14.527,
     'g_ffn_2': 5.334}
    for name, (base, spread) in spreads.items():
        noise = np.random.default_rng([zlib.crc32(name.encode()), seed]).standard_normal(out[name].shape)
        drawn = base * np.exp(spread * noise) if base else spread * noise
        out[name] = __import__('jax').numpy.asarray(drawn.astype(out[name].dtype))
    for name, factor in factors.items():
        out[name] = (out[name] * factor).astype(out[name].dtype)
    return out
```

```python
from contextlib import ExitStack

import numpy as np

import concourse.bass as bass
from concourse import mybir

F32 = mybir.dt.float32
F32R = mybir.dt.float32r
ACT = mybir.ActivationFunctionType
ALU = mybir.AluOpType
AX = mybir.AxisListType.X

P = 128
S = 512
NI = S // P
D = 1024
KT = D // P
SLOTS = 4
AHEAD = 2
HD = 64
EPS = 1e-6
BIG = 1e30
LINE = 384
NC_PAD = 32
CMP_T = 16
RET_HEADS = 4
STRIP = S + (NI - 1) * P
D_FF = 2816
FT = D_FF // P

KC, VC, KA, VA, KS, VS, KW, VW, QA, QB, ZA, ZB = 0, 1, 2, 3, 4, 5, 6, 7, 8, 12, 16, 20
IN_COLS = [1792, 1920, 512, 640, 2048, 2176, 2304, 2432]
Q_COLS = [0, 1280]
Z_COLS = [768, 2560]
GB_COL = 3072
GA_COL, GR_COL = 9216, 10240

V_C, V_ADA, V_NORM, V_CONV, V_RET, V_MIX, V_FFN, V_FIN, V_GAIN = 0, 8, 32, 40, 64, 80, 88, 96, 104
N_VEC = 110
VEC_DMAS = 22

U_IN, U_Z, U_WO, U_CONV, U_YA, U_QKV, U_GATE, U_YR, U_O, U_FF, U_DOWN = (
    0, 16, 24, 32, 56, 72, 104, 128, 144, 152, 196)
O_IN, O_Z, O_WO, O_CONV, O_YA, O_QKV, O_GATE, O_YR, O_O, O_FF, O_DOWN = (
    0, 16, 24, 32, 56, 72, 104, 128, 136, 144, 188)
U_PAIRED = 18

NORM_TILES = [QA, QA + 1, QA + 2, QA + 3, QB, QB + 1, QB + 2, QB + 3, KA, KS, KW]
NORM_GAINS = [0, 0, 0, 0, 1, 1, 1, 1, 2, 4, 5]
NORM_GROUPS = [(0, 4), (4, 8), (8, 11)]
BCAST_AT = {19: (0, 1, 2), 20: (3, 4, 5), 21: (6, 7, 8), 22: (9, 10)}
NORM_O = [O_WO, O_O, O_DOWN]
RS_BANK = [4, 5, 6, 4]
PV_BANK = [5, 6, 7, 4]

N_GROUPS = 3 * NI
N_ATT = 8 * N_GROUPS
STEPS = N_ATT + 6


class Step:

    def __init__(self, s):
        self.group, n = divmod(s, 8)
        self.i, self.branch = divmod(self.group, 3)
        self.j, self.g = divmod(n, 2)
        self.head = 4 * self.g + self.j
        blocks = self.i + 1 if self.branch else min(2, self.i + 1)
        self.width = P * blocks
        self.first_block = self.i + 1 - blocks


def att(s):
    return Step(s)


def tail_at(s):
    i, rest = divmod(s - 5, 24)
    return i - 1 if rest == 0 and i > 0 else None


class Own:

    def __init__(self, eng, sem):
        self.eng, self.sem, self.base, self.n, self.it, self.per = eng, sem, 0, 0, None, 0

    def __call__(self, ins):
        ins.then_inc(self.sem, 1)
        self.n += 1
        return ins

    def wait(self):
        v = self.base + self.n
        self.eng.wait_ge(self.sem, v if self.it is None else self.it * self.per + v)

    def begin(self, it, per, first=0):
        self.base += self.n
        self.n, self.it, self.per = 0, it, per
        self.base -= first * per
        self.first = first

    def end(self, count):
        assert self.n == self.per, (self.n, self.per)
        self.base += self.first * self.per + count * self.per
        self.n, self.it = 0, None


def at(it, per, base):
    return base if it is None else it * per + base


def hybrid_block(nc, x, c, w_ada, b_ada, norm_gain, w_in, b_nsa_gate, q_gain_a, k_gain_a, sinks,
                 q_gain_b, k_gain_cmp, k_gain_sel, k_gain_win, cmp_pos_k, cmp_pos_v, w_cmp_k1,
                 w_cmp_k2, w_cmp_v1, w_cmp_v2, w_out, rel_bias, g_mix_2, w_in_2, w_conv_2, dec_f_2,
                 dec_b_2, g_ret_2, w_a_out_2, w_r_out_2, w_o_2, g_ffn_2, w_ff_gate_2, w_ff_up_2,
                 w_ff_down_2, g_final_2, bias_onehot, rope_cos, rope_sin, out):
    line_dram = nc.dram_tensor("bias_line", [P, 16, LINE], F32).ap()
    x1_dram = nc.dram_tensor("x1_spill", [P, KT, S], F32).ap()

    with ExitStack() as stack:
        KB = 1024
        BASE = 16512

        def sb(name, shape, kb, dt=F32):
            return nc.alloc_sbuf_tensor_at(name, shape, dt, offset=BASE + int(kb * KB))

        def sem(name):
            return stack.enter_context(nc.semaphore(name))

        raw = sb("w_raw", [P, SLOTS, KT, P], 0)
        whi = sb("w_hi", [P, SLOTS, KT, P], 16, F32R)
        wlo = sb("w_lo", [P, SLOTS, KT, P], 32, F32R)
        c_at = [48 * KB]

        def const(name, shape, dt=F32):
            t = sb(name, shape, c_at[0] / KB, dt)
            c_at[0] += (int(np.prod(shape[1:])) * 4 + 31) // 32 * 32
            return t

        ident = const("ident", [P, P])
        col = const("columns", [P, N_VEC])
        pos_col = const("pos_columns", [P, 2 * CMP_T])
        mean512 = const("ones_over_512", [P, P])
        ones1 = const("ones1", [P, 1])
        half_sel = const("half_select", [P, 2])
        minus_half = const("minus_half", [P, 1])
        csilu = const("csilu", [P, 8])
        mod = const("mod", [P, 24])
        s1 = const("norm_times_scale", [P, 8])
        gains = const("gains", [P, 6])
        line_far = const("bias_far", [P, 8])
        nsink = const("sinks_negated", [P, 8])
        gate_bias = const("gate_bias", [P, 24])
        gates = const("branch_gates", [P, NI, 24])
        sumsq = const("sum_squares", [P, NI])
        msq = const("mean_squares", [P, NI])
        rstd = const("rstd", [P, NI])
        msq_h = const("head_mean_squares", [P, 88])
        rstd_h = const("head_rstd", [P, 88])
        kcmp = const("k_compressed", [P, NC_PAD])
        kc_sq = const("k_compressed_squared", [P, NC_PAD])
        kc_ms = const("k_compressed_mean_squares", [P, 2])
        kc_rs = const("k_compressed_rstd", [P, 2])
        cmask = const("compressed_mask", [P, NI, NC_PAD])
        cmin = const("compressed_min", [P, 2, 16])
        cden = const("compressed_sum", [P, 2, 16])
        ccoef = const("compressed_coefficient", [P, NI, 8])
        w2k = sb("w_cmp_k2_twice", [P, 2, 2, HD], 56)
        w2v = sb("w_cmp_v2", [P, 2, HD], 57)
        vbd = const("v_compressed_diagonal", [P, 2, 4 * HD])
        decay = const("decay_logits", [P, 8])
        lg = const("log_decay", [P, 8])
        lt = const("log_decay_steps", [P, 5, 8])
        row_min = const("row_min", [P, 2, 8])
        den = const("row_sum", [P, 2, 8])
        sink_arg = const("sink_arg", [P, 8])
        sink_exp = const("sink_exp", [P, 8])
        coef = const("coefficient", [P, 2, 8])
        assert c_at[0] <= 56 * KB, c_at
        cos_t = sb("cos", [P, S], 56)
        sin_t = sb("sin", [P, S], 58)
        R = 60
        x_t = sb("x_t", [P, KT, S], R + 131)
        x_tok = sb("x_tok", [P, NI, D], R)
        t_h = sb("t_h", [P, KT, S], R)
        ada = sb("w_ada_shift_scale", [P, KT, 2048], R + 16)
        ada_g = sb("w_ada_gate", [P, KT, D], R + 95)
        acc = sb("ada_sum", [P, 2048], 40)
        acc_g = sb("ada_sum_gate", [P, D], R + 90)
        line = sb("bias_lines", [P, 16, LINE], 16)
        rel = sb("rel_bias_sb", [33, 16], R + 80)
        vec = sb("vec", [P, P], R + 81)
        vec2 = sb("vec2", [2 * CMP_T, P], R + 82)
        sqx = sb("sqx", [P, D], R + 83)
        onehot = sb("onehot", [33, 2, LINE], R + 87)
        band_a = sb("band_a", [P, 8, 256], R)
        band_b = sb("band_b", [P, 8, S], R + 8)
        w1 = sb("w_cmp1", [P, CMP_T, 256], R + 24)
        shifted = sb("shifted", [P, 2, S], R + 40)
        xp = sb("cmp_in", [P, CMP_T, 2, NC_PAD], R + 44)
        h_hi = sb("h_hi", [P, KT, S], R + 48, F32R)
        h_lo = sb("h_lo", [P, KT, S], R + 64, F32R)
        proj = sb("proj", [P, 24, S], R + 80)
        gb_raw = sb("gate_w", [P, KT, 24], R + 128)
        gb_hi = sb("gate_w_hi", [P, KT, 24], R + 128.75, F32R)
        gb_lo = sb("gate_w_lo", [P, KT, 24], R + 129.5, F32R)
        hid = sb("cmp_hidden", [P, 2, 64], R + 130.25)
        hid_v = sb("cmp_hidden_v", [P, 2, 2, 4, NC_PAD], R + 24)
        sc = sb("scores_sb", [P, 2, S], R + 24)
        pt = sb("probs_t", [P, 2, S], R + 28)
        ob = sb("out_b", [P, NI, S], R + 32)
        oa = sb("out_a", [P, S], R + 40)
        o_tmp = sb("out_tmp", [P, S], R + 42)
        y_f = sb("y_f", [P, 2, NI, P], R + 44)
        y_hi = sb("y_hi", [P, KT, S], R + 48, F32R)
        y_lo = sb("y_lo", [P, KT, S], R + 64, F32R)
        g_hi = sb("g_hi", [P, KT, S], R, F32R)
        g_lo = sb("g_lo", [P, KT, S], R + 16, F32R)
        ya = sb("ya", [P, KT, S], R + 32)
        conv_ev = sb("conv_evac", [P, 2, 3, S], R + 48)
        t_g = sb("t_g", [P, KT, S], R + 60)
        u_pad = sb("u_pad", [P, S + 2], R + 76.5)
        conv_t = sb("conv_t", [P, S], R + 79)
        tt = sb("temps", [P, 5, S], R + 88)
        a_hi = sb("a_hi", [P, KT, S], R + 99, F32R)
        a_lo = sb("a_lo", [P, KT, S], R + 115, F32R)
        ret = sb("ret", [P, 16, S], R + 48)
        ret_hi = sb("ret_hi", [P, 16, S], R + 48, F32R)
        ret_lo = sb("ret_lo", [P, 16, S], R + 99, F32R)
        strip = sb("strip", [P, STRIP], R + 80)
        delta = sb("delta", [P, STRIP], R + 83.5)
        strip2 = sb("strip2", [P, STRIP], R + 87)
        v_t = sb("v_t", [P, 2, S], R + 91)
        p_f = sb("p_f", [P, 2, S], R + 95)
        q_hi = sb("q_hi", [P, 2, S], R + 99, F32R)
        q_lo = sb("q_lo", [P, 2, S], R + 103, F32R)
        k_hi = sb("k_hi", [P, 2, S], R + 107, F32R)
        k_lo = sb("k_lo", [P, 2, S], R + 111, F32R)
        v_hi = sb("v_hi", [P, NI, S], R + 115, F32R)
        v_lo = sb("v_lo", [P, NI, S], R + 123, F32R)
        p_hi = sb("p_hi", [P, NI, S], R + 131, F32R)
        p_lo = sb("p_lo", [P, NI, S], R + 139, F32R)
        qk_raw = sb("qk_raw", [P, 4, S], R + 131)
        rot_t = sb("rot_t", [P, 2, S], R + 139)
        rot_o = sb("rot_o", [P, 2, S], R + 143)
        sg = sb("silu_g", [P, 4, S], R + 80)
        head_sum = sb("head_sum", [P, S], R + 88)
        head_sq = sb("head_sq", [P, 2, S], R + 90)
        head_ssq = sb("head_ssq", [P, S], R + 94)
        val = sb("ret_val", [P, S], R + 96)
        val2 = sb("ret_val2", [P, S], 56)
        val3 = sb("ret_val3", [P, S], 58)
        sig_r = sb("sigmoid_r", [P, KT, S], R + 131)
        yr_t = sb("yr_part", [P, 2, S], 56)
        mg_t = sb("merged_t", [P, S], R + 96)
        m_hi = sb("m_hi", [P, KT, S], R, F32R)
        m_lo = sb("m_lo", [P, KT, S], R + 16, F32R)
        x1_back = sb("x1_back", [P, KT, S], R + 80)
        tt_o = sb("temps_o", [P, 5, S], R + 32)
        t_f = sb("t_f", [P, KT, S], R + 48)
        f_hi = sb("f_hi", [P, KT, S], R + 99, F32R)
        f_lo = sb("f_lo", [P, KT, S], R + 115, F32R)
        act_hi = sb("act_hi", [P, FT, S], R, F32R)
        act_lo = sb("act_lo", [P, FT, S], R + 44, F32R)
        y_out = sb("y_out", [P, KT, S], R + 99)
        out_tok = sb("out_tok", [P, NI, D], R)

        ps = nc.alloc_psum_tensor("ps", [P, 8, S], F32)

        raw_in = [sem(f"raw_in{s}") for s in range(SLOTS)]
        raw_in2 = [sem(f"raw_in2_{s}") for s in range(SLOTS)]
        hi_done, lo_done = sem("hi_done"), sem("lo_done")
        unit_done = sem("unit_done")
        evac = sem("evac")
        names = ("dve_own pool_own vec_in misc_in x_in adag_in onehot_in line_out band_in w1_in sh_in "
                 "gbw_in tab_in consts csilu_done col_t col_done x_tr x_ev sumsq_done line_mm line_ev "
                 "rms_in rms_rs rms_bc ada_done mod_mm mod_done th_done hh_done hl_done adag_done modg_mm "
                 "band_fill sq_done st_mm hms_done hrs_done bc_mm qk_done gb_cv gb_cl gb_mm gb_add gb_done "
                 "xp_done c1_mm hid_done c2_mm kc_ev kcsq_done kst_mm kms_done krs_done kbc_mm kcmp_done vbd_done "
                 "vt_mm vt_ev cs_mm csub_done cexp_done ctr_mm cpt_d cpt_a co_mm co_done "
                 "s_mm s_bias s_exp t_mm pt_d pt_a pv_mm comb_done arg_done sinkexp_done ytr_mm yf_done yh_done yl_done "
                 "spill_done lgexp_done delta_done af_done ah_done al_done "
                 "lgt_done strip_done rot_done qkh_done qkl_done vtr_mm vh_done vl_done rs_mm pm_done ph_done pl_done rpv_mm "
                 "hsum_done mu_mm sub_done hsq_done hssq_done rst_mm rms2_done rrs_done rbc_mm val_done rh_done rl_done "
                 "back_in pool_own2 ob_done decay_done hpair_done ret_ev far_done mg_done mh_done ml_done prod_done fh_done fl_done fin_mm fin_a fin_d out_done").split()
        m = {n: sem(n) for n in names}
        ada_in = [sem(f"ada_in{k}") for k in range(KT // 2)]
        nrm = {n: sem(n) for n in ("x_done xsq_done ss_done nst_mm ms_done rs_done nbc_mm t_done h_done l_done").split()}

        def gate_of(branch):
            return gates[:].rearrange("p i (h b) -> p i h b", b=3)[:, :, :, branch]

        def pe_unit(pe, it, per, u, per_o, o, mov_hi, mov_lo, kts=KT, k0=0, first=True, last=True,
                    hi_sem=None, lo_sem=None, lo_all=None):
            slot, bank = u % SLOTS, ps[:, o % 4]
            pe.wait_ge(hi_done, at(it, per, u + 1))
            pe.wait_ge(lo_done, at(it, per, u + 1))
            if first and o >= 4:
                pe.wait_ge(evac, at(it, per_o, o - 3))
            passes = ((whi, mov_hi, hi_sem), (wlo, mov_hi, None), (whi, mov_lo, lo_sem))
            for n, (w, mov, ready) in enumerate(passes):
                if n == 2 and lo_all is not None:
                    pe.wait_ge(*lo_all)
                for k in range(kts):
                    if ready is not None:
                        pe.wait_ge(ready, k + 1)
                    mm = pe.matmul(bank, w[:, slot, k], mov[:, k0 + k],
                                   start=first and n == 0 and k == 0,
                                   stop=last and n == 2 and k == kts - 1)
            mm.then_inc(unit_done, 1)

        def act_convert(act, it, per, u, kts=KT):
            slot = u % SLOTS
            act.wait_ge(raw_in[slot], at(it, 4 * per, 16 * (u // SLOTS + 1)))
            if u < U_PAIRED:
                act.wait_ge(raw_in2[slot], at(it, 4 * per, 16 * (u // SLOTS + 1)))
            if u >= SLOTS:
                act.wait_ge(unit_done, at(it, per, u - 3))
            act.activation(whi[:, slot, 0:kts], raw[:, slot, 0:kts], ACT.Copy).then_inc(hi_done, 1)

        def dve_convert(dve, it, per, u, kts=KT):
            slot = u % SLOTS
            dve.wait_ge(hi_done, at(it, per, u + 1))
            nc.vector.tensor_tensor(wlo[:, slot, 0:kts], raw[:, slot, 0:kts], whi[:, slot, 0:kts].bitcast(F32),
                                    ALU.subtract).then_inc(lo_done, 1)

        def act_out(act, it, per, u, dst, o, func, scale=1.0):
            count = at(it, per, u + 1)
            apart(act, it)
            act.wait_ge(unit_done, count)
            act.activation(dst, ps[:, o % 4], func, scale=scale).then_inc(evac, 1)

        def apart(eng, it):
            if it is not None:
                eng.wait_ge(hi_done, 1)

        def tile_of(t, it, per, n):
            if it is None:
                return t[:, n]
            return t[:, bass.ds(it * per + n, 1)].rearrange("p a n -> p (a n)")

        def col_of(t, it, per, n):
            return t[:, n:n + 1] if it is None else t[:, bass.ds(it * per + n, 1)]

        w_in_v = w_in[0].rearrange("(k p) n -> p k n", p=P)
        w_out_v = w_out[0].rearrange("(k p) n -> p k n", p=P)
        w_in2_v = w_in_2[0].rearrange("(k p) n -> p k n", p=P)
        w_ya_v = w_a_out_2[0].rearrange("(k p) n -> p k n", p=P)
        w_yr_v = w_r_out_2[0].rearrange("(k p) n -> p k n", p=P)
        w_o_v = w_o_2[0].rearrange("(k p) n -> p k n", p=P)
        w_g_v = w_ff_gate_2[0].rearrange("(k p) n -> p k n", p=P)
        w_u_v = w_ff_up_2[0].rearrange("(k p) n -> p k n", p=P)
        w_d_v = w_ff_down_2[0].rearrange("(k p) n -> p k n", p=P)
        w_ada_v = w_ada[0].rearrange("(k p) n -> p k n", p=P)

        block = stack.enter_context(nc.Block())

        @block.sync
        def _(sp):
            def rows(dst, first, src):
                sp.dma_start(dst[first:first + src.shape[0], :], src).then_inc(m["vec_in"], 16)

            rows(vec, V_C, c.rearrange("a (m p) -> (a m) p", p=P))
            rows(vec, V_ADA, b_ada.rearrange("a (m p) -> (a m) p", p=P))
            for g, src in enumerate((q_gain_a, q_gain_b, k_gain_a, k_gain_cmp, k_gain_sel, k_gain_win)):
                for half in range(2):
                    sp.dma_start(vec[V_GAIN + g:V_GAIN + g + 1, half * HD:(half + 1) * HD],
                                 src).then_inc(m["vec_in"], 16)
            rows(vec, V_NORM, norm_gain.rearrange("a (m p) -> (a m) p", p=P))
            rows(vec, V_CONV, w_conv_2.rearrange("a t (m p) -> (a t m) p", p=P))
            rows(vec, V_RET, g_ret_2.rearrange("a (m p) -> (a m) p", p=P))
            rows(vec, V_MIX, g_mix_2.rearrange("a (m p) -> (a m) p", p=P))
            rows(vec, V_FFN, g_ffn_2.rearrange("a (m p) -> (a m) p", p=P))
            rows(vec, V_FIN, g_final_2.rearrange("(m p) -> m p", p=P))
            rows(vec2, 0, cmp_pos_k.rearrange("a (q l) d -> (a q) (l d)", l=2))
            rows(vec2, CMP_T, cmp_pos_v.rearrange("a (q l) d -> (a q) (l d)", l=2))
            sp.dma_start(x_tok[:], x[0].rearrange("(i p) d -> p i d", p=P)).then_inc(m["x_in"], 16)
            for k in range(KT):
                sp.dma_start(ada[:, k], w_ada_v[:, k, 0:2048]).then_inc(ada_in[k // 2], 16)
            def load(it, per, u, src, kts=KT):
                slot = u % SLOTS
                if u >= SLOTS:
                    converted = at(it, per, u - 3)
                    apart(sp, it)
                    sp.wait_ge(hi_done, converted)
                    sp.wait_ge(lo_done, converted)
                sp.dma_start(raw[:, slot, 0:kts], src).then_inc(raw_in[slot], 16)

            def load_pair(u, dst, dst2, src, src2):
                if u >= SLOTS:
                    sp.wait_ge(hi_done, u - 3)
                    sp.wait_ge(lo_done, u - 3)
                sp.dma_start(dst, src).then_inc(raw_in[u % SLOTS], 16)
                sp.dma_start(dst2, src2).then_inc(raw_in2[u % SLOTS], 16)

            def load_halves(u, cut):
                r, w = raw[:, u % SLOTS], w_in_v[:, :, cut:cut + P]
                load_pair(u, r[:, 0:4], r[:, 4:8], w[:, 0:4], w[:, 4:8])

            for u in range(4):
                load_halves(u, IN_COLS[u])
            sp.dma_start(gb_raw[:], w_in_v[:, :, GB_COL:GB_COL + 24]).then_inc(m["gbw_in"], 16)
            for k in range(0, KT, 4):
                sp.dma_start(ada_g[:, k:k + 4], w_ada_v[:, k:k + 4, 2048:3072]).then_inc(m["adag_in"], 16)
            for u in range(4, 8):
                load_halves(u, IN_COLS[u])
            for u in range(8, 16):
                a = Q_COLS[(u - 8) // 4] + (u % 4) * HD
                r = raw[:, u % SLOTS]
                load_pair(u, r[:, :, 0:HD], r[:, :, HD:P], w_in_v[:, :, a:a + HD],
                          w_in_v[:, :, a + 4 * HD:a + 5 * HD])
            for u in range(16, 24):
                a = Z_COLS[(u - 16) // 4] + (u % 4) * P
                if u < U_PAIRED:
                    load_halves(u, a)
                else:
                    load(None, 0, u, w_in_v[:, :, a:a + P])

            def wide(n):
                return bass.ds(n, P)

            with sp.Fori(0, 2) as it:
                for k in range(4):
                    load(it, 4, U_WO + k, w_out_v[:, :, wide(it * 512 + k * P)])
            with sp.Fori(0, 2) as it:
                for t in range(4):
                    for n, off in enumerate((0, 2048, 1024)):
                        load(it, 12, U_CONV + 3 * t + n, w_in2_v[:, :, wide(it * 512 + off + t * P)])
            with sp.Fori(0, 4) as it:
                for t in range(2):
                    load(it, 4, U_YA + 2 * t, w_in2_v[:, :, wide(it * 256 + GA_COL + t * P)])
                    load(it, 4, U_YA + 2 * t + 1, w_ya_v[:, :, wide((it * 2 + t) * P)])
            with sp.Fori(0, 4) as it:
                for k in range(8):
                    if k < 4:
                        cut = it * 256 + (3072 + 1024 * (k // 2) + (k % 2) * P)
                    else:
                        cut = it * 512 + (5120 + (k - 4) * P)
                    load(it, 8, U_QKV + k, w_in2_v[:, :, wide(cut)])
            with sp.Fori(0, 2) as it:
                for k in range(12):
                    h, n = divmod(k, 6)
                    if n < 4:
                        cut = it * 1024 + (7168 + h * 512 + n * P)
                    else:
                        cut = it * 512 + (GR_COL + h * 256 + (n - 4) * P)
                    load(it, 12, U_GATE + k, w_in2_v[:, :, wide(cut)])
            with sp.Fori(0, 2) as it:
                for k in range(8):
                    half = k % 2
                    load(it, 8, U_YR + k, w_yr_v[:, 8 * half:8 * half + 8, wide(it * 512 + (k // 2) * P)])
            with sp.Fori(0, 2) as it:
                for k in range(4):
                    load(it, 4, U_O + k, w_o_v[:, :, wide(it * 512 + k * P)])
            with sp.Fori(0, FT // 2) as it:
                for t in range(2):
                    load(it, 4, U_FF + 2 * t, w_g_v[:, :, wide(it * 256 + t * P)])
                    load(it, 4, U_FF + 2 * t + 1, w_u_v[:, :, wide(it * 256 + t * P)])
            with sp.Fori(0, 2) as it:
                for k in range(12):
                    t, part = divmod(k, 3)
                    kts = KT if part < 2 else FT - 2 * KT
                    load(it, 12, U_DOWN + k, w_d_v[:, 8 * part:8 * part + kts, wide(it * 512 + t * P)], kts)
            for i in range(NI):
                sp.wait_ge(m["fin_a"], i + 1)
                sp.wait_ge(m["fin_d"], i + 1)
                sp.dma_start(out[0].rearrange("(i p) d -> p i d", p=P)[:, i], out_tok[:, i]).then_inc(m["out_done"], 16)
            sp.wait_ge(m["out_done"], 16 * NI)

        @block.gpsimd
        def _(pool):
            g = nc.gpsimd
            own = Own(pool, m["pool_own"])
            pool.dma_start(onehot[:], bias_onehot).then_inc(m["onehot_in"], 16)
            pool.dma_start(rel[0:32, :], rel_bias).then_inc(m["onehot_in"], 16)
            own(g.memset(rel[32:33, :], BIG))
            pool.dma_start(nsink[:], sinks.partition_broadcast(P)).then_inc(m["misc_in"], 16)
            pool.dma_start(gate_bias[:], b_nsa_gate.partition_broadcast(P)).then_inc(m["misc_in"], 16)
            pool.dma_start(decay[:, 0:4], dec_f_2.partition_broadcast(P)).then_inc(m["misc_in"], 16)
            pool.dma_start(decay[:, 4:8], dec_b_2.partition_broadcast(P)).then_inc(m["misc_in"], 16)
            for dst, w in ((w2k[:, :, 0], w_cmp_k2), (w2k[:, :, 1], w_cmp_k2), (w2v[:], w_cmp_v2)):
                pool.dma_start(dst, w[0].rearrange("(k p) d -> p k d", p=P)).then_inc(m["misc_in"], 16)
            own.wait()
            own(g.memset(ident[:], 0.0))
            own(g.memset(half_sel[:], 1.0 / HD))
            own(g.memset(cmask[:], 0.0))
            own.wait()
            own(g.affine_select(out=ident[:], in_=ident[:], compare_op=ALU.not_equal, fill=1.0, base=0,
                                pattern=[[-1, P]], channel_multiplier=1))
            own(g.affine_select(out=half_sel[:, 0:1], in_=half_sel[:, 0:1], compare_op=ALU.is_ge, fill=0.0,
                                base=HD - 1, pattern=[[0, 1]], channel_multiplier=-1))
            own(g.affine_select(out=half_sel[:, 1:2], in_=half_sel[:, 1:2], compare_op=ALU.is_ge, fill=0.0,
                                base=-HD, pattern=[[0, 1]], channel_multiplier=1))
            own(g.affine_select(out=cmask[:], in_=cmask[:], compare_op=ALU.is_ge, fill=BIG, base=-31,
                                pattern=[[P, NI], [-16, NC_PAD]], channel_multiplier=1))
            own(g.memset(mean512[:], 1.0 / 512))
            own(g.memset(minus_half[:], -0.5))
            own.wait()
            g.memset(ones1[:], 1.0).then_inc(m["consts"], 1)

            def rsqrt(dst, src, n, parts=P):
                return g.tensor_tensor(dst, src, minus_half[0:parts, :].to_broadcast([parts, n]), ALU.pow)

            pool.wait_ge(m["rms_in"], 1)
            rsqrt(rstd[:], msq[:], NI).then_inc(m["rms_rs"], 1)

            pool.wait_ge(m["line_ev"], 16)
            pool.dma_start(line_dram, line[:]).then_inc(m["line_out"], 16)
            pool.wait_ge(m["line_out"], 16)
            pool.wait_ge(m["hl_done"], KT)
            skew = [[16 * LINE - 1, P], [LINE, 8], [1, 256]]
            pool.dma_start(band_a[:], bass.AP(line_dram.tensor, 127, skew)).then_inc(m["band_in"], 16)
            pool.dma_start(band_b[:, :, 256:512],
                           bass.AP(line_dram.tensor, 8 * LINE + 127, skew)).then_inc(m["band_in"], 16)
            for n, (w, t) in enumerate(((w_cmp_k1, KC), (w_cmp_v1, VC))):
                if n:
                    pool.wait_ge(m["c1_mm"], 1)
                pool.dma_start(w1[:], w[0].rearrange("(q p) d -> p q d", p=P)).then_inc(m["w1_in"], 16)
                pool.wait_ge(evac, t + 1)
                if n:
                    pool.wait_ge(m["xp_done"], 1)
                for half in range(2):
                    for l in range(2):
                        pool.dma_start(shifted[HD * l:HD * l + HD, half, 0:S - l],
                                       proj[HD * half:HD * half + HD, t, l:S]).then_inc(m["sh_in"], 16)
                if n == 0:
                    hrs = 0
                    for a, b in NORM_GROUPS:
                        hrs += 1
                        if hrs == 2:
                            pool.wait_ge(m["kms_done"], 1)
                            rsqrt(kc_rs[0:NC_PAD, :], kc_ms[0:NC_PAD, :], 2, NC_PAD).then_inc(m["krs_done"], 1)
                        pool.wait_ge(m["hms_done"], hrs)
                        rsqrt(rstd_h[:, 8 * a:8 * b], msq_h[:, 8 * a:8 * b], 8 * (b - a)).then_inc(m["hrs_done"], 1)

            def norm_rs(q):
                pool.wait_ge(nrm["ms_done"], q + 1)
                rsqrt(rstd[:], msq[:], NI).then_inc(nrm["rs_done"], 1)

            norm_rs(0)
            pool.dma_start(cos_t[:], rope_cos).then_inc(m["tab_in"], 16)
            pool.dma_start(sin_t[:], rope_sin).then_inc(m["tab_in"], 16)
            pool.wait_ge(nrm["t_done"], KT)
            pool.dma_start(x1_dram, x_t[:]).then_inc(m["spill_done"], 16)
            pool.wait_ge(m["al_done"], 8)
            g.iota(delta[:], [[1, STRIP]], base=-(NI - 1) * P, channel_multiplier=-1,
                   allow_small_or_imprecise_dtypes=True).then_inc(m["delta_done"], 1)
            pool.wait_ge(m["spill_done"], 16)

            hown = Own(pool, m["pool_own2"])
            pool.wait_ge(m["ret_ev"], 16)
            with pool.Fori(0, 2) as it:
                hown.begin(it, 6)
                for hh in range(2):
                    r = [tile_of(ret, it, 8, 4 * hh + t) for t in range(4)]
                    hown(g.tensor_tensor(head_sum[:], r[0], r[1], ALU.add))
                    hown.wait()
                    hown(g.tensor_tensor(head_sum[:], head_sum[:], r[2], ALU.add))
                    hown.wait()
                    g.tensor_tensor(head_sum[:], head_sum[:], r[3], ALU.add).then_inc(m["hsum_done"], 1)
                    pool.wait_ge(m["hsq_done"], at(it, 8, 4 * hh + 2))
                    g.tensor_tensor(head_ssq[:], head_sq[:, 0], head_sq[:, 1], ALU.add).then_inc(m["hpair_done"], 1)
                    pool.wait_ge(m["hpair_done"], at(it, 2, hh + 1))
                    pool.wait_ge(m["hsq_done"], at(it, 8, 4 * hh + 3))
                    hown(g.tensor_tensor(head_ssq[:], head_ssq[:], head_sq[:, 0], ALU.add))
                    hown.wait()
                    pool.wait_ge(m["hsq_done"], at(it, 8, 4 * hh + 4))
                    g.tensor_tensor(head_ssq[:], head_ssq[:], head_sq[:, 1], ALU.add).then_inc(m["hssq_done"], 1)
                    pool.wait_ge(m["rms2_done"], at(it, 2, hh + 1))
                    rsqrt(rstd[:], msq[:], NI).then_inc(m["rrs_done"], 1)
            hown.end(2)
            pool.wait_ge(m["rl_done"], 16)
            pool.dma_start(x1_back[:], x1_dram).then_inc(m["back_in"], 16)
            norm_rs(1)
            norm_rs(2)

        @block.scalar
        def _(act):
            a = nc.scalar
            act.wait_ge(m["x_in"], 16)
            for i in range(NI):
                if i:
                    act.wait_ge(m["sumsq_done"], i)
                a.activation(sqx[:], x_tok[:, i], ACT.Square, accum_out=sumsq[:, i:i + 1]).then_inc(m["sumsq_done"], 1)
            act.wait_ge(m["col_done"], 1)
            a.activation(csilu[:], col[:, V_C:V_C + 8], ACT.Silu).then_inc(m["csilu_done"], 1)
            for k in range(KT):
                act.wait_ge(m["x_tr"], k + 1)
                a.activation(x_t[:, k], ps[:, k % 4], ACT.Copy).then_inc(m["x_ev"], 1)
            for h in range(16):
                act.wait_ge(m["line_mm"], h + 1)
                a.activation(line[:, h], ps[:, 4 + h % 3, 0:LINE], ACT.Copy).then_inc(m["line_ev"], 1)
            act.wait_ge(m["line_ev"], 16)
            a.activation(line_far[:], line[:, 8:16, 0:1].rearrange("p h n -> p (h n)"), ACT.Copy).then_inc(m["far_done"], 1)
            act.wait_ge(m["line_out"], 16)
            act_convert(act, None, 0, 0)
            act_convert(act, None, 0, 1)
            act.wait_ge(m["gbw_in"], 16)
            a.activation(gb_hi[:], gb_raw[:], ACT.Copy).then_inc(m["gb_cv"], 1)
            act.wait_ge(m["mod_done"], 1)
            for k in range(KT):
                act.wait_ge(m["th_done"], k + 1)
                a.activation(h_hi[:, k], t_h[:, k], ACT.Identity, bias=mod[:, k:k + 1]).then_inc(m["hh_done"], 1)
            for n in range(4):
                act_convert(act, None, 0, n + AHEAD)
                act_out(act, None, 0, n, proj[:, n], n, ACT.Copy)
            act.wait_ge(m["adag_done"], 1)
            with act.Fori(0, 3) as it:
                for k in range(4, 8):
                    act_convert(act, it, 4, k + AHEAD)
                    act_out(act, it, 4, k, tile_of(proj, it, 4, k), k, ACT.Copy)
            def square(t):
                if t >= 4:
                    act.wait_ge(m["st_mm"], t - 3)
                else:
                    act.wait_ge(evac, NORM_TILES[t] + 1)
                a.activation(proj[:, 20 + t % 4], proj[:, NORM_TILES[t]], ACT.Square).then_inc(m["sq_done"], 1)

            for n in range(16, 24):
                act_convert(act, None, 0, n + AHEAD)
                if n == 20:
                    act.wait_ge(m["st_mm"], 11)
                act_out(act, None, 0, n, proj[:, n], n, ACT.Silu)
                if n < 19:
                    for t in range(*NORM_GROUPS[n - 16]):
                        square(t)
                if n == 16:
                    act.wait_ge(m["c1_mm"], 1)
                    a.activation(hid[:], ps[:, 7, 0:128].rearrange("p (c n) -> p c n", c=2), ACT.Silu).then_inc(m["hid_done"], 1)
                if n == 17:
                    act.wait_ge(m["c2_mm"], 1)
                    for g in range(2):
                        half = slice(g * HD, (g + 1) * HD)
                        a.activation(kcmp[half, :], ps[half, 7, 128 + 32 * g:160 + 32 * g], ACT.Copy).then_inc(m["kc_ev"], 1)
                    act.wait_ge(m["kc_ev"], 2)
                    a.activation(kc_sq[:], kcmp[:], ACT.Square).then_inc(m["kcsq_done"], 1)
                if n == 21:
                    act.wait_ge(m["c1_mm"], 2)
                    for t in range(2):
                        hidden = ps[:, 7, 192 + 64 * t:256 + 64 * t].rearrange("p (g n) -> p g n", g=2)
                        a.activation(hid_v[:, t], hidden.unsqueeze(2).to_broadcast([P, 2, 4, NC_PAD]),
                                     ACT.Silu).then_inc(m["hid_done"], 1)
            for n, t in enumerate((VA, VS, VW)):
                act.wait_ge(m["vt_mm"], n + 1)
                a.activation(proj[:, t], ps[:, 5 + n], ACT.Copy).then_inc(m["vt_ev"], 1)
            act.wait_ge(m["gb_add"], 1)
            a.activation(gates[:], gates[:], ACT.Sigmoid).then_inc(m["gb_done"], 1)
            act.wait_ge(m["csub_done"], 1)
            a.activation(sc[:], sc[:], ACT.Exp, scale=-1.0).then_inc(m["cexp_done"], 1)
            act.wait_ge(m["ctr_mm"], 1)
            a.activation(pt[:, 0], ps[:, 2], ACT.Copy).then_inc(m["cpt_a"], 1)

            for s in range(STEPS):
                if s < N_ATT:
                    G, n = divmod(s, 8)
                    act.wait_ge(m["s_bias"], s + 1)
                    if n == 0 and G >= 2:
                        act.wait_ge(m["comb_done"], G - 1)
                    w = att(s).width
                    a.activation(sc[:, s % 2, 0:w], sc[:, s % 2, 0:w], ACT.Exp, scale=-1.0,
                                 bias=row_min[:, G % 2, n:n + 1],
                                 accum_out=den[:, G % 2, att(s).head:att(s).head + 1]).then_inc(m["s_exp"], 1)
                t = s - 1
                if 0 <= t < N_ATT and t % 2 == 1:
                    act.wait_ge(m["t_mm"], t + 1)
                    if t >= 2:
                        act.wait_ge(m["pv_mm"], t - 1)
                    w = att(t).width
                    a.activation(pt[:, 1, 0:w], ps[:, 3, 0:w], ACT.Copy).then_inc(m["pt_a"], 1)
                G, n = divmod(s, 8)
                if n == 0 and G >= 1 and G <= N_GROUPS and (G - 1) % 3 == 0:
                    act.wait_ge(m["arg_done"], (G - 1) // 3 + 1)
                    a.activation(sink_exp[:], sink_arg[:], ACT.Exp).then_inc(m["sinkexp_done"], 1)
                i = tail_at(s)
                if i is not None:
                    for half in range(2):
                        act.wait_ge(m["yf_done"], 2 * i + half + 1)
                        a.activation(y_hi[:, 4 * half:4 * half + 4, i * P:(i + 1) * P], y_f[:, half],
                                     ACT.Copy).then_inc(m["yh_done"], 1)

            def out_and_square(it, per, u, per_o, o, q, t, scale):
                act_out(act, it, per, u, t[:, o % 2], o, ACT.Copy, scale)
                count = at(it, per_o, q * KT + o - NORM_O[q] + 1)
                apart(act, it)
                act.wait_ge(nrm["x_done"], count)
                a.activation(t[:, 2 + o % 2], tile_of(x_t, it, per_o, o - NORM_O[q]), ACT.Square).then_inc(nrm["xsq_done"], 1)

            def round_norm(q, dst, t):
                for k in range(KT):
                    act.wait_ge(nrm["t_done"], q * KT + k + 1)
                    a.activation(dst[:, k], t[:, k], ACT.Copy).then_inc(nrm["h_done"], 1)

            with act.Fori(0, 2) as it:
                for k in range(4):
                    act_convert(act, it, 4, U_WO + k + AHEAD)
                    out_and_square(it, 4, U_WO + k, 4, O_WO + k, 0, tt, col_of(mod, it, 4, 16 + k))
            round_norm(0, g_hi, t_g)
            act.wait_ge(m["lgt_done"], 1)
            a.activation(lt[:, 1], lt[:, 0], ACT.Exp, scale=-1.0).then_inc(m["lgexp_done"], 1)
            with act.Fori(0, 2) as it:
                for t in range(4):
                    for n in range(3):
                        act_convert(act, it, 12, U_CONV + 3 * t + n + AHEAD)
                        act_out(act, it, 12, U_CONV + 3 * t + n, conv_ev[:, t % 2, n], O_CONV + 3 * t + n, ACT.Copy)
                    count = at(it, 4, t + 1)
                    apart(act, it)
                    act.wait_ge(m["af_done"], count)
                    a.activation(tile_of(a_hi, it, 4, t), tt[:, t % 2], ACT.Copy).then_inc(m["ah_done"], 1)
            with act.Fori(0, 4) as it:
                for t in range(2):
                    act_convert(act, it, 4, U_YA + 2 * t + AHEAD)
                    act_out(act, it, 4, U_YA + 2 * t, tt[:, t], O_YA + 2 * t, ACT.Sigmoid)
                    act_convert(act, it, 4, U_YA + 2 * t + 1 + AHEAD)
                    act_out(act, it, 4, U_YA + 2 * t + 1, tt[:, 2 + t], O_YA + 2 * t + 1, ACT.Copy)
            act.wait_ge(m["spill_done"], 16)
            with act.Fori(0, RET_HEADS) as it:
                def p_round(j):
                    act.wait_ge(m["pm_done"], at(it, 4, j + 1))
                    a.activation(p_hi[:, j], p_f[:, j % 2], ACT.Copy).then_inc(m["ph_done"], 1)

                def v_round(t):
                    act.wait_ge(m["vtr_mm"], at(it, 4, t + 1))
                    a.activation(v_hi[:, :, t * P:(t + 1) * P],
                                 ps[:, 4 + t].rearrange("p (j e) -> p j e", j=NI), ACT.Copy).then_inc(m["vh_done"], 1)

                for k in range(8):
                    act_convert(act, it, 8, U_QKV + k + AHEAD)
                    dst = qk_raw[:, k] if k < 4 else v_t[:, k % 2]
                    act_out(act, it, 8, U_QKV + k, dst, O_QKV + k, ACT.Copy)
                    if k == 1:
                        act.wait_ge(m["strip_done"], at(it, 1, 1))
                        a.activation(strip[:], strip[:], ACT.Exp).then_inc(m["decay_done"], 1)
                    if k in (3, 5):
                        dst = q_hi if k == 3 else k_hi
                        act.wait_ge(m["rot_done"], at(it, 2, (k - 1) // 2))
                        for t in range(2):
                            a.activation(dst[:, t], rot_o[:, t], ACT.Copy).then_inc(m["qkh_done"], 1)
                    if k >= 5:
                        v_round(k - 5)
                for j in range(3):
                    p_round(j)
                v_round(3)
                p_round(3)
                for t in range(4):
                    count = at(it, 4, t + 1)
                    apart(act, it)
                    act.wait_ge(m["rpv_mm"], count)
                    a.activation(tile_of(ret, it, 4, t), ps[:, PV_BANK[t]], ACT.Copy).then_inc(m["ret_ev"], 1)
            with act.Fori(0, 2) as it:
                for k in range(12):
                    hh, n = divmod(k, 6)
                    act_convert(act, it, 12, U_GATE + k + AHEAD)
                    if n < 4:
                        act_out(act, it, 12, U_GATE + k, sg[:, n], O_GATE + k, ACT.Silu)
                    else:
                        act_out(act, it, 12, U_GATE + k, tile_of(sig_r, it, 4, 2 * hh + n - 4), O_GATE + k, ACT.Sigmoid)
                    if n == 1:
                        for t in range(4):
                            act.wait_ge(m["sub_done"], at(it, 8, 4 * hh + t + 1))
                            if t >= 2:
                                count = at(it, 2, hh + 1)
                                apart(act, it)
                                act.wait_ge(m["hpair_done"], count)
                            a.activation(head_sq[:, t % 2], tile_of(ret, it, 8, 4 * hh + t), ACT.Square).then_inc(m["hsq_done"], 1)
                    if n == 5:
                        for t in range(4):
                            count = at(it, 8, 4 * hh + t + 1)
                            apart(act, it)
                            act.wait_ge(m["val_done"], count)
                            a.activation(tile_of(ret_hi, it, 8, 4 * hh + t), (val2, val3)[t % 2][:],
                                         ACT.Copy).then_inc(m["rh_done"], 1)
            with act.Fori(0, 2) as it:
                for k in range(8):
                    act_convert(act, it, 8, U_YR + k + AHEAD)
                    if k % 2:
                        act_out(act, it, 8, U_YR + k, yr_t[:, (k // 2) % 2], O_YR + k // 2, ACT.Copy)
                        count = at(it, 4, k // 2 + 1)
                        apart(act, it)
                        act.wait_ge(m["mg_done"], count)
                        a.activation(tile_of(m_hi, it, 4, k // 2), mg_t[:], ACT.Copy).then_inc(m["mh_done"], 1)
            with act.Fori(0, 2) as it:
                for k in range(4):
                    act_convert(act, it, 4, U_O + k + AHEAD)
                    out_and_square(it, 4, U_O + k, 4, O_O + k, 1, tt_o, 1.0)
            round_norm(1, f_hi, t_f)
            with act.Fori(0, FT // 2) as it:
                for t in range(2):
                    act_convert(act, it, 4, U_FF + 2 * t + AHEAD)
                    act_out(act, it, 4, U_FF + 2 * t, tt[:, t], O_FF + 2 * t, ACT.Silu)
                    act_convert(act, it, 4, U_FF + 2 * t + 1 + AHEAD)
                    act_out(act, it, 4, U_FF + 2 * t + 1, tt[:, 2 + t], O_FF + 2 * t + 1, ACT.Copy)
                    count = at(it, 2, t + 1)
                    apart(act, it)
                    act.wait_ge(m["prod_done"], count)
                    a.activation(tile_of(act_hi, it, 2, t), tt[:, 4], ACT.Copy).then_inc(m["fh_done"], 1)

            for k in range(24):
                t, part = divmod(k, 3)
                if k + AHEAD < 24:
                    act_convert(act, None, 0, U_DOWN + k + AHEAD, KT if (k + AHEAD) % 3 < 2 else FT - 2 * KT)
                if part == 2:
                    out_and_square(None, 0, U_DOWN + k, 0, O_DOWN + t, 2, tt, 1.0)
            for i in range(NI):
                act.wait_ge(m["fin_mm"], 2 * i + 2)
                a.activation(out_tok[:, i, 512:1024], ps[:, 2 * (i % 2) + 1], ACT.Copy).then_inc(m["fin_a"], 1)

        @block.vector
        def _(dve):
            v = nc.vector
            own = Own(dve, m["dve_own"])
            dve.wait_ge(m["col_t"], 1)
            own(v.tensor_copy(col[:], ps[:, 7, 0:N_VEC]))
            own(v.tensor_copy(pos_col[:], ps[:, 7, P:P + 2 * CMP_T]))
            own.wait()
            own(v.tensor_scalar(gains[:, 0:2], col[:, V_GAIN:V_GAIN + 2], 0.125, None, ALU.mult))
            v.tensor_scalar(gains[:, 2:6], col[:, V_GAIN + 2:V_GAIN + 6], -1.0, None, ALU.mult).then_inc(m["col_done"], 1)
            dve.wait_ge(m["csilu_done"], 1)
            for k in range(KT):
                if k % 2 == 0:
                    dve.wait_ge(ada_in[k // 2], 32)
                if k == 0:
                    own(v.tensor_scalar(acc[:], ada[:, 0], csilu[:, 0:1], None, ALU.mult))
                else:
                    own.wait()
                    ins = v.scalar_tensor_tensor(out=acc[:], in0=ada[:, k], scalar=csilu[:, k:k + 1], in1=acc[:],
                                                 op0=ALU.mult, op1=ALU.add)
                    if k < KT - 1:
                        own(ins)
                    else:
                        ins.then_inc(m["ada_done"], 1)
                if k == 1:
                    dve.wait_ge(m["sumsq_done"], NI)
                    v.tensor_scalar(msq[:], sumsq[:], 1.0 / D, EPS, ALU.mult, ALU.add).then_inc(m["rms_in"], 1)
                    dve.wait_ge(m["misc_in"], 16 * 7)
                    own(v.tensor_scalar(nsink[:], nsink[:], -1.0, None, ALU.mult))
            dve.wait_ge(m["mod_mm"], 1)
            own(v.tensor_tensor(mod[:, 0:16], ps[:, 4, 0:16], col[:, V_ADA:V_ADA + 16], ALU.add))
            own.wait()
            v.scalar_tensor_tensor(out=s1[:], in0=mod[:, 8:16], scalar=1.0, in1=col[:, V_NORM:V_NORM + 8],
                                   op0=ALU.add, op1=ALU.mult).then_inc(m["mod_done"], 1)
            dve.wait_ge(m["mod_done"], 1)
            dve.wait_ge(m["rms_bc"], 1)
            dve.wait_ge(m["x_ev"], KT)
            for k in range(KT):
                v.scalar_tensor_tensor(out=t_h[:, k], in0=x_t[:, k], scalar=s1[:, k:k + 1], in1=ps[:, 5],
                                       op0=ALU.mult, op1=ALU.mult).then_inc(m["th_done"], 1)
            dve.wait_ge(m["th_done"], KT)
            for k in range(KT):
                dve.wait_ge(m["hh_done"], k + 1)
                v.scalar_tensor_tensor(out=h_lo[:, k], in0=t_h[:, k], scalar=mod[:, k:k + 1], in1=h_hi[:, k].bitcast(F32),
                                       op0=ALU.add, op1=ALU.subtract).then_inc(m["hl_done"], 1)
                if k < AHEAD:
                    dve_convert(dve, None, 0, k)
            dve.wait_ge(m["gb_cv"], 1)
            v.tensor_tensor(gb_lo[:], gb_raw[:], gb_hi[:].bitcast(F32), ALU.subtract).then_inc(m["gb_cl"], 1)
            dve.wait_ge(m["adag_in"], 32)
            for n in range(4):
                dve_convert(dve, None, 0, n + AHEAD)
                for k in (2 * n, 2 * n + 1):
                    if k == 0:
                        own(v.tensor_scalar(acc_g[:], ada_g[:, 0], csilu[:, 0:1], None, ALU.mult))
                    else:
                        own.wait()
                        ins = v.scalar_tensor_tensor(out=acc_g[:], in0=ada_g[:, k], scalar=csilu[:, k:k + 1],
                                                     in1=acc_g[:], op0=ALU.mult, op1=ALU.add)
                        if k < KT - 1:
                            own(ins)
                        else:
                            ins.then_inc(m["adag_done"], 1)
            with dve.Fori(0, 3) as it:
                for k in range(4, 8):
                    dve_convert(dve, it, 4, k + AHEAD)

            def cmp_input(n):
                if n == 0:
                    own(v.memset(xp[:], 0.0))
                    own.wait()
                else:
                    dve.wait_ge(m["c1_mm"], 1)
                dve.wait_ge(m["sh_in"], 64 * (n + 1))
                for half in range(2):
                    src = bass.AP(shifted[:].tensor, shifted[:, half, 0:1].offset,
                                  [list(shifted[:].ap[0]), [2, CMP_T], [16, NC_PAD - 1]])
                    pos = pos_col[:, n * CMP_T:(n + 1) * CMP_T].unsqueeze(2).to_broadcast([P, CMP_T, NC_PAD - 1])
                    ins = v.tensor_tensor(xp[:, :, half, 0:NC_PAD - 1], src, pos, ALU.add)
                    if half == 0:
                        own(ins)
                    else:
                        ins.then_inc(m["xp_done"], 1)

            def head_norm(t):
                dve.wait_ge(m["bc_mm"], t + 1)
                tile = proj[:, NORM_TILES[t]]
                g = NORM_GAINS[t]
                v.scalar_tensor_tensor(out=tile, in0=tile, scalar=gains[:, g:g + 1], in1=ps[:, 5 + t % 2],
                                       op0=ALU.mult, op1=ALU.mult).then_inc(m["qk_done"], 1)

            cmp_input(0)
            dve.wait_ge(m["band_in"], 32)
            dve.wait_ge(m["far_done"], 1)
            v.tensor_copy(band_b[:, :, 0:256], line_far[:].unsqueeze(2).to_broadcast([P, 8, 256])).then_inc(m["band_fill"], 1)
            for n in range(16, 24):
                dve_convert(dve, None, 0, n + AHEAD)
                if n == 16:
                    dve.wait_ge(m["modg_mm"], 1)
                    own(v.tensor_tensor(mod[:, 16:24], ps[:, 6, 0:8], col[:, V_ADA + 16:V_ADA + 24], ALU.add))
                if n < 19:
                    a, b = NORM_GROUPS[n - 16]
                    dve.wait_ge(m["st_mm"], b)
                    v.tensor_scalar(msq_h[:, 8 * a:8 * b], ps[:, 4, 8 * a:8 * b], EPS, None, ALU.add).then_inc(m["hms_done"], 1)
                if n == 17:
                    dve.wait_ge(m["kst_mm"], 1)
                    v.tensor_scalar(kc_ms[0:NC_PAD, :], ps[0:NC_PAD, 7, 448:450], EPS, None, ALU.add).then_inc(m["kms_done"], 1)
                if n == 19:
                    dve.wait_ge(m["kbc_mm"], 1)
                    v.scalar_tensor_tensor(out=kcmp[:], in0=kcmp[:], scalar=gains[:, 3:4], in1=ps[:, 7, 480:512],
                                           op0=ALU.mult, op1=ALU.mult).then_inc(m["kcmp_done"], 1)
                    cmp_input(1)
                if n == 20:
                    own(v.memset(vbd[:], 0.0))
                for t in BCAST_AT.get(n, ()):
                    head_norm(t)
                if n == 22:
                    dve.wait_ge(m["c2_mm"], 2)
                    own.wait()
                    for g in range(2):
                        for j in range(4):
                            part = slice(32 * j, 32 * j + 32)
                            v.tensor_copy(vbd[part, g, j * HD:(j + 1) * HD],
                                          ps[part, 7, 320 + g * HD:384 + g * HD]).then_inc(m["vbd_done"], 1)
            dve.wait_ge(m["gb_mm"], 1)
            bias4 = gate_bias[:].unsqueeze(1).to_broadcast([P, NI, 24])
            own.wait()
            v.tensor_tensor(gates[:], ps[:, 4, 96:192].rearrange("p (i n) -> p i n", i=NI), bias4,
                            ALU.add).then_inc(m["gb_add"], 1)

            dve.wait_ge(m["cs_mm"], 1)
            for g in range(2):
                for i in range(NI):
                    own(v.tensor_tensor(sc[:, g, i * P:(i + 1) * P].rearrange("p (j n) -> p j n", j=4),
                                        ps[:, g, i * P:(i + 1) * P].rearrange("p (j n) -> p j n", j=4),
                                        cmask[:, i].unsqueeze(1).to_broadcast([P, 4, NC_PAD]), ALU.add))
            own.wait()
            flat = sc[:].rearrange("p g (q n) -> p (g q) n", n=NC_PAD)
            own(v.tensor_reduce(cmin[:].rearrange("p g q -> p (g q)"), flat, AX, ALU.min))
            own.wait()
            own(v.tensor_scalar(cmin[:], cmin[:], BIG / 10, None, ALU.min))
            own.wait()
            v.tensor_tensor(flat, flat, cmin[:].rearrange("p g q -> p (g q)").unsqueeze(2).to_broadcast([P, 32, NC_PAD]),
                            ALU.subtract).then_inc(m["csub_done"], 1)
            dve.wait_ge(m["cexp_done"], 1)
            own(v.tensor_reduce(cden[:].rearrange("p g q -> p (g q)"), flat, AX, ALU.add))
            own.wait()
            own(v.tensor_scalar(cden[:], cden[:], 1e-30, None, ALU.max))
            own.wait()
            own(v.reciprocal(cden[:], cden[:]))
            own.wait()
            dve.wait_ge(m["gb_done"], 1)
            for g in range(2):
                own(v.tensor_tensor(ccoef[:, :, 4 * g:4 * g + 4], cden[:, g].rearrange("p (i j) -> p i j", i=NI),
                                    gate_of(0)[:, :, 4 * g:4 * g + 4], ALU.mult))
            dve.wait_ge(m["ctr_mm"], 1)
            v.tensor_copy(pt[:, 1], ps[:, 3]).then_inc(m["cpt_d"], 1)
            own.wait()
            for i in range(NI):
                dve.wait_ge(m["co_mm"], i + 1)
                v.tensor_tensor(ob[:, i].rearrange("p (h d) -> p h d", h=8),
                                ps[:, 4 + i].rearrange("p (h d) -> p h d", h=8),
                                ccoef[:, i].unsqueeze(2).to_broadcast([P, 8, HD]), ALU.mult).then_inc(m["co_done"], 1)
            dve.wait_ge(m["co_done"], NI)

            for s in range(STEPS):
                if s < N_ATT:
                    u = att(s)
                    G = s // 8
                    dve.wait_ge(m["s_mm"], s + 1)
                    if s >= 2:
                        dve.wait_ge(m["t_mm"], s - 1)
                    if u.branch == 0:
                        band, start = band_a[:, u.head, 256 - u.width:256], nsink[:, u.head:u.head + 1]
                    else:
                        band, start = band_b[:, u.head, S - u.width:S], 3e38
                    v.tensor_tensor_reduce(sc[:, s % 2, 0:u.width], ps[:, s % 2, 0:u.width], band, 1.0, start,
                                           ALU.add, ALU.min, row_min[:, G % 2, s % 8:s % 8 + 1]).then_inc(m["s_bias"], 1)
                    if s % 8 == 7 and u.branch == 0:
                        dve.wait_ge(m["s_bias"], s + 1)
                        v.tensor_tensor(sink_arg[:].rearrange("p (g j) -> p j g", g=2),
                                        row_min[:, G % 2].rearrange("p (j g) -> p j g", g=2),
                                        nsink[:].rearrange("p (g j) -> p j g", g=2), ALU.subtract).then_inc(m["arg_done"], 1)
                t = s - 1
                if 0 <= t < N_ATT and t % 2 == 0:
                    dve.wait_ge(m["t_mm"], t + 1)
                    if t >= 2:
                        dve.wait_ge(m["pv_mm"], t - 1)
                    w = att(t).width
                    v.tensor_copy(pt[:, 0, 0:w], ps[:, 2, 0:w]).then_inc(m["pt_d"], 1)
                if s % 8 == 1 and s > 8:
                    G = s // 8 - 1
                    i, branch = divmod(G, 3)
                    dve.wait_ge(m["pv_mm"], 8 * G + 8)
                    dve.wait_ge(m["s_exp"], 8 * G + 8)
                    cf, dn = coef[:, G % 2], den[:, G % 2]
                    heads = ps[:, 4 + G % 2].rearrange("p (h d) -> p h d", h=8)
                    if branch == 0:
                        dve.wait_ge(m["sinkexp_done"], i + 1)
                        own(v.tensor_tensor(dn, dn, sink_exp[:], ALU.add))
                        own.wait()
                    own(v.reciprocal(cf, dn))
                    own.wait()
                    if branch:
                        own(v.tensor_tensor(cf, cf, gate_of(branch)[:, i], ALU.mult))
                        own.wait()
                    elif i:
                        dve.wait_ge(m["ytr_mm"], i)
                    dst = o_tmp if branch else oa
                    ins = v.tensor_tensor(dst[:].rearrange("p (h d) -> p h d", h=8), heads,
                                          cf.unsqueeze(2).to_broadcast([P, 8, HD]), ALU.mult).then_inc(m["comb_done"], 1)
                    if branch:
                        dve.wait_ge(m["comb_done"], G + 1)
                        v.tensor_tensor(ob[:, i], ob[:, i], o_tmp[:], ALU.add).then_inc(m["ob_done"], 1)
                i = tail_at(s)
                if i is not None:
                    for half in range(2):
                        dve.wait_ge(m["ytr_mm"], i + 1)
                        if i:
                            dve.wait_ge(m["yl_done"], 2 * i - 1 + half)
                        z = (ZA, ZB)[half]
                        v.tensor_tensor(y_f[:, half], ps[:, 6 + half].rearrange("p (t d) -> p t d", t=4),
                                        proj[:, z:z + 4, i * P:(i + 1) * P], ALU.mult).then_inc(m["yf_done"], 1)
                    for half in range(2):
                        dve.wait_ge(m["yh_done"], 2 * i + half + 1)
                        rows = slice(4 * half, 4 * half + 4)
                        v.tensor_tensor(y_lo[:, rows, i * P:(i + 1) * P], y_f[:, half],
                                        y_hi[:, rows, i * P:(i + 1) * P].bitcast(F32), ALU.subtract).then_inc(m["yl_done"], 1)

            def residual(it, per, o, q, t, x_of):
                dve.wait_ge(evac, at(it, per, o + 1))
                n = o - NORM_O[q]
                v.tensor_tensor(tile_of(x_t, it, per, n), t[:, o % 2], tile_of(x_of, it, per, n),
                                ALU.add).then_inc(nrm["x_done"], 1)
                dve.wait_ge(nrm["xsq_done"], at(it, per, q * KT + n + 1))
                if n or it is not None:
                    dve.wait_ge(nrm["ss_done"], at(it, per, q * (KT + 1) + n + 1))
                v.tensor_tensor(t[:, 4], t[:, 4], t[:, 2 + o % 2], ALU.add).then_inc(nrm["ss_done"], 1)

            def norm(q, gain, t, lo, hi, gap=None):
                dve.wait_ge(nrm["nst_mm"], q + 1)
                v.tensor_scalar(msq[:], ps[:, 4, 0:NI], 1.0 / D, EPS, ALU.mult, ALU.add).then_inc(nrm["ms_done"], 1)
                dve.wait_ge(nrm["nbc_mm"], q + 1)
                for k in range(KT):
                    v.scalar_tensor_tensor(out=t[:, k], in0=x_t[:, k], scalar=col[:, gain + k:gain + k + 1], in1=ps[:, 5],
                                           op0=ALU.mult, op1=ALU.mult).then_inc(nrm["t_done"], 1)
                if lo is not None:
                    for k in range(KT):
                        dve.wait_ge(nrm["h_done"], q * KT + k + 1)
                        v.tensor_tensor(lo[:, k], t[:, k], hi[:, k].bitcast(F32), ALU.subtract).then_inc(nrm["l_done"], 1)

            dve.wait_ge(unit_done, U_WO)
            v.memset(tt[:, 4], 0.0).then_inc(nrm["ss_done"], 1)
            with dve.Fori(0, 2) as it:
                for k in range(4):
                    dve_convert(dve, it, 4, U_WO + k + AHEAD)
                    residual(it, 4, O_WO + k, 0, tt, x_t)
            norm(0, V_MIX, t_g, g_lo, g_hi)
            own(v.tensor_scalar(lt[:, 0], decay[:], -1.0, None, ALU.mult))
            own.wait()
            own(v.tensor_tensor(lt[:, 0], lt[:, 0], decay[:], ALU.max))
            own.wait()
            v.tensor_copy(lt[:, 4], lt[:, 0]).then_inc(m["lgt_done"], 1)
            dve.wait_ge(m["lgexp_done"], 1)
            own(v.tensor_scalar(lt[:, 2], lt[:, 1], 2.0, None, ALU.add))
            own.wait()
            own(v.reciprocal(lt[:, 2], lt[:, 2]))
            own.wait()
            own(v.tensor_tensor(lt[:, 2], lt[:, 2], lt[:, 1], ALU.mult))
            own.wait()
            own(v.tensor_tensor(lt[:, 3], lt[:, 2], lt[:, 2], ALU.mult))
            own(v.memset(lg[:], 1.0 / 19))
            own.wait()
            for n in range(17, -1, -2):
                own(v.tensor_tensor(lg[:], lg[:], lt[:, 3], ALU.mult))
                own.wait()
                own(v.tensor_scalar(lg[:], lg[:], 1.0 / n, None, ALU.add))
                own.wait()
            own(v.tensor_tensor(lg[:], lg[:], lt[:, 2], ALU.mult))
            own(v.tensor_scalar(lt[:, 1], decay[:], 0.0, None, ALU.min))
            own.wait()
            own(v.scalar_tensor_tensor(out=lg[:], in0=lg[:], scalar=-2.0, in1=lt[:, 1], op0=ALU.mult, op1=ALU.add))
            own.wait()
            own(v.tensor_scalar(lg[:, 4:8], lg[:, 4:8], -1.0, None, ALU.mult))
            own(v.memset(u_pad[:, 0:1], 0.0))
            own(v.memset(u_pad[:, S + 1:S + 2], 0.0))
            with dve.Fori(0, 2) as it:
                own.begin(it, 16)
                for t in range(4):
                    ev = conv_ev[:, t % 2]
                    tap = [col_of(col, it, 4, V_CONV + 8 * n + t) for n in range(3)]
                    dve_convert(dve, it, 12, U_CONV + 3 * t + AHEAD)
                    dve_convert(dve, it, 12, U_CONV + 3 * t + 1 + AHEAD)
                    dve.wait_ge(evac, at(it, 12, O_CONV + 3 * t + 2))
                    own.wait()
                    own(v.tensor_tensor(u_pad[:, 1:S + 1], ev[:, 0], ev[:, 1], ALU.mult))
                    own.wait()
                    own(v.tensor_scalar(conv_t[:], u_pad[:, 1:S + 1], tap[1], None, ALU.mult))
                    own.wait()
                    own(v.scalar_tensor_tensor(out=conv_t[:], in0=u_pad[:, 0:S], scalar=tap[0], in1=conv_t[:],
                                               op0=ALU.mult, op1=ALU.add))
                    own.wait()
                    own(v.scalar_tensor_tensor(out=conv_t[:], in0=u_pad[:, 2:S + 2], scalar=tap[2], in1=conv_t[:],
                                               op0=ALU.mult, op1=ALU.add))
                    dve_convert(dve, it, 12, U_CONV + 3 * t + 2 + AHEAD)
                    dve.wait_ge(evac, at(it, 12, O_CONV + 3 * t + 3))
                    own.wait()
                    v.tensor_tensor(tt[:, t % 2], conv_t[:], ev[:, 2], ALU.mult).then_inc(m["af_done"], 1)
                    dve.wait_ge(m["ah_done"], at(it, 4, t + 1))
                    v.tensor_tensor(tile_of(a_lo, it, 4, t), tt[:, t % 2], tile_of(a_hi, it, 4, t).bitcast(F32),
                                    ALU.subtract).then_inc(m["al_done"], 1)
                    dve.wait_ge(m["al_done"], at(it, 4, t + 1))
                own.end(2)
            with dve.Fori(0, 4) as it:
                own.begin(it, 2)
                for t in range(2):
                    dve_convert(dve, it, 4, U_YA + 2 * t + AHEAD)
                    dve_convert(dve, it, 4, U_YA + 2 * t + 1 + AHEAD)
                    dve.wait_ge(evac, at(it, 4, O_YA + 2 * t + 2))
                    own(v.tensor_tensor(tile_of(ya, it, 2, t), tt[:, t], tt[:, 2 + t], ALU.mult))
                own.end(4)
            dve.wait_ge(m["delta_done"], 1)
            dve.wait_ge(m["tab_in"], 32)
            own.wait()
            with dve.Fori(0, RET_HEADS) as it:
                own.begin(it, 12)

                def rotate(r):
                    for n, (x0, x1, op) in enumerate(((cos_t, sin_t, ALU.subtract), (sin_t, cos_t, ALU.add))):
                        if n:
                            own.wait()
                        own(v.tensor_tensor(rot_t[:, 0], qk_raw[:, r], x0[:], ALU.mult))
                        own(v.tensor_tensor(rot_t[:, 1], qk_raw[:, r + 1], x1[:], ALU.mult))
                        own.wait()
                        ins = v.tensor_tensor(rot_o[:, n], rot_t[:, 0], rot_t[:, 1], op)
                        if n == 0:
                            own(ins)
                        else:
                            ins.then_inc(m["rot_done"], 1)

                def rest(hi, lo, base):
                    for t in range(2):
                        dve.wait_ge(m["qkh_done"], at(it, 4, base + t + 1))
                        v.tensor_tensor(lo[:, t], rot_o[:, t], hi[:, t].bitcast(F32), ALU.subtract).then_inc(m["qkl_done"], 1)

                def v_rest(t):
                    dve.wait_ge(m["vh_done"], at(it, 4, t + 1))
                    cut = slice(t * P, (t + 1) * P)
                    v.tensor_tensor(v_lo[:, :, cut], ps[:, 4 + t].rearrange("p (j e) -> p j e", j=NI),
                                    v_hi[:, :, cut].bitcast(F32), ALU.subtract).then_inc(m["vl_done"], 1)

                def p_mult(j):
                    if j >= 2:
                        dve.wait_ge(m["pl_done"], at(it, 4, j - 1))
                    dve.wait_ge(m["rs_mm"], at(it, 4, j + 1))
                    cut = (NI - 1 - j) * P
                    v.scalar_tensor_tensor(out=p_f[:, j % 2], in0=ps[:, RS_BANK[j]], scalar=0.0625,
                                           in1=strip[:, cut:cut + S], op0=ALU.mult, op1=ALU.mult).then_inc(m["pm_done"], 1)

                def p_rest(j):
                    dve.wait_ge(m["ph_done"], at(it, 4, j + 1))
                    v.tensor_tensor(p_lo[:, j], p_f[:, j % 2], p_hi[:, j].bitcast(F32), ALU.subtract).then_inc(m["pl_done"], 1)

                for k in range(8):
                    dve_convert(dve, it, 8, U_QKV + k + AHEAD)
                    if k == 0:
                        own(v.tensor_scalar(strip[:], delta[:], 0.0, col_of(lg, it, 1, 0), ALU.max, ALU.mult))
                        own(v.tensor_scalar(strip2[:], delta[:], 0.0, col_of(lg, it, 1, 4), ALU.min, ALU.mult))
                        own.wait()
                        v.tensor_tensor(strip[:], strip[:], strip2[:], ALU.add).then_inc(m["strip_done"], 1)
                    if k in (2, 4):
                        dve.wait_ge(evac, at(it, 8, O_QKV + k))
                        rotate(k - 2)
                    if k == 3:
                        rest(q_hi, q_lo, 0)
                    if k == 5:
                        rest(k_hi, k_lo, 2)
                    if k >= 5:
                        v_rest(k - 5)
                dve.wait_ge(m["decay_done"], at(it, 1, 1))
                p_mult(0)
                p_mult(1)
                p_rest(0)
                p_mult(2)
                p_rest(1)
                v_rest(3)
                p_mult(3)
                p_rest(2)
                p_rest(3)
                own.end(RET_HEADS)
            with dve.Fori(0, 2) as it:
                own.begin(it, 8)
                for k in range(12):
                    hh, n = divmod(k, 6)
                    dve_convert(dve, it, 12, U_GATE + k + AHEAD)
                    if n == 1:
                        dve.wait_ge(m["mu_mm"], at(it, 2, hh + 1))
                        for t in range(4):
                            r = tile_of(ret, it, 8, 4 * hh + t)
                            v.tensor_tensor(r, r, ps[:, 4], ALU.subtract).then_inc(m["sub_done"], 1)
                    if n == 3:
                        dve.wait_ge(m["rst_mm"], at(it, 2, hh + 1))
                        v.tensor_scalar(msq[:], ps[:, 5, 0:NI], 1.0 / 512, EPS, ALU.mult, ALU.add).then_inc(m["rms2_done"], 1)
                    if n == 5:
                        dve.wait_ge(m["rbc_mm"], at(it, 2, hh + 1))
                        dve.wait_ge(evac, at(it, 12, O_GATE + 6 * hh + 4))

                        def ret_rest(t):
                            dve.wait_ge(m["rh_done"], at(it, 8, 4 * hh + t + 1))
                            v.tensor_tensor(tile_of(ret_lo, it, 8, 4 * hh + t), (val2, val3)[t % 2][:],
                                            tile_of(ret_hi, it, 8, 4 * hh + t).bitcast(F32), ALU.subtract).then_inc(m["rl_done"], 1)

                        for t in range(4):
                            own(v.scalar_tensor_tensor(out=val[:], in0=tile_of(ret, it, 8, 4 * hh + t),
                                                       scalar=col_of(col, it, 8, V_RET + 4 * hh + t), in1=ps[:, 6],
                                                       op0=ALU.mult, op1=ALU.mult))
                            own.wait()
                            if t >= 2:
                                dve.wait_ge(m["rl_done"], at(it, 8, 4 * hh + t - 1))
                            v.tensor_tensor((val2, val3)[t % 2][:], val[:], sg[:, t], ALU.mult).then_inc(m["val_done"], 1)
                            if t:
                                ret_rest(t - 1)
                            dve.wait_ge(m["val_done"], at(it, 8, 4 * hh + t + 1))
                        ret_rest(3)
                own.end(2)
            with dve.Fori(0, 2) as it:
                own.begin(it, 4)
                for k in range(8):
                    dve_convert(dve, it, 8, U_YR + k + AHEAD)
                    if k % 2:
                        t = k // 2
                        dve.wait_ge(evac, at(it, 4, O_YR + t + 1))
                        own(v.tensor_tensor(yr_t[:, t % 2], yr_t[:, t % 2], tile_of(sig_r, it, 4, t), ALU.mult))
                        own.wait()
                        v.tensor_tensor(mg_t[:], yr_t[:, t % 2], tile_of(ya, it, 4, t), ALU.add).then_inc(m["mg_done"], 1)
                        dve.wait_ge(m["mh_done"], at(it, 4, t + 1))
                        v.tensor_tensor(tile_of(m_lo, it, 4, t), mg_t[:], tile_of(m_hi, it, 4, t).bitcast(F32),
                                        ALU.subtract).then_inc(m["ml_done"], 1)
                        dve.wait_ge(m["ml_done"], at(it, 4, t + 1))
                own.end(2)
            dve.wait_ge(m["back_in"], 16)
            v.memset(tt_o[:, 4], 0.0).then_inc(nrm["ss_done"], 1)
            with dve.Fori(0, 2) as it:
                for k in range(4):
                    dve_convert(dve, it, 4, U_O + k + AHEAD)
                    residual(it, 4, O_O + k, 1, tt_o, x1_back)
            norm(1, V_FFN, t_f, f_lo, f_hi)
            with dve.Fori(0, FT // 2) as it:
                for t in range(2):
                    dve_convert(dve, it, 4, U_FF + 2 * t + AHEAD)
                    dve_convert(dve, it, 4, U_FF + 2 * t + 1 + AHEAD)
                    dve.wait_ge(evac, at(it, 4, O_FF + 2 * t + 2))
                    v.tensor_tensor(tt[:, 4], tt[:, t], tt[:, 2 + t], ALU.mult).then_inc(m["prod_done"], 1)
                    dve.wait_ge(m["fh_done"], at(it, 2, t + 1))
                    v.tensor_tensor(tile_of(act_lo, it, 2, t), tt[:, 4], tile_of(act_hi, it, 2, t).bitcast(F32),
                                    ALU.subtract).then_inc(m["fl_done"], 1)
                    dve.wait_ge(m["fl_done"], at(it, 2, t + 1))
            dve.wait_ge(m["fl_done"], FT)
            v.memset(tt[:, 4], 0.0).then_inc(nrm["ss_done"], 1)
            for k in range(24):
                t, part = divmod(k, 3)
                if k + AHEAD < 24:
                    dve_convert(dve, None, 0, U_DOWN + k + AHEAD, KT if (k + AHEAD) % 3 < 2 else FT - 2 * KT)
                if part == 2:
                    residual(None, 0, O_DOWN + t, 2, tt, x_t)
            norm(2, V_FIN, y_out, None, None)
            for i in range(NI):
                dve.wait_ge(m["fin_mm"], 2 * i + 1)
                v.tensor_copy(out_tok[:, i, 0:512], ps[:, 2 * (i % 2)]).then_inc(m["fin_d"], 1)

        @block.tensor
        def _(pe):
            def trans(dst, src, parts=P):
                return pe.transpose(dst, src, ident[0:parts, 0:parts])

            def blk(i):
                return slice(i * P, (i + 1) * P)

            def row_on_half(g, bank, cols, src, parts=P):
                wide = src.to_broadcast([parts, HD])
                if g == 0:
                    return trans(ps[0:HD, bank, cols], wide, parts)
                return pe.matmul(ps[HD:P, bank, cols], wide, ident[0:parts, 0:parts], start=True, stop=True)

            pe.wait_ge(m["consts"], 1)
            pe.wait_ge(m["vec_in"], VEC_DMAS * 16)
            trans(ps[:, 7, 0:N_VEC], vec[0:N_VEC, :], N_VEC)
            trans(ps[:, 7, P:P + 2 * CMP_T], vec2[:], 2 * CMP_T).then_inc(m["col_t"], 1)
            pe.wait_ge(m["x_in"], 16)
            for k in range(KT):
                if k >= 4:
                    pe.wait_ge(m["x_ev"], k - 3)
                for i in range(NI):
                    mm = trans(ps[:, k % 4, blk(i)], x_tok[:, i, blk(k)])
                mm.then_inc(m["x_tr"], 1)
            pe.wait_ge(m["onehot_in"], 32)
            pe.wait_ge(m["pool_own"], 1)
            for h in range(16):
                if h >= 3:
                    pe.wait_ge(m["line_ev"], h - 2)
                pe.matmul(ps[:, 4 + h % 3, 0:LINE], rel[:, h:h + 1].to_broadcast([33, P]), onehot[:, h // 8],
                          start=True, stop=True).then_inc(m["line_mm"], 1)
            pe.wait_ge(m["line_ev"], 16)
            pe.wait_ge(m["rms_rs"], 1)

            def rows_bc(bank):
                for i in range(NI):
                    mm = trans(ps[:, bank, blk(i)], rstd[:, i:i + 1].to_broadcast([P, P]))
                return mm

            rows_bc(5).then_inc(m["rms_bc"], 1)

            def column_sums(bank, src, n):
                for q in range(n):
                    mm = pe.matmul(ps[:, bank, q:q + 1], src[:, blk(q)], ones1[:], start=True, stop=True)
                return mm

            pe.wait_ge(m["ada_done"], 1)
            column_sums(4, acc, 16).then_inc(m["mod_mm"], 1)
            for n in range(4):
                pe_unit(pe, None, 0, n, 0, n, h_hi, h_lo, hi_sem=m["hh_done"] if n == 0 else None,
                        lo_sem=m["hl_done"] if n == 0 else None)
            pe.wait_ge(m["adag_done"], 1)
            column_sums(6, acc_g, 8).then_inc(m["modg_mm"], 1)
            with pe.Fori(0, 3) as it:
                for k in range(4, 8):
                    pe_unit(pe, it, 4, k, 4, k, h_hi, h_lo)

            def head_stats(t):
                pe.wait_ge(m["sq_done"], t + 1)
                for i in range(NI):
                    mm = pe.matmul(ps[:, 4, 8 * t + 2 * i:8 * t + 2 * i + 2], proj[:, 20 + t % 4, blk(i)], half_sel[:],
                                   start=True, stop=True)
                mm.then_inc(m["st_mm"], 1)

            def cmp_hidden(n, c0):
                for c in range(2):
                    for q in range(CMP_T):
                        mm = pe.matmul(ps[:, 7, c0 + 64 * c:c0 + 64 * c + 64], w1[:, q, blk(c)],
                                       xp[:, q].rearrange("p g n -> p (g n)"), start=q == 0, stop=q == CMP_T - 1)
                mm.then_inc(m["c1_mm"], 1)

            pe.wait_ge(m["w1_in"], 16)
            pe.wait_ge(m["xp_done"], 1)
            cmp_hidden(0, 0)
            for n in range(16, 24):
                pe_unit(pe, None, 0, n, 0, n, h_hi, h_lo)
                if n < 19:
                    if n > 16:
                        pe.wait_ge(m["hms_done"], n - 16)
                    else:
                        pe.wait_ge(m["mod_done"], 1)
                    for t in range(*NORM_GROUPS[n - 16]):
                        head_stats(t)
                if n == 16:
                    pe.wait_ge(m["hid_done"], 1)
                    for t in range(2):
                        mm = pe.matmul(ps[:, 7, P:P + 64], w2k[:, t].rearrange("p a d -> p (a d)"), hid[:, t],
                                       start=t == 0, stop=t == 1)
                    mm.then_inc(m["c2_mm"], 1)
                if n == 17:
                    pe.wait_ge(m["kcsq_done"], 1)
                    pe.matmul(ps[0:NC_PAD, 7, 448:450], kc_sq[:], half_sel[:], start=True, stop=True).then_inc(m["kst_mm"], 1)
                if n == 19:
                    pe.wait_ge(m["krs_done"], 1)
                    for g in range(2):
                        mm = row_on_half(g, 7, slice(480, 512), kc_rs[0:NC_PAD, g:g + 1], NC_PAD)
                    mm.then_inc(m["kbc_mm"], 1)
                for t in BCAST_AT.get(n, ()):
                    group = [a <= t < b for a, b in NORM_GROUPS].index(True)
                    pe.wait_ge(m["hrs_done"], group + 1)
                    if t >= 2:
                        pe.wait_ge(m["qk_done"], t - 1)
                    for i in range(NI):
                        for g in range(2):
                            n_h = 8 * t + 2 * i + g
                            mm = row_on_half(g, 5 + t % 2, blk(i), rstd_h[:, n_h:n_h + 1])
                    mm.then_inc(m["bc_mm"], 1)
                if n == 21:
                    pe.wait_ge(m["w1_in"], 32)
                    pe.wait_ge(m["xp_done"], 2)
                    pe.wait_ge(m["kcmp_done"], 1)
                    cmp_hidden(1, 192)
                if n == 22:
                    pe.wait_ge(m["hid_done"], 3)
                    for g in range(2):
                        for t in range(2):
                            mm = pe.matmul(ps[:, 7, 320 + HD * g:384 + HD * g],
                                           hid_v[:, t, g].rearrange("p j n -> p (j n)"),
                                           w2v[:, t], start=t == 0, stop=t == 1)
                    mm.then_inc(m["c2_mm"], 1)
            pe.wait_ge(m["qk_done"], len(NORM_TILES))
            for n, t in enumerate((VA, VS, VW)):
                if n == 2:
                    pe.wait_ge(m["vbd_done"], 8)
                for i in range(NI):
                    mm = trans(ps[:, 5 + n, blk(i)], proj[:, t, blk(i)])
                mm.then_inc(m["vt_mm"], 1)
            pe.wait_ge(m["gb_cl"], 1)
            pe.wait_ge(m["hms_done"], 3)
            for i in range(NI):
                for n, (h, w) in enumerate(((h_hi, gb_hi), (h_lo, gb_hi), (h_hi, gb_lo))):
                    for k in range(KT):
                        mm = pe.matmul(ps[:, 4, 96 + 24 * i:120 + 24 * i], h[:, k, blk(i)], w[:, k],
                                       start=n == 0 and k == 0, stop=n == 2 and k == KT - 1)
            mm.then_inc(m["gb_mm"], 1)
            pe.wait_ge(evac, U_WO)
            for i in range(NI):
                for j in range(4):
                    for g in range(2):
                        half = slice(g * HD, (g + 1) * HD)
                        c = i * P + j * NC_PAD
                        mm = pe.matmul(ps[:, g, c:c + NC_PAD], proj[half, QB + j, blk(i)], kcmp[half, :],
                                       start=True, stop=True)
            mm.then_inc(m["cs_mm"], 1)
            pe.wait_ge(m["cexp_done"], 1)
            for g in range(2):
                for i in range(NI):
                    mm = trans(ps[:, 2 + g, blk(i)], sc[:, g, blk(i)])
            mm.then_inc(m["ctr_mm"], 1)
            pe.wait_ge(m["cpt_a"], 1)
            pe.wait_ge(m["cpt_d"], 1)
            pe.wait_ge(m["gb_add"], 1)
            pe.wait_ge(m["vt_ev"], 3)
            for i in range(NI):
                for g in range(2):
                    mm = pe.matmul(ps[:, 4 + i, 256 * g:256 * g + 256], pt[:, g, blk(i)], vbd[:, g], start=True, stop=True)
                mm.then_inc(m["co_mm"], 1)

            for s in range(STEPS):
                if s < N_ATT:
                    u = att(s)
                    if s >= 2:
                        pe.wait_ge(m["s_bias"], s - 1)
                    half = slice(u.g * HD, (u.g + 1) * HD)
                    q, k = (QB if u.branch else QA) + u.j, (KA, KS, KW)[u.branch]
                    pe.matmul(ps[:, s % 2, 0:u.width], proj[half, q, blk(u.i)],
                              proj[half, k, u.first_block * P:u.first_block * P + u.width],
                              start=True, stop=True).then_inc(m["s_mm"], 1)
                t = s - 1
                if 0 <= t < N_ATT:
                    pe.wait_ge(m["s_exp"], t + 1)
                    if t == 0:
                        pe.wait_ge(m["ctr_mm"], 1)
                    if t >= 2:
                        pe.wait_ge(m["pt_a" if t % 2 else "pt_d"], t // 2)
                    for b in range(att(t).width // P):
                        mm = trans(ps[:, 2 + t % 2, blk(b)], sc[:, t % 2, blk(b)])
                    mm.then_inc(m["t_mm"], 1)
                t = s - 2
                if 0 <= t < N_ATT:
                    u = att(t)
                    pe.wait_ge(m["pt_a" if t % 2 else "pt_d"], t // 2 + 1)
                    if t == 0:
                        pe.wait_ge(m["co_done"], NI)
                    elif t % 8 == 0 and u.group >= 2:
                        pe.wait_ge(m["comb_done"], u.group - 1)
                    v, blocks = (VA, VS, VW)[u.branch], u.width // P
                    for b in range(blocks):
                        c = (u.first_block + b) * P + u.g * HD
                        mm = pe.matmul(ps[:, 4 + u.group % 2, u.head * HD:(u.head + 1) * HD], pt[:, t % 2, blk(b)],
                                       proj[:, v, c:c + HD], start=b == 0, stop=b == blocks - 1)
                    mm.then_inc(m["pv_mm"], 1)
                i = tail_at(s)
                if i is not None:
                    pe.wait_ge(m["ob_done"], 2 * i + 2)
                    pe.wait_ge(m["comb_done"], 3 * i + 3)
                    if i:
                        pe.wait_ge(m["yf_done"], 2 * i)
                    for half, o in enumerate((oa, ob[:, i])):
                        for b in range(4):
                            mm = trans(ps[:, 6 + half, blk(b)], o[:, blk(b)])
                    mm.then_inc(m["ytr_mm"], 1)

            def norm(q, t, scratch):
                pe.wait_ge(nrm["ss_done"], q * (KT + 1) + KT + 1)
                for i in range(NI):
                    mm = pe.matmul(ps[:, 4, i:i + 1], scratch[:, 4, blk(i)], ones1[:], start=True, stop=True)
                mm.then_inc(nrm["nst_mm"], 1)
                pe.wait_ge(nrm["rs_done"], q + 1)
                rows_bc(5).then_inc(nrm["nbc_mm"], 1)

            pe.wait_ge(m["yh_done"], 2 * NI)
            with pe.Fori(0, 2) as it:
                for k in range(4):
                    pe_unit(pe, it, 4, U_WO + k, 4, O_WO + k, y_hi, y_lo,
                            lo_all=(m["yl_done"], 2 * NI) if k == 0 else None)
            norm(0, t_g, tt)
            pe.wait_ge(nrm["h_done"], KT)
            with pe.Fori(0, 2) as it:
                for k in range(12):
                    pe_unit(pe, it, 12, U_CONV + k, 12, O_CONV + k, g_hi, g_lo,
                            lo_all=(nrm["l_done"], KT) if k == 0 else None)
            with pe.Fori(0, 4) as it:
                for t in range(2):
                    pe_unit(pe, it, 4, U_YA + 2 * t, 4, O_YA + 2 * t, g_hi, g_lo)
                    if t == 0:
                        pe.wait_ge(m["ah_done"], KT)
                    pe_unit(pe, it, 4, U_YA + 2 * t + 1, 4, O_YA + 2 * t + 1, a_hi, a_lo,
                            lo_all=(m["al_done"], KT) if t == 0 else None)
            with pe.Fori(0, RET_HEADS) as it:
                def v_trans(t):
                    pe.wait_ge(evac, at(it, 8, O_QKV + 5 + t))
                    for j in range(NI):
                        mm = trans(ps[:, 4 + t, blk(j)], v_t[:, t % 2, blk(j)])
                    mm.then_inc(m["vtr_mm"], 1)

                def scores(j):
                    for n, (k, q) in enumerate(((k_hi, q_hi), (k_lo, q_hi), (k_hi, q_lo))):
                        for t in range(2):
                            mm = pe.matmul(ps[:, RS_BANK[j]], k[:, t, blk(j)], q[:, t], start=n == 0 and t == 0,
                                           stop=n == 2 and t == 1)
                    mm.then_inc(m["rs_mm"], 1)

                for k in range(8):
                    pe_unit(pe, it, 8, U_QKV + k, 8, O_QKV + k, g_hi, g_lo)
                    if k >= 5:
                        v_trans(k - 5)
                pe.wait_ge(m["qkl_done"], at(it, 4, 4))
                for j in range(3):
                    pe.wait_ge(m["vl_done"], at(it, 4, j + 1))
                    scores(j)
                v_trans(3)
                pe.wait_ge(m["pm_done"], at(it, 4, 1))
                scores(3)
                pe.wait_ge(m["vl_done"], at(it, 4, 4))
                pe.wait_ge(m["pl_done"], at(it, 4, 4))
                for t in range(4):
                    for n, (w, p) in enumerate(((v_hi, p_hi), (v_lo, p_hi), (v_hi, p_lo))):
                        for j in range(NI):
                            mm = pe.matmul(ps[:, PV_BANK[t]], w[:, j, blk(t)], p[:, j], start=n == 0 and j == 0,
                                           stop=n == 2 and j == NI - 1)
                    mm.then_inc(m["rpv_mm"], 1)
            with pe.Fori(0, 2) as it:
                for k in range(12):
                    hh, n = divmod(k, 6)
                    pe_unit(pe, it, 12, U_GATE + k, 12, O_GATE + k, g_hi, g_lo)
                    if n == 0:
                        pe.wait_ge(m["hsum_done"], at(it, 2, hh + 1))
                        pe.matmul(ps[:, 4], mean512[:], head_sum[:], start=True, stop=True).then_inc(m["mu_mm"], 1)
                    if n == 2:
                        pe.wait_ge(m["hssq_done"], at(it, 2, hh + 1))
                        column_sums(5, head_ssq, NI).then_inc(m["rst_mm"], 1)
                    if n == 4:
                        pe.wait_ge(m["rrs_done"], at(it, 2, hh + 1))
                        rows_bc(6).then_inc(m["rbc_mm"], 1)
            pe.wait_ge(m["rh_done"], 2 * KT)
            with pe.Fori(0, 2) as it:
                for k in range(8):
                    half = k % 2
                    pe_unit(pe, it, 8, U_YR + k, 4, O_YR + k // 2, ret_hi, ret_lo, k0=8 * half, first=half == 0,
                            last=half == 1, lo_all=(m["rl_done"], 2 * KT) if k == 0 else None)
            pe.wait_ge(m["mh_done"], KT)
            with pe.Fori(0, 2) as it:
                for k in range(4):
                    pe_unit(pe, it, 4, U_O + k, 4, O_O + k, m_hi, m_lo,
                            lo_all=(m["ml_done"], KT) if k == 0 else None)
            norm(1, t_f, tt_o)
            pe.wait_ge(nrm["h_done"], KT + KT)
            with pe.Fori(0, FT // 2) as it:
                for k in range(4):
                    pe_unit(pe, it, 4, U_FF + k, 4, O_FF + k, f_hi, f_lo,
                            lo_all=(nrm["l_done"], 2 * KT) if k == 0 else None)
            pe.wait_ge(m["fh_done"], FT)
            with pe.Fori(0, 2) as it:
                for k in range(12):
                    t, part = divmod(k, 3)
                    pe_unit(pe, it, 12, U_DOWN + k, 4, O_DOWN + t, act_hi, act_lo, KT if part < 2 else FT - 2 * KT,
                            8 * part, part == 0, part == 2, lo_all=(m["fl_done"], FT) if k == 0 else None)
            norm(2, None, tt)
            pe.wait_ge(nrm["t_done"], 2 * KT + KT)
            for i in range(NI):
                if i >= 2:
                    pe.wait_ge(m["fin_d"], i - 1)
                    pe.wait_ge(m["fin_a"], i - 1)
                for half in range(2):
                    for k in range(4):
                        mm = trans(ps[:, 2 * (i % 2) + half, blk(k)], y_out[:, 4 * half + k, blk(i)])
                    mm.then_inc(m["fin_mm"], 1)


_INS = ['x', 'c', 'w_ada', 'b_ada', 'norm_gain', 'w_in', 'b_nsa_gate', 'q_gain_a', 'k_gain_a', 'sinks', 'q_gain_b',
        'k_gain_cmp', 'k_gain_sel', 'k_gain_win', 'cmp_pos_k', 'cmp_pos_v', 'w_cmp_k1', 'w_cmp_k2', 'w_cmp_v1',
        'w_cmp_v2', 'w_out', 'rel_bias', 'g_mix_2', 'w_in_2', 'w_conv_2', 'dec_f_2', 'dec_b_2', 'g_ret_2',
        'w_a_out_2', 'w_r_out_2', 'w_o_2', 'g_ffn_2', 'w_ff_gate_2', 'w_ff_up_2', 'w_ff_down_2', 'g_final_2']
_OUTS = [((1, S, D), 'float32')]


def bias_onehot_table():
    dist = 255 - np.arange(LINE)
    near = np.maximum(dist, 0)
    far = 16 + (np.log(np.maximum(near, 1).astype(np.float32) / np.float32(16)) / np.log(8.0) * 16).astype(np.int32)
    bucket = np.where(near < 16, near, np.minimum(far, 31))
    table = np.zeros((33, 2, LINE), np.float32)
    for q, allowed in enumerate(((dist >= 0) & (dist < 128), dist >= 0)):
        for x in range(LINE):
            if allowed[x]:
                table[bucket[x], q, x] = -1.0
            else:
                table[32, q, x] = 1.0
    return table


def rope_tables():
    pos = np.arange(S, dtype=np.float32)
    freqs = np.power(np.float32(10000.0), -np.arange(0, 256, 2, dtype=np.float32) / np.float32(256))
    ang = (pos[None, :] * freqs[:, None].astype(np.float32)).astype(np.float32)
    return np.cos(ang).astype(np.float32), np.sin(ang).astype(np.float32)


def kernel(**inputs):
    import numpy as _np
    import concourse.bacc as _bacc
    from concourse import mybir as _mybir
    from concourse.bass_utils import run_bass_kernel_spmd as _run

    nc = _bacc.Bacc("TRN2", target_bir_lowering=False, num_devices=1)
    arrays, args = {}, []
    cos, sin = rope_tables()
    shape_only = [("bias_onehot", bias_onehot_table()), ("rope_cos", cos), ("rope_sin", sin)]
    for name, value in [(name, inputs[name]) for name in _INS] + shape_only:
        a = _np.ascontiguousarray(value)
        arrays[f"in_{name}_dram"] = a
        args.append(nc.dram_tensor(f"in_{name}_dram", a.shape, _mybir.dt.from_np(a.dtype), kind="ExternalInput").ap())
    for i, (shape, dtype) in enumerate(_OUTS):
        dt = _mybir.dt.from_np(_np.dtype(dtype))
        args.append(nc.dram_tensor(f"out_{i}_dram", shape, dt, kind="ExternalOutput").ap())
    hybrid_block(nc, *args)
    r = _run(nc, [arrays], core_ids=[0])
    return r.results[0]["out_0_dram"]
```

```python
from contextlib import ExitStack

import numpy as np

import concourse.bass as bass
from concourse import mybir

F32 = mybir.dt.float32
F32R = mybir.dt.float32r
ACT = mybir.ActivationFunctionType
ALU = mybir.AluOpType
AX = mybir.AxisListType.X

P = 128
S = 512
NI = S // P
D = 1024
KT = D // P
SLOTS = 4
AHEAD = 2
HD = 64
EPS = 1e-6
BIG = 1e30
LINE = 384
NC_PAD = 32
CMP_T = 16
RET_HEADS = 4
STRIP = S + (NI - 1) * P
D_FF = 2816
FT = D_FF // P

KC, VC, KA, VA, KS, VS, KW, VW, QA, QB, ZA, ZB = 0, 1, 2, 3, 4, 5, 6, 7, 8, 12, 16, 20
IN_COLS = [1792, 1920, 512, 640, 2048, 2176, 2304, 2432]
Q_COLS = [0, 1280]
Z_COLS = [768, 2560]
GB_COL = 3072
GA_COL, GR_COL = 9216, 10240

V_C, V_ADA, V_NORM, V_CONV, V_RET, V_MIX, V_FFN, V_FIN, V_GAIN = 0, 8, 32, 40, 64, 80, 88, 96, 104
N_VEC = 110
VEC_DMAS, VEC2_DMAS = 3, 19

PHASE_OUTS = (16, 8, 1, KT, 3 * KT, 2 * KT, 8 * RET_HEADS, 16 + KT, KT, KT, 2 * FT, KT)
PHASE_UNITS = (16, 8, 1, KT, 3 * KT, 2 * KT, 8 * RET_HEADS, 16 + KT, 2 * KT, KT, 2 * FT, 3 * KT)
_, U_Z, U_GB, U_WO, U_CONV, U_YA, U_QKV, U_GATE, U_YR, U_O, U_FF, U_DOWN = (
    sum(PHASE_UNITS[:n]) for n in range(len(PHASE_UNITS)))
_, O_Z, O_GB, O_WO, O_CONV, O_YA, O_QKV, O_GATE, O_YR, O_O, O_FF, O_DOWN = (
    sum(PHASE_OUTS[:n]) for n in range(len(PHASE_OUTS)))
N_OUTS = sum(PHASE_OUTS)
U_PAIRED = 18

NORM_TILES = [QA, QA + 1, QA + 2, QA + 3, QB, QB + 1, QB + 2, QB + 3, KA, KS, KW]
NORM_GAINS = [0, 0, 0, 0, 1, 1, 1, 1, 2, 4, 5]
NORM_GROUPS = [(0, 4), (4, 8), (8, 11)]
BCAST_AT = {18: (0, 1), 19: (2, 3), 20: (4, 5), 21: (6, 7), 22: (8, 9), 23: (10,)}
NORM_O = [O_WO, O_O, O_DOWN]
FIN_ORDER = (1, 2, 3, 0)
RS_BANK = [4, 5, (O_QKV + 4) % 4, (O_QKV + 5) % 4]
PV_BANK = [5, 6, 7, 4]

N_GROUPS = 3 * NI
N_ATT = 8 * N_GROUPS
STEPS = N_ATT + 9


class Step:

    def __init__(self, s):
        self.group, n = divmod(s, 8)
        self.i, self.branch = divmod(self.group, 3)
        self.j, self.g = divmod(n, 2)
        self.head = 4 * self.g + self.j
        blocks = self.i + 1 if self.branch else min(2, self.i + 1)
        self.width = P * blocks
        self.first_block = self.i + 1 - blocks


def norm_group(t):
    return [a <= t < b for a, b in NORM_GROUPS].index(True)


def att(s):
    return Step(s)


def tail_at(s):
    i, rest = divmod(s - 5, 24)
    return i - 1 if rest == 0 and i > 0 else None


class Own:

    def __init__(self, eng, sem):
        self.eng, self.sem, self.base, self.n, self.it, self.per = eng, sem, 0, 0, None, 0

    def __call__(self, ins):
        ins.then_inc(self.sem, 1)
        self.n += 1
        return ins

    def wait(self):
        v = self.base + self.n
        self.eng.wait_ge(self.sem, v if self.it is None else self.it * self.per + v)

    def begin(self, it, per, first=0):
        self.base += self.n
        self.n, self.it, self.per = 0, it, per
        self.base -= first * per
        self.first = first

    def end(self, count):
        assert self.n == self.per, (self.n, self.per)
        self.base += self.first * self.per + count * self.per
        self.n, self.it = 0, None


def at(it, per, base):
    return base if it is None else it * per + base


def hybrid_block(nc, x, c, w_ada, b_ada, norm_gain, w_in, b_nsa_gate, q_gain_a, k_gain_a, sinks,
                 q_gain_b, k_gain_cmp, k_gain_sel, k_gain_win, cmp_pos_k, cmp_pos_v, w_cmp_k1,
                 w_cmp_k2, w_cmp_v1, w_cmp_v2, w_out, rel_bias, g_mix_2, w_in_2, w_conv_2, dec_f_2,
                 dec_b_2, g_ret_2, w_a_out_2, w_r_out_2, w_o_2, g_ffn_2, w_ff_gate_2, w_ff_up_2,
                 w_ff_down_2, g_final_2, bias_onehot, rope_cos, rope_sin, out):
    line_dram = nc.dram_tensor("bias_line", [P, 16, LINE], F32).ap()
    x1_dram = nc.dram_tensor("x1_spill", [P, KT, S], F32).ap()

    with ExitStack() as stack:
        KB = 1024
        BASE = 16512

        def sb(name, shape, kb, dt=F32):
            return nc.alloc_sbuf_tensor_at(name, shape, dt, offset=BASE + int(kb * KB))

        def sem(name):
            return stack.enter_context(nc.semaphore(name))

        raw = sb("w_raw", [P, SLOTS, KT, P], 0)
        whi = sb("w_hi", [P, SLOTS, KT, P], 16, F32R)
        wlo = sb("w_lo", [P, SLOTS, KT, P], 32, F32R)
        c_at = [48 * KB]

        def const(name, shape, dt=F32):
            t = sb(name, shape, c_at[0] / KB, dt)
            c_at[0] += (int(np.prod(shape[1:])) * 4 + 31) // 32 * 32
            return t

        ident = const("ident", [P, P])
        col = const("columns", [P, N_VEC])
        pos_col = const("pos_columns", [P, 2 * CMP_T])
        mean512 = const("ones_over_512", [P, P])
        ones1 = const("ones1", [P, 1])
        half_sel = const("half_select", [P, 2])
        minus_half = const("minus_half", [P, 1])
        csilu = const("csilu", [P, 8])
        mod = const("mod", [P, 24])
        s1 = const("norm_times_scale", [P, 8])
        gains = const("gains", [P, 6])
        line_far = const("bias_far", [P, 8])
        nsink = const("sinks_negated", [P, 8])
        gate_bias = const("gate_bias", [P, 24])
        gates = const("branch_gates", [P, NI, 24])
        sumsq = const("sum_squares", [P, NI])
        msq = const("mean_squares", [P, NI])
        rstd = const("rstd", [P, NI])
        msq_h = const("head_mean_squares", [P, 88])
        rstd_h = const("head_rstd", [P, 88])
        kcmp = const("k_compressed", [P, NC_PAD])
        kcz = const("k_compressed_by_group", [P, 2, NC_PAD])
        kc_sq = const("k_compressed_squared", [P, NC_PAD])
        kc_ms = const("k_compressed_mean_squares", [P, 2])
        kc_rs = const("k_compressed_rstd", [P, 2])
        cmask = const("compressed_mask", [P, NI, NC_PAD])
        cmin = const("compressed_min", [P, 2, 16])
        cden = const("compressed_sum", [P, 2, 16])
        ccoef = const("compressed_coefficient", [P, NI, 8])
        w2k = sb("w_cmp_k2_twice", [P, 2, 2, HD], 56)
        w2v = sb("w_cmp_v2", [P, 2, HD], 57)
        vbd = const("v_compressed_diagonal", [P, 2, 4 * HD])
        decay = const("decay_logits", [P, 8])
        lg = const("log_decay", [P, 8])
        lt = const("log_decay_steps", [P, 5, 8])
        row_min = const("row_min", [P, 2, 8])
        den = const("row_sum", [P, 2, 8])
        sink_arg = const("sink_arg", [P, 8])
        sink_exp = const("sink_exp", [P, 8])
        coef = const("coefficient", [P, 2, 8])
        assert c_at[0] <= 56 * KB, c_at
        cos_t = sb("cos", [P, S], 56)
        sin_t = sb("sin", [P, S], 58)
        R = 60
        x_t = sb("x_t", [P, KT, S], R + 131)
        x_tok = sb("x_tok", [P, NI, D], R)
        t_h = sb("t_h", [P, KT, S], R)
        ada = sb("w_ada_shift_scale", [P, KT, 2048], R + 16)
        ada_g = sb("w_ada_gate", [P, KT, D], R + 95)
        acc = sb("ada_sum", [P, 2048], 40)
        acc_g = sb("ada_sum_gate", [P, D], R + 44)
        line = sb("bias_lines", [P, 16, LINE], R + 95)
        rel = sb("rel_bias_sb", [33, 16], R + 80)
        vec = sb("vec", [P, P], R + 93)
        vec2 = sb("vec2", [2 * CMP_T, P], R + 94)
        sqx = sb("sqx", [P, D], R + 83)
        onehot = sb("onehot", [33, 2, LINE], R + 87)
        band_a = sb("band_a", [P, 8, 256], R)
        band_b = sb("band_b", [P, 8, S], R + 8)
        w1 = sb("w_cmp1", [P, CMP_T, 256], R + 24)
        shifted = sb("shifted", [P, 2, S], R + 40)
        xp = sb("cmp_in", [P, CMP_T, 2, NC_PAD], R + 44)
        h_hi = sb("h_hi", [P, KT, S], R + 48, F32R)
        h_lo = sb("h_lo", [P, KT, S], R + 64, F32R)
        proj = sb("proj", [P, 24, S], R + 80)
        ka0 = sb("k_local_group0", [P, S], R + 128)
        rs_bc = sb("rstd_wide", [P, 2, S], R + 40)
        gb_t = sb("gates_t", [P, S], R + 44)
        hid = sb("cmp_hidden", [P, 2, 64], R + 130.25)
        hid_v = sb("cmp_hidden_v", [P, 2, 2, 4, NC_PAD], R + 24)
        sc = sb("scores_sb", [P, 2, S], R + 24)
        pt = sb("probs_t", [P, 2, S], R + 28)
        ob = sb("out_b", [P, NI, S], R + 32)
        oa = sb("out_a", [P, S], R + 40)
        o_tmp = sb("out_tmp", [P, S], R + 42)
        y_f = sb("y_f", [P, 2, NI, P], R + 44)
        y_hi = sb("y_hi", [P, KT, S], R + 48, F32R)
        y_lo = sb("y_lo", [P, KT, S], R + 64, F32R)
        g_hi = sb("g_hi", [P, KT, S], R, F32R)
        g_lo = sb("g_lo", [P, KT, S], R + 16, F32R)
        ya = sb("ya", [P, KT, S], R + 32)
        conv_ev = sb("conv_evac", [P, 2, 3, S], R + 48)
        t_g = sb("t_g", [P, KT, S], R + 60)
        u_pad = sb("u_pad", [P, S + 2], R + 76.5)
        conv_t = sb("conv_t", [P, S], R + 79)
        tt = sb("temps", [P, 5, S], R + 88)
        a_hi = sb("a_hi", [P, KT, S], R + 99, F32R)
        a_lo = sb("a_lo", [P, KT, S], R + 115, F32R)
        ret = sb("ret", [P, 16, S], R + 48)
        ret_hi = sb("ret_hi", [P, 16, S], R + 48, F32R)
        ret_lo = sb("ret_lo", [P, 16, S], R + 99, F32R)
        strip = sb("strip", [P, STRIP], R + 80)
        delta = sb("delta", [P, STRIP], R + 83.5)
        strip2 = sb("strip2", [P, STRIP], R + 87)
        v_t = sb("v_t", [P, 2, S], R + 91)
        p_f = sb("p_f", [P, 2, S], R + 95)
        q_hi = sb("q_hi", [P, 2, S], R + 99, F32R)
        q_lo = sb("q_lo", [P, 2, S], R + 103, F32R)
        k_hi = sb("k_hi", [P, 2, S], R + 107, F32R)
        k_lo = sb("k_lo", [P, 2, S], R + 111, F32R)
        v_hi = sb("v_hi", [P, NI, S], R + 115, F32R)
        v_lo = sb("v_lo", [P, NI, S], R + 123, F32R)
        p_hi = sb("p_hi", [P, NI, S], R + 131, F32R)
        p_lo = sb("p_lo", [P, NI, S], R + 139, F32R)
        qk_raw = sb("qk_raw", [P, 4, S], R + 131)
        rot_t = sb("rot_t", [P, 2, S], R + 139)
        rot_o = sb("rot_o", [P, 2, S], R + 143)
        sg = sb("silu_g", [P, 4, S], R + 80)
        head_sum = sb("head_sum", [P, S], R + 88)
        head_sq = sb("head_sq", [P, 2, S], R + 90)
        head_ssq = sb("head_ssq", [P, S], R + 94)
        val = sb("ret_val", [P, S], R + 96)
        val2 = sb("ret_val2", [P, S], 56)
        val3 = sb("ret_val3", [P, S], 58)
        sig_r = sb("sigmoid_r", [P, KT, S], R + 131)
        yr_t = sb("yr_part", [P, 2, S], 56)
        mg_t = sb("merged_t", [P, S], R + 96)
        m_hi = sb("m_hi", [P, KT, S], R, F32R)
        m_lo = sb("m_lo", [P, KT, S], R + 16, F32R)
        x1_back = sb("x1_back", [P, KT, S], R + 80)
        tt_o = sb("temps_o", [P, 5, S], R + 32)
        t_f = sb("t_f", [P, KT, S], R + 48)
        f_hi = sb("f_hi", [P, KT, S], R + 99, F32R)
        f_lo = sb("f_lo", [P, KT, S], R + 115, F32R)
        act_hi = sb("act_hi", [P, FT, S], R, F32R)
        act_lo = sb("act_lo", [P, FT, S], R + 44, F32R)
        y_out = sb("y_out", [P, KT, S], R + 99)
        out_tok = sb("out_tok", [P, NI, D], R)

        ps = nc.alloc_psum_tensor("ps", [P, 8, S], F32)

        raw_in = [sem(f"raw_in{s}") for s in range(SLOTS)]
        raw_in2 = [sem(f"raw_in2_{s}") for s in range(SLOTS)]
        hi_done, lo_done = sem("hi_done"), sem("lo_done")
        unit_done = sem("unit_done")
        evac = sem("evac")
        names = ("dve_own pool_own vec_in vec2_in misc_in x_in adag_in onehot_in line_out band_in w1_in sh_in "
                 "tab_in consts csilu_done col_t col_done x_tr x_ev sumsq_done line_mm line_ev "
                 "rms_in rms_rs rms_bc ada_done mod_mm mod_done th_done hh_done hl_done adag_done modg_mm "
                 "band_fill sq_done st_mm hms_done hrs_done bc_mm qk_done gb_mm gb_add gb_done "
                 "xp_done c1_mm hid_done c2_mm kc_ev kcsq_done kst_mm rw_done kms_done krs_done kbc_mm kcmp_done vbd_done "
                 "vt_mm vt_ev cs_mm csub_done cexp_done ctr_mm cpt_d cpt_a co_mm co_done "
                 "s_mm s_bias s_exp t_mm pt_d pt_a pv_mm comb_done arg_done sinkexp_done ytr_mm yf_done yh_done yl_done "
                 "spill_done lgexp_done delta_done af_done ah_done al_done "
                 "lgt_done strip_done rot_done qkh_done qkl_done vtr_mm vh_done vl_done rs_mm pm_done ph_done pl_done rpv_mm "
                 "hsum_done mu_mm sub_done hsq_done hssq_done rst_mm rms2_done rrs_done rbc_mm val_done rh_done rl_done "
                 "back_in pool_own2 ob_done decay_done hpair_done ret_ev far_done mg_done mh_done ml_done prod_done fh_done fl_done fin_mm fin_a fin_d out_done").split()
        m = {n: sem(n) for n in names}
        ada_in = [sem(f"ada_in{k}") for k in range(KT // 2)]
        nrm = {n: sem(n) for n in ("x_done xsq_done ss_done nst_mm ms_done rs_done nbc_mm t_done h_done l_done").split()}

        k_group0 = (ka0[:], proj[:, KC], proj[:, VC])

        def gate_of(branch):
            return gates[:].rearrange("p i (h b) -> p i h b", b=3)[:, :, :, branch]

        def pe_unit(pe, it, per, u, per_o, o, mov_hi, mov_lo, kts=KT, k0=0, first=True, last=True,
                    hi_sem=None, lo_sem=None, base=0):
            slot, bank = u % SLOTS, ps[:, o % 4]
            pe.wait_ge(hi_done, at(it, per, u + 1))
            pe.wait_ge(lo_done, at(it, per, u + 1))
            if first and o >= 4:
                pe.wait_ge(evac, at(it, per_o, o - 3))
            passes = ((whi, mov_hi, hi_sem), (wlo, mov_hi, None), (whi, mov_lo, lo_sem))
            for n, (w, mov, ready) in enumerate(passes):
                for k in range(kts):
                    if ready is not None:
                        pe.wait_ge(ready, base + k0 + k + 1)
                    mm = pe.matmul(bank, w[:, slot, k], mov[:, k0 + k],
                                   start=first and n == 0 and k == 0,
                                   stop=last and n == 2 and k == kts - 1)
            mm.then_inc(unit_done, 1)

        def act_convert(act, it, per, u, kts=KT):
            slot = u % SLOTS
            act.wait_ge(raw_in[slot], at(it, 4 * per, 16 * (u // SLOTS + 1)))
            if u < U_PAIRED:
                act.wait_ge(raw_in2[slot], at(it, 4 * per, 16 * (u // SLOTS + 1)))
            if u >= SLOTS:
                act.wait_ge(unit_done, at(it, per, u - 3))
            act.activation(whi[:, slot, 0:kts], raw[:, slot, 0:kts], ACT.Copy).then_inc(hi_done, 1)

        def dve_convert(dve, it, per, u, kts=KT):
            slot = u % SLOTS
            dve.wait_ge(hi_done, at(it, per, u + 1))
            nc.vector.tensor_tensor(wlo[:, slot, 0:kts], raw[:, slot, 0:kts], whi[:, slot, 0:kts].bitcast(F32),
                                    ALU.subtract).then_inc(lo_done, 1)

        def act_out(act, it, per, u, dst, o, func, scale=1.0):
            count = at(it, per, u + 1)
            apart(act, it)
            act.wait_ge(unit_done, count)
            act.activation(dst, ps[:, o % 4], func, scale=scale).then_inc(evac, 1)

        def apart(eng, it):
            if it is not None:
                eng.wait_ge(hi_done, 1)

        def tile_of(t, it, per, n):
            if it is None:
                return t[:, n]
            return t[:, bass.ds(it * per + n, 1)].rearrange("p a n -> p (a n)")

        def col_of(t, it, per, n):
            return t[:, n:n + 1] if it is None else t[:, bass.ds(it * per + n, 1)]

        w_in_v = w_in[0].rearrange("(k p) n -> p k n", p=P)
        w_out_v = w_out[0].rearrange("(k p) n -> p k n", p=P)
        w_in2_v = w_in_2[0].rearrange("(k p) n -> p k n", p=P)
        w_ya_v = w_a_out_2[0].rearrange("(k p) n -> p k n", p=P)
        w_yr_v = w_r_out_2[0].rearrange("(k p) n -> p k n", p=P)
        w_o_v = w_o_2[0].rearrange("(k p) n -> p k n", p=P)
        w_g_v = w_ff_gate_2[0].rearrange("(k p) n -> p k n", p=P)
        w_u_v = w_ff_up_2[0].rearrange("(k p) n -> p k n", p=P)
        w_d_v = w_ff_down_2[0].rearrange("(k p) n -> p k n", p=P)
        w_ada_v = w_ada[0].rearrange("(k p) n -> p k n", p=P)

        block = stack.enter_context(nc.Block())

        @block.sync
        def _(sp):
            for first, src in ((V_C, c), (V_ADA, b_ada), (V_NORM, norm_gain)):
                n = src.shape[1] // P
                sp.dma_start(vec[first:first + n, :], src.rearrange("a (m p) -> (a m) p", p=P)).then_inc(m["vec_in"], 16)
            sp.dma_start(x_tok[:], x[0].rearrange("(i p) d -> p i d", p=P)).then_inc(m["x_in"], 16)
            for k in range(KT):
                sp.dma_start(ada[:, k], w_ada_v[:, k, 0:2048]).then_inc(ada_in[k // 2], 16)
            def load(it, per, u, src, kts=KT):
                slot = u % SLOTS
                if u >= SLOTS:
                    converted = at(it, per, u - 3)
                    apart(sp, it)
                    sp.wait_ge(hi_done, converted)
                    sp.wait_ge(lo_done, converted)
                sp.dma_start(raw[:, slot, 0:kts], src).then_inc(raw_in[slot], 16)

            def load_pair(u, dst, dst2, src, src2):
                if u >= SLOTS:
                    sp.wait_ge(hi_done, u - 3)
                    sp.wait_ge(lo_done, u - 3)
                sp.dma_start(dst, src).then_inc(raw_in[u % SLOTS], 16)
                sp.dma_start(dst2, src2).then_inc(raw_in2[u % SLOTS], 16)

            def load_halves(u, cut):
                r, w = raw[:, u % SLOTS], w_in_v[:, :, cut:cut + P]
                load_pair(u, r[:, 0:4], r[:, 4:8], w[:, 0:4], w[:, 4:8])

            for u in range(4):
                load_halves(u, IN_COLS[u])
            sp.wait_ge(m["line_out"], 16)
            sp.wait_ge(m["far_done"], 1)
            for k in range(0, KT, 4):
                sp.dma_start(ada_g[:, k:k + 4], w_ada_v[:, k:k + 4, 2048:3072]).then_inc(m["adag_in"], 16)
            for u in range(4, 8):
                load_halves(u, IN_COLS[u])
            for u in range(8, 16):
                a = Q_COLS[(u - 8) // 4] + (u % 4) * HD
                r = raw[:, u % SLOTS]
                load_pair(u, r[:, :, 0:HD], r[:, :, HD:P], w_in_v[:, :, a:a + HD],
                          w_in_v[:, :, a + 4 * HD:a + 5 * HD])
            for u in range(16, 24):
                a = Z_COLS[(u - 16) // 4] + (u % 4) * P
                if u < U_PAIRED:
                    load_halves(u, a)
                else:
                    load(None, 0, u, w_in_v[:, :, a:a + P])
            load(None, 0, U_GB, w_in_v[:, :, GB_COL + 24 - P:GB_COL + 24])

            def wide(n):
                return bass.ds(n, P)

            with sp.Fori(0, 2) as it:
                for k in range(4):
                    load(it, 4, U_WO + k, w_out_v[:, :, wide(it * 512 + k * P)])
            with sp.Fori(0, 2) as it:
                for t in range(4):
                    for n, off in enumerate((0, 2048, 1024)):
                        load(it, 12, U_CONV + 3 * t + n, w_in2_v[:, :, wide(it * 512 + off + t * P)])
            with sp.Fori(0, 4) as it:
                for t in range(2):
                    load(it, 4, U_YA + 2 * t, w_in2_v[:, :, wide(it * 256 + GA_COL + t * P)])
                    load(it, 4, U_YA + 2 * t + 1, w_ya_v[:, :, wide((it * 2 + t) * P)])
            with sp.Fori(0, 4) as it:
                for k in range(8):
                    if k < 4:
                        cut = it * 256 + (3072 + 1024 * (k // 2) + (k % 2) * P)
                    else:
                        cut = it * 512 + (5120 + (k - 4) * P)
                    load(it, 8, U_QKV + k, w_in2_v[:, :, wide(cut)])
            with sp.Fori(0, 2) as it:
                for k in range(12):
                    h, n = divmod(k, 6)
                    if n >= 2:
                        cut = it * 1024 + (7168 + h * 512 + (n - 2) * P)
                    else:
                        cut = it * 512 + (GR_COL + h * 256 + n * P)
                    load(it, 12, U_GATE + k, w_in2_v[:, :, wide(cut)])
            with sp.Fori(0, 2) as it:
                for k in range(8):
                    half = k % 2
                    load(it, 8, U_YR + k, w_yr_v[:, 8 * half:8 * half + 8, wide(it * 512 + (k // 2) * P)])
            with sp.Fori(0, 2) as it:
                for k in range(4):
                    load(it, 4, U_O + k, w_o_v[:, :, wide(it * 512 + k * P)])
            with sp.Fori(0, FT // 2) as it:
                for t in range(2):
                    load(it, 4, U_FF + 2 * t, w_g_v[:, :, wide(it * 256 + t * P)])
                    load(it, 4, U_FF + 2 * t + 1, w_u_v[:, :, wide(it * 256 + t * P)])
            with sp.Fori(0, 2) as it:
                for k in range(12):
                    t, part = divmod(k, 3)
                    kts = KT if part < 2 else FT - 2 * KT
                    load(it, 12, U_DOWN + k, w_d_v[:, 8 * part:8 * part + kts, wide(it * 512 + t * P)], kts)
            for n, i in enumerate(FIN_ORDER):
                sp.wait_ge(m["fin_a"], n + 1)
                sp.wait_ge(m["fin_d"], n + 1)
                sp.dma_start(out[0].rearrange("(i p) d -> p i d", p=P)[:, i], out_tok[:, i]).then_inc(m["out_done"], 16)
            sp.wait_ge(m["out_done"], 16 * NI)

        @block.gpsimd
        def _(pool):
            g = nc.gpsimd
            own = Own(pool, m["pool_own"])
            pool.dma_start(onehot[:], bias_onehot).then_inc(m["onehot_in"], 16)
            pool.dma_start(rel[0:32, :], rel_bias).then_inc(m["onehot_in"], 16)
            own(g.memset(rel[32:33, :], BIG))
            own.wait()
            own(g.memset(ident[:], 0.0))
            own(g.memset(half_sel[:], 1.0 / HD))
            own(g.memset(cmask[:], 0.0))
            own.wait()
            own(g.affine_select(out=ident[:], in_=ident[:], compare_op=ALU.not_equal, fill=1.0, base=0,
                                pattern=[[-1, P]], channel_multiplier=1))
            own(g.affine_select(out=half_sel[:, 0:1], in_=half_sel[:, 0:1], compare_op=ALU.is_ge, fill=0.0,
                                base=HD - 1, pattern=[[0, 1]], channel_multiplier=-1))
            own(g.affine_select(out=half_sel[:, 1:2], in_=half_sel[:, 1:2], compare_op=ALU.is_ge, fill=0.0,
                                base=-HD, pattern=[[0, 1]], channel_multiplier=1))
            own(g.affine_select(out=cmask[:], in_=cmask[:], compare_op=ALU.is_ge, fill=BIG, base=-31,
                                pattern=[[P, NI], [-16, NC_PAD]], channel_multiplier=1))
            own(g.memset(mean512[:], 1.0 / 512))
            own(g.memset(minus_half[:], -0.5))
            own.wait()
            g.memset(ones1[:], 1.0).then_inc(m["consts"], 1)

            pool.dma_start(nsink[:], sinks.partition_broadcast(P)).then_inc(m["misc_in"], 16)
            pool.dma_start(gate_bias[:], b_nsa_gate.partition_broadcast(P)).then_inc(m["misc_in"], 16)
            pool.dma_start(decay[:, 0:4], dec_f_2.partition_broadcast(P)).then_inc(m["misc_in"], 16)
            pool.dma_start(decay[:, 4:8], dec_b_2.partition_broadcast(P)).then_inc(m["misc_in"], 16)
            for dst, w in ((w2k[:, :, 0], w_cmp_k2), (w2k[:, :, 1], w_cmp_k2), (w2v[:], w_cmp_v2)):
                pool.dma_start(dst, w[0].rearrange("(k p) d -> p k d", p=P)).then_inc(m["misc_in"], 16)
            def rows(dst, first, src):
                pool.dma_start(dst[first:first + src.shape[0], :], src).then_inc(m["vec2_in"], 16)

            for head, src in enumerate((q_gain_a, q_gain_b, k_gain_a, k_gain_cmp, k_gain_sel, k_gain_win)):
                for half in range(2):
                    pool.dma_start(vec[V_GAIN + head:V_GAIN + head + 1, half * HD:(half + 1) * HD],
                                   src).then_inc(m["vec2_in"], 16)
            rows(vec, V_CONV, w_conv_2.rearrange("a t (m p) -> (a t m) p", p=P))
            rows(vec, V_RET, g_ret_2.rearrange("a (m p) -> (a m) p", p=P))
            rows(vec, V_MIX, g_mix_2.rearrange("a (m p) -> (a m) p", p=P))
            rows(vec, V_FFN, g_ffn_2.rearrange("a (m p) -> (a m) p", p=P))
            rows(vec, V_FIN, g_final_2.rearrange("(m p) -> m p", p=P))
            rows(vec2, 0, cmp_pos_k.rearrange("a (q l) d -> (a q) (l d)", l=2))
            rows(vec2, CMP_T, cmp_pos_v.rearrange("a (q l) d -> (a q) (l d)", l=2))

            def rsqrt(dst, src, n, parts=P):
                return g.tensor_tensor(dst, src, minus_half[0:parts, :].to_broadcast([parts, n]), ALU.pow)

            pool.wait_ge(m["rms_in"], 1)
            rsqrt(rstd[:], msq[:], NI).then_inc(m["rms_rs"], 1)

            pool.wait_ge(m["line_ev"], 16)
            pool.wait_ge(m["ada_done"], 1)
            pool.dma_start(line_dram, line[:]).then_inc(m["line_out"], 16)
            pool.wait_ge(m["line_out"], 16)
            pool.wait_ge(m["hl_done"], KT)
            skew = [[16 * LINE - 1, P], [LINE, 8], [1, 256]]
            pool.dma_start(band_a[:], bass.AP(line_dram.tensor, 127, skew)).then_inc(m["band_in"], 16)
            pool.dma_start(band_b[:, :, 256:512],
                           bass.AP(line_dram.tensor, 8 * LINE + 127, skew)).then_inc(m["band_in"], 16)
            for n, (w, t) in enumerate(((w_cmp_k1, KC), (w_cmp_v1, VC))):
                if n:
                    pool.wait_ge(m["c1_mm"], 1)
                pool.dma_start(w1[:], w[0].rearrange("(q p) d -> p q d", p=P)).then_inc(m["w1_in"], 16)
                pool.wait_ge(evac, t + 1)
                if n:
                    pool.wait_ge(m["xp_done"], 1)
                for half in range(2):
                    for l in range(2):
                        pool.dma_start(shifted[HD * l:HD * l + HD, half, 0:S - l],
                                       proj[HD * half:HD * half + HD, t, l:S]).then_inc(m["sh_in"], 16)
            for n, (a, b) in enumerate(NORM_GROUPS):
                if n == 1:
                    pool.wait_ge(m["kms_done"], 1)
                    rsqrt(kc_rs[0:NC_PAD, :], kc_ms[0:NC_PAD, :], 2, NC_PAD).then_inc(m["krs_done"], 1)
                pool.wait_ge(m["hms_done"], n + 1)
                rsqrt(rstd_h[:, 8 * a:8 * b], msq_h[:, 8 * a:8 * b], 8 * (b - a)).then_inc(m["hrs_done"], 1)

            def norm_rs(q):
                pool.wait_ge(nrm["ms_done"], q + 1)
                rsqrt(rstd[:], msq[:], NI).then_inc(nrm["rs_done"], 1)

            norm_rs(0)
            pool.dma_start(cos_t[:], rope_cos).then_inc(m["tab_in"], 16)
            pool.dma_start(sin_t[:], rope_sin).then_inc(m["tab_in"], 16)
            pool.wait_ge(nrm["t_done"], KT)
            pool.dma_start(x1_dram, x_t[:]).then_inc(m["spill_done"], 16)
            pool.wait_ge(m["al_done"], 8)
            g.iota(delta[:], [[1, STRIP]], base=-(NI - 1) * P, channel_multiplier=-1,
                   allow_small_or_imprecise_dtypes=True).then_inc(m["delta_done"], 1)
            pool.wait_ge(m["spill_done"], 16)

            hown = Own(pool, m["pool_own2"])
            pool.wait_ge(m["ret_ev"], 16)
            with pool.Fori(0, 2) as it:
                hown.begin(it, 6)
                for hh in range(2):
                    r = [tile_of(ret, it, 8, 4 * hh + t) for t in range(4)]
                    hown(g.tensor_tensor(head_sum[:], r[0], r[1], ALU.add))
                    hown.wait()
                    hown(g.tensor_tensor(head_sum[:], head_sum[:], r[2], ALU.add))
                    hown.wait()
                    g.tensor_tensor(head_sum[:], head_sum[:], r[3], ALU.add).then_inc(m["hsum_done"], 1)
                    pool.wait_ge(m["hsq_done"], at(it, 8, 4 * hh + 2))
                    g.tensor_tensor(head_ssq[:], head_sq[:, 0], head_sq[:, 1], ALU.add).then_inc(m["hpair_done"], 1)
                    pool.wait_ge(m["hpair_done"], at(it, 2, hh + 1))
                    pool.wait_ge(m["hsq_done"], at(it, 8, 4 * hh + 3))
                    hown(g.tensor_tensor(head_ssq[:], head_ssq[:], head_sq[:, 0], ALU.add))
                    hown.wait()
                    pool.wait_ge(m["hsq_done"], at(it, 8, 4 * hh + 4))
                    g.tensor_tensor(head_ssq[:], head_ssq[:], head_sq[:, 1], ALU.add).then_inc(m["hssq_done"], 1)
                    pool.wait_ge(m["rms2_done"], at(it, 2, hh + 1))
                    rsqrt(rstd[:], msq[:], NI).then_inc(m["rrs_done"], 1)
            hown.end(2)
            pool.wait_ge(m["rl_done"], 16)
            pool.dma_start(x1_back[:], x1_dram).then_inc(m["back_in"], 16)
            norm_rs(1)
            norm_rs(2)

        @block.scalar
        def _(act):
            a = nc.scalar
            act.wait_ge(m["col_done"], 1)
            a.activation(csilu[:], col[:, V_C:V_C + 8], ACT.Silu).then_inc(m["csilu_done"], 1)
            for h in range(16):
                act.wait_ge(m["line_mm"], h + 1)
                a.activation(line[:, h], ps[:, 4 + h % 3, 0:LINE], ACT.Copy).then_inc(m["line_ev"], 1)
            act.wait_ge(m["line_ev"], 16)
            a.activation(line_far[:], line[:, 8:16, 0:1].rearrange("p h n -> p (h n)"), ACT.Copy).then_inc(m["far_done"], 1)
            act.wait_ge(m["x_in"], 16)
            for i in range(NI):
                if i:
                    act.wait_ge(m["sumsq_done"], i)
                a.activation(sqx[:], x_tok[:, i], ACT.Square, accum_out=sumsq[:, i:i + 1]).then_inc(m["sumsq_done"], 1)
            for k in range(KT):
                act.wait_ge(m["x_tr"], k + 1)
                a.activation(x_t[:, k], ps[:, k % 4], ACT.Copy).then_inc(m["x_ev"], 1)
            act_convert(act, None, 0, 0)
            act_convert(act, None, 0, 1)
            act.wait_ge(m["mod_done"], 1)
            for k in range(KT):
                act.wait_ge(m["th_done"], k + 1)
                a.activation(h_hi[:, k], t_h[:, k], ACT.Identity, bias=mod[:, k:k + 1]).then_inc(m["hh_done"], 1)
            for n in range(8):
                act_convert(act, None, 0, n + AHEAD)
                if n == 7:
                    act.wait_ge(m["adag_done"], 1)
                act_out(act, None, 0, n, proj[:, n], n, ACT.Copy)
            with act.Fori(0, 2) as it:
                for k in range(8, 12):
                    act_convert(act, it, 4, k + AHEAD)
                    act_out(act, it, 4, k, tile_of(proj, it, 4, k), k, ACT.Copy)
            def square(t):
                if t >= 4:
                    act.wait_ge(m["st_mm"], t - 3)
                else:
                    act.wait_ge(evac, NORM_TILES[t] + 1)
                a.activation(proj[:, 20 + t % 4], proj[:, NORM_TILES[t]], ACT.Square).then_inc(m["sq_done"], 1)

            for n in range(16, 24):
                act_convert(act, None, 0, n + AHEAD)
                if n == 16:
                    act.wait_ge(m["c1_mm"], 1)
                    a.activation(hid[:], ps[:, 7, 0:128].rearrange("p (c n) -> p c n", c=2), ACT.Silu).then_inc(m["hid_done"], 1)
                if n == 17:
                    act.wait_ge(m["c2_mm"], 1)
                    for g in range(2):
                        half = slice(g * HD, (g + 1) * HD)
                        a.activation(kcmp[half, :], ps[half, 7, 128 + 32 * g:160 + 32 * g], ACT.Copy).then_inc(m["kc_ev"], 1)
                    act.wait_ge(m["kc_ev"], 2)
                    a.activation(kc_sq[:], kcmp[:], ACT.Square).then_inc(m["kcsq_done"], 1)
                if n == 22:
                    act.wait_ge(m["c1_mm"], 2)
                    for t in range(2):
                        hidden = ps[:, 7, 192 + 64 * t:256 + 64 * t].rearrange("p (g n) -> p g n", g=2)
                        a.activation(hid_v[:, t], hidden.unsqueeze(2).to_broadcast([P, 2, 4, NC_PAD]),
                                     ACT.Silu).then_inc(m["hid_done"], 1)
                if n < 19:
                    for t in range(*NORM_GROUPS[n - 16]):
                        square(t)
                for t in BCAST_AT.get(n, ()):
                    act.wait_ge(m["hrs_done"], norm_group(t) + 1)
                    if t == 0:
                        act.wait_ge(m["xp_done"], 2)
                    if t >= 2:
                        act.wait_ge(m["bc_mm"], t - 1)
                    a.activation(rs_bc[:, t % 2].rearrange("p (n d) -> p n d", d=HD),
                                 rstd_h[:, 8 * t:8 * t + 8].unsqueeze(2).to_broadcast([P, 8, HD]),
                                 ACT.Copy).then_inc(m["rw_done"], 1)
                if n == 20:
                    act.wait_ge(m["st_mm"], 11)
                act_out(act, None, 0, n, proj[:, n], n, ACT.Silu)
            act_convert(act, None, 0, U_GB + AHEAD)
            act.wait_ge(m["csub_done"], 1)
            a.activation(sc[:], sc[:], ACT.Exp, scale=-1.0).then_inc(m["cexp_done"], 1)
            act_out(act, None, 0, U_GB, gb_t[:], O_GB, ACT.Copy)
            for n, t in enumerate((VA, VS, VW)):
                act.wait_ge(m["vt_mm"], n + 1)
                a.activation(proj[:, t], ps[:, 5 + n], ACT.Copy).then_inc(m["vt_ev"], 1)
            act.wait_ge(m["ctr_mm"], 1)
            a.activation(pt[:, 0], ps[:, 2], ACT.Copy).then_inc(m["cpt_a"], 1)
            act.wait_ge(m["gb_add"], 1)
            a.activation(gates[:], gates[:], ACT.Sigmoid).then_inc(m["gb_done"], 1)

            for s in range(STEPS):
                if s < N_ATT:
                    G, n = divmod(s, 8)
                    act.wait_ge(m["s_bias"], s + 1)
                    if n == 0 and G >= 2:
                        act.wait_ge(m["comb_done"], G - 1)
                    w = att(s).width
                    a.activation(sc[:, s % 2, 0:w], sc[:, s % 2, 0:w], ACT.Exp, scale=-1.0,
                                 bias=row_min[:, G % 2, n:n + 1],
                                 accum_out=den[:, G % 2, att(s).head:att(s).head + 1]).then_inc(m["s_exp"], 1)
                t = s - 1
                if 0 <= t < N_ATT and t % 2 == 1:
                    act.wait_ge(m["t_mm"], t + 1)
                    if t >= 2:
                        act.wait_ge(m["pv_mm"], t - 1)
                    w = att(t).width
                    a.activation(pt[:, 1, 0:w], ps[:, 3, 0:w], ACT.Copy).then_inc(m["pt_a"], 1)
                G, n = divmod(s, 8)
                if n == 0 and G >= 1 and G <= N_GROUPS and (G - 1) % 3 == 0:
                    act.wait_ge(m["arg_done"], (G - 1) // 3 + 1)
                    a.activation(sink_exp[:], sink_arg[:], ACT.Exp).then_inc(m["sinkexp_done"], 1)
                for half in range(2):
                    i = tail_at(s - half - 1)
                    if i is not None:
                        act.wait_ge(m["yf_done"], 2 * i + half + 1)
                        a.activation(y_hi[:, 4 * half:4 * half + 4, i * P:(i + 1) * P], y_f[:, half],
                                     ACT.Copy).then_inc(m["yh_done"], 1)

            def out_and_square(it, per, u, per_o, o, q, t, scale):
                act_out(act, it, per, u, t[:, o % 2], o, ACT.Copy, scale)
                count = at(it, per_o, q * KT + o - NORM_O[q] + 1)
                apart(act, it)
                act.wait_ge(nrm["x_done"], count)
                a.activation(t[:, 2 + o % 2], tile_of(x_t, it, per_o, o - NORM_O[q]), ACT.Square).then_inc(nrm["xsq_done"], 1)

            def round_norm(q, dst, t):
                for k in range(KT):
                    act.wait_ge(nrm["t_done"], q * KT + k + 1)
                    a.activation(dst[:, k], t[:, k], ACT.Copy).then_inc(nrm["h_done"], 1)

            with act.Fori(0, 2) as it:
                for k in range(4):
                    act_convert(act, it, 4, U_WO + k + AHEAD)
                    out_and_square(it, 4, U_WO + k, 4, O_WO + k, 0, tt, col_of(mod, it, 4, 16 + k))
            round_norm(0, g_hi, t_g)
            act.wait_ge(m["lgt_done"], 1)
            a.activation(lt[:, 1], lt[:, 0], ACT.Exp, scale=-1.0).then_inc(m["lgexp_done"], 1)
            with act.Fori(0, 2) as it:
                for t in range(4):
                    for n in range(3):
                        act_convert(act, it, 12, U_CONV + 3 * t + n + AHEAD)
                        act_out(act, it, 12, U_CONV + 3 * t + n, conv_ev[:, t % 2, n], O_CONV + 3 * t + n, ACT.Copy)
                    count = at(it, 4, t + 1)
                    apart(act, it)
                    act.wait_ge(m["af_done"], count)
                    a.activation(tile_of(a_hi, it, 4, t), tt[:, t % 2], ACT.Copy).then_inc(m["ah_done"], 1)
            with act.Fori(0, 4) as it:
                for t in range(2):
                    act_convert(act, it, 4, U_YA + 2 * t + AHEAD)
                    act_out(act, it, 4, U_YA + 2 * t, tt[:, t], O_YA + 2 * t, ACT.Sigmoid)
                    act_convert(act, it, 4, U_YA + 2 * t + 1 + AHEAD)
                    act_out(act, it, 4, U_YA + 2 * t + 1, tt[:, 2 + t], O_YA + 2 * t + 1, ACT.Copy)
            act.wait_ge(m["spill_done"], 16)
            with act.Fori(0, RET_HEADS) as it:
                def p_round(j):
                    act.wait_ge(m["pm_done"], at(it, 4, j + 1))
                    a.activation(p_hi[:, j], p_f[:, j % 2], ACT.Copy).then_inc(m["ph_done"], 1)

                def v_round(t):
                    act.wait_ge(m["vtr_mm"], at(it, 4, t + 1))
                    a.activation(v_hi[:, :, t * P:(t + 1) * P],
                                 ps[:, 4 + t].rearrange("p (j e) -> p j e", j=NI), ACT.Copy).then_inc(m["vh_done"], 1)

                for k in range(8):
                    act_convert(act, it, 8, U_QKV + k + AHEAD)
                    dst = qk_raw[:, k] if k < 4 else v_t[:, k % 2]
                    act_out(act, it, 8, U_QKV + k, dst, O_QKV + k, ACT.Copy)
                    if k == 1:
                        act.wait_ge(m["strip_done"], at(it, 1, 1))
                        a.activation(strip[:], strip[:], ACT.Exp).then_inc(m["decay_done"], 1)
                    if k in (3, 5):
                        dst = q_hi if k == 3 else k_hi
                        act.wait_ge(m["rot_done"], at(it, 2, (k - 1) // 2))
                        for t in range(2):
                            a.activation(dst[:, t], rot_o[:, t], ACT.Copy).then_inc(m["qkh_done"], 1)
                    if k >= 5:
                        v_round(k - 5)
                for j in range(3):
                    p_round(j)
                v_round(3)
                p_round(3)
                for t in range(4):
                    count = at(it, 4, t + 1)
                    apart(act, it)
                    act.wait_ge(m["rpv_mm"], count)
                    a.activation(tile_of(ret, it, 4, t), ps[:, PV_BANK[t]], ACT.Copy).then_inc(m["ret_ev"], 1)
            with act.Fori(0, 2) as it:
                for k in range(12):
                    hh, n = divmod(k, 6)
                    act_convert(act, it, 12, U_GATE + k + AHEAD)
                    if n >= 2:
                        act_out(act, it, 12, U_GATE + k, sg[:, n - 2], O_GATE + k, ACT.Silu)
                    else:
                        act_out(act, it, 12, U_GATE + k, tile_of(sig_r, it, 4, 2 * hh + n), O_GATE + k, ACT.Sigmoid)
                    if n == 1:
                        for t in range(4):
                            act.wait_ge(m["sub_done"], at(it, 8, 4 * hh + t + 1))
                            if t >= 2:
                                count = at(it, 2, hh + 1)
                                apart(act, it)
                                act.wait_ge(m["hpair_done"], count)
                            a.activation(head_sq[:, t % 2], tile_of(ret, it, 8, 4 * hh + t), ACT.Square).then_inc(m["hsq_done"], 1)
                    if n == 5:
                        for t in range(4):
                            count = at(it, 8, 4 * hh + t + 1)
                            apart(act, it)
                            act.wait_ge(m["val_done"], count)
                            a.activation(tile_of(ret_hi, it, 8, 4 * hh + t), (val2, val3)[t % 2][:],
                                         ACT.Copy).then_inc(m["rh_done"], 1)
            with act.Fori(0, 2) as it:
                for k in range(8):
                    act_convert(act, it, 8, U_YR + k + AHEAD)
                    if k % 2:
                        act_out(act, it, 8, U_YR + k, yr_t[:, (k // 2) % 2], O_YR + k // 2, ACT.Copy)
                        count = at(it, 4, k // 2 + 1)
                        apart(act, it)
                        act.wait_ge(m["mg_done"], count)
                        a.activation(tile_of(m_hi, it, 4, k // 2), mg_t[:], ACT.Copy).then_inc(m["mh_done"], 1)
            with act.Fori(0, 2) as it:
                for k in range(4):
                    act_convert(act, it, 4, U_O + k + AHEAD)
                    out_and_square(it, 4, U_O + k, 4, O_O + k, 1, tt_o, 1.0)
            round_norm(1, f_hi, t_f)
            with act.Fori(0, FT // 2) as it:
                for t in range(2):
                    act_convert(act, it, 4, U_FF + 2 * t + AHEAD)
                    act_out(act, it, 4, U_FF + 2 * t, tt[:, t], O_FF + 2 * t, ACT.Silu)
                    act_convert(act, it, 4, U_FF + 2 * t + 1 + AHEAD)
                    act_out(act, it, 4, U_FF + 2 * t + 1, tt[:, 2 + t], O_FF + 2 * t + 1, ACT.Copy)
                    count = at(it, 2, t + 1)
                    apart(act, it)
                    act.wait_ge(m["prod_done"], count)
                    a.activation(tile_of(act_hi, it, 2, t), tt[:, 4], ACT.Copy).then_inc(m["fh_done"], 1)

            for k in range(24):
                t, part = divmod(k, 3)
                if k + AHEAD < 24:
                    act_convert(act, None, 0, U_DOWN + k + AHEAD, KT if (k + AHEAD) % 3 < 2 else FT - 2 * KT)
                if part == 2:
                    out_and_square(None, 0, U_DOWN + k, 0, O_DOWN + t, 2, tt, 1.0)
            act.wait_ge(nrm["rs_done"], 3)
            for n, i in enumerate(FIN_ORDER):
                act.wait_ge(m["fin_mm"], n + 1 if i else 2 * NI)
                a.activation(out_tok[:, i, 0:512], ps[:, 4 + i], ACT.Copy, scale=rstd[:, i:i + 1]).then_inc(m["fin_a"], 1)

        @block.vector
        def _(dve):
            v = nc.vector
            own = Own(dve, m["dve_own"])
            dve.wait_ge(m["col_t"], 1)
            v.tensor_copy(col[:, 0:V_CONV], ps[:, 7, 0:V_CONV]).then_inc(m["col_done"], 1)
            dve.wait_ge(m["csilu_done"], 1)
            for k in range(KT):
                if k % 2 == 0:
                    dve.wait_ge(ada_in[k // 2], 32)
                if k == 0:
                    own(v.tensor_scalar(acc[:], ada[:, 0], csilu[:, 0:1], None, ALU.mult))
                else:
                    own.wait()
                    ins = v.scalar_tensor_tensor(out=acc[:], in0=ada[:, k], scalar=csilu[:, k:k + 1], in1=acc[:],
                                                 op0=ALU.mult, op1=ALU.add)
                    if k < KT - 1:
                        own(ins)
                    else:
                        ins.then_inc(m["ada_done"], 1)
                if k == 5:
                    dve.wait_ge(m["sumsq_done"], NI)
                    v.tensor_scalar(msq[:], sumsq[:], 1.0 / D, EPS, ALU.mult, ALU.add).then_inc(m["rms_in"], 1)
            for k in range(AHEAD):
                dve_convert(dve, None, 0, k)
            dve.wait_ge(m["mod_mm"], 1)
            own(v.tensor_tensor(mod[:, 8:16], ps[:, 4, 0:8], col[:, V_ADA + 8:V_ADA + 16], ALU.add))
            own.wait()
            own(v.scalar_tensor_tensor(out=s1[:], in0=mod[:, 8:16], scalar=1.0, in1=col[:, V_NORM:V_NORM + 8],
                                       op0=ALU.add, op1=ALU.mult))
            own.wait()
            dve.wait_ge(m["rms_bc"], 1)
            dve.wait_ge(m["x_ev"], KT)
            for k in range(KT):
                v.scalar_tensor_tensor(out=t_h[:, k], in0=x_t[:, k], scalar=s1[:, k:k + 1], in1=ps[:, 5],
                                       op0=ALU.mult, op1=ALU.mult).then_inc(m["th_done"], 1)
                if k == 1:
                    dve.wait_ge(m["mod_mm"], 2)
                    v.tensor_tensor(mod[:, 0:8], ps[:, 6, 0:8], col[:, V_ADA:V_ADA + 8], ALU.add).then_inc(m["mod_done"], 1)
            dve.wait_ge(m["th_done"], KT)
            dve.wait_ge(m["mod_done"], 1)
            for k in range(KT):
                dve.wait_ge(m["hh_done"], k + 1)
                v.scalar_tensor_tensor(out=h_lo[:, k], in0=t_h[:, k], scalar=mod[:, k:k + 1], in1=h_hi[:, k].bitcast(F32),
                                       op0=ALU.add, op1=ALU.subtract).then_inc(m["hl_done"], 1)
            dve.wait_ge(m["misc_in"], 16 * 7)
            own(v.tensor_scalar(nsink[:], nsink[:], -1.0, None, ALU.mult))
            for n in range(8):
                dve_convert(dve, None, 0, n + AHEAD)
                if n == 4:
                    dve.wait_ge(m["col_t"], 2)
                    own(v.tensor_copy(col[:, V_CONV:N_VEC], ps[:, 7, V_CONV:N_VEC]))
                    own(v.tensor_copy(pos_col[:], ps[:, 7, P:P + 2 * CMP_T]))
                    own.wait()
                    own(v.tensor_scalar(gains[:, 0:2], col[:, V_GAIN:V_GAIN + 2], 0.125, None, ALU.mult))
                    own(v.tensor_scalar(gains[:, 2:6], col[:, V_GAIN + 2:V_GAIN + 6], -1.0, None, ALU.mult))
                for k in (2 * n - 2, 2 * n - 1) if 1 <= n <= 4 else ():
                    if k == 0:
                        dve.wait_ge(m["adag_in"], 32)
                        own(v.tensor_scalar(acc_g[:], ada_g[:, 0], csilu[:, 0:1], None, ALU.mult))
                    else:
                        own.wait()
                        ins = v.scalar_tensor_tensor(out=acc_g[:], in0=ada_g[:, k], scalar=csilu[:, k:k + 1],
                                                     in1=acc_g[:], op0=ALU.mult, op1=ALU.add)
                        if k < KT - 1:
                            own(ins)
                        else:
                            ins.then_inc(m["adag_done"], 1)
            with dve.Fori(0, 2) as it:
                for k in range(8, 12):
                    dve_convert(dve, it, 4, k + AHEAD)

            def cmp_input(n):
                if n == 0:
                    own(v.memset(xp[:], 0.0))
                    own.wait()
                else:
                    dve.wait_ge(m["c1_mm"], 1)
                dve.wait_ge(m["sh_in"], 64 * (n + 1))
                for half in range(2):
                    src = bass.AP(shifted[:].tensor, shifted[:, half, 0:1].offset,
                                  [list(shifted[:].ap[0]), [2, CMP_T], [16, NC_PAD - 1]])
                    pos = pos_col[:, n * CMP_T:(n + 1) * CMP_T].unsqueeze(2).to_broadcast([P, CMP_T, NC_PAD - 1])
                    ins = v.tensor_tensor(xp[:, :, half, 0:NC_PAD - 1], src, pos, ALU.add)
                    if half == 0:
                        own(ins)
                    else:
                        ins.then_inc(m["xp_done"], 1)

            def head_norm(t):
                dve.wait_ge(m["bc_mm"], t + 1)
                tile = proj[:, NORM_TILES[t]]
                g = NORM_GAINS[t]
                if t >= 8:
                    low, high = slice(0, HD), slice(HD, P)
                    own(v.scalar_tensor_tensor(out=k_group0[t - 8][low, :], in0=tile[low, :], scalar=gains[low, g:g + 1],
                                               in1=ps[low, 5 + t % 2], op0=ALU.mult, op1=ALU.mult))
                    v.scalar_tensor_tensor(out=tile[high, :], in0=tile[high, :], scalar=gains[high, g:g + 1],
                                           in1=ps[high, 5 + t % 2], op0=ALU.mult, op1=ALU.mult).then_inc(m["qk_done"], 1)
                    own.wait()
                    own(v.memset(tile[low, :], 0.0))
                    return
                v.scalar_tensor_tensor(out=tile, in0=tile, scalar=gains[:, g:g + 1], in1=ps[:, 5 + t % 2],
                                       op0=ALU.mult, op1=ALU.mult).then_inc(m["qk_done"], 1)

            cmp_input(0)
            dve.wait_ge(m["band_in"], 32)
            dve.wait_ge(m["far_done"], 1)
            v.tensor_copy(band_b[:, :, 0:256], line_far[:].unsqueeze(2).to_broadcast([P, 8, 256])).then_inc(m["band_fill"], 1)
            for n in range(16, 24):
                dve_convert(dve, None, 0, n + AHEAD)
                if n == 16:
                    dve.wait_ge(m["modg_mm"], 1)
                    own(v.tensor_tensor(mod[:, 16:24], ps[:, 6, 0:8], col[:, V_ADA + 16:V_ADA + 24], ALU.add))
                if n < 19:
                    a, b = NORM_GROUPS[n - 16]
                    dve.wait_ge(m["st_mm"], b)
                    v.tensor_scalar(msq_h[:, 8 * a:8 * b], ps[:, 4, 8 * a:8 * b], EPS, None, ALU.add).then_inc(m["hms_done"], 1)
                if n == 17:
                    cmp_input(1)
                    dve.wait_ge(m["kst_mm"], 1)
                    v.tensor_scalar(kc_ms[0:NC_PAD, :], ps[0:NC_PAD, 7, 448:450], EPS, None, ALU.add).then_inc(m["kms_done"], 1)
                if n == 19:
                    dve.wait_ge(m["kbc_mm"], 1)
                    own(v.memset(kcz[:], 0.0))
                    own.wait()
                    for g in range(2):
                        half = slice(g * HD, (g + 1) * HD)
                        v.scalar_tensor_tensor(out=kcz[half, g], in0=kcmp[half, :], scalar=gains[half, 3:4],
                                               in1=ps[half, 7, 480:512], op0=ALU.mult, op1=ALU.mult).then_inc(m["kcmp_done"], 1)
                if n == 20:
                    own(v.memset(vbd[:], 0.0))
                    for k0 in k_group0:
                        own(v.memset(k0[HD:P, :], 0.0))
                for t in BCAST_AT.get(n, ()):
                    head_norm(t)
                if n == 22:
                    dve.wait_ge(m["c2_mm"], 2)
                    own.wait()
                    for g in range(2):
                        for j in range(4):
                            part = slice(32 * j, 32 * j + 32)
                            v.tensor_copy(vbd[part, g, j * HD:(j + 1) * HD],
                                          ps[part, 7, 320 + g * HD:384 + g * HD]).then_inc(m["vbd_done"], 1)
            dve_convert(dve, None, 0, U_GB + AHEAD)
            dve.wait_ge(m["cs_mm"], 1)
            for g in range(2):
                for i in range(NI):
                    own(v.tensor_tensor(sc[:, g, i * P:(i + 1) * P].rearrange("p (j n) -> p j n", j=4),
                                        ps[:, 2 + i // 2].rearrange("p (i j g n) -> p i j g n", i=2, j=4, g=2)[:, i % 2, :, g],
                                        cmask[:, i].unsqueeze(1).to_broadcast([P, 4, NC_PAD]), ALU.add))
            own.wait()
            flat = sc[:].rearrange("p g (q n) -> p (g q) n", n=NC_PAD)
            own(v.tensor_reduce(cmin[:].rearrange("p g q -> p (g q)"), flat, AX, ALU.min))
            own.wait()
            own(v.tensor_scalar(cmin[:], cmin[:], BIG / 10, None, ALU.min))
            own.wait()
            v.tensor_tensor(flat, flat, cmin[:].rearrange("p g q -> p (g q)").unsqueeze(2).to_broadcast([P, 32, NC_PAD]),
                            ALU.subtract).then_inc(m["csub_done"], 1)
            dve.wait_ge(m["gb_mm"], 1)
            bias4 = gate_bias[:].unsqueeze(1).to_broadcast([P, NI, 24])
            own.wait()
            v.tensor_tensor(gates[:], ps[:, 4].rearrange("p (i n) -> p i n", i=NI)[:, :, P - 24:P], bias4,
                            ALU.add).then_inc(m["gb_add"], 1)

            dve.wait_ge(m["cexp_done"], 1)
            own(v.tensor_reduce(cden[:].rearrange("p g q -> p (g q)"), flat, AX, ALU.add))
            own.wait()
            own(v.tensor_scalar(cden[:], cden[:], 1e-30, None, ALU.max))
            own.wait()
            own(v.reciprocal(cden[:], cden[:]))
            own.wait()
            dve.wait_ge(m["ctr_mm"], 1)
            v.tensor_copy(pt[:, 1], ps[:, 3]).then_inc(m["cpt_d"], 1)
            dve.wait_ge(m["gb_done"], 1)
            for g in range(2):
                own(v.tensor_tensor(ccoef[:, :, 4 * g:4 * g + 4], cden[:, g].rearrange("p (i j) -> p i j", i=NI),
                                    gate_of(0)[:, :, 4 * g:4 * g + 4], ALU.mult))
            own.wait()
            for i in range(NI):
                dve.wait_ge(m["co_mm"], i + 1)
                v.tensor_tensor(ob[:, i].rearrange("p (h d) -> p h d", h=8),
                                ps[:, 4 + i].rearrange("p (h d) -> p h d", h=8),
                                ccoef[:, i].unsqueeze(2).to_broadcast([P, 8, HD]), ALU.mult).then_inc(m["co_done"], 1)
            dve.wait_ge(m["co_done"], NI)

            for s in range(STEPS):
                if s < N_ATT:
                    u = att(s)
                    G = s // 8
                    dve.wait_ge(m["s_mm"], s + 1)
                    if s >= 2:
                        dve.wait_ge(m["t_mm"], s - 1)
                    if u.branch == 0:
                        band, start = band_a[:, u.head, 256 - u.width:256], nsink[:, u.head:u.head + 1]
                    else:
                        band, start = band_b[:, u.head, S - u.width:S], 3e38
                    v.tensor_tensor_reduce(sc[:, s % 2, 0:u.width], ps[:, s % 2, 0:u.width], band, 1.0, start,
                                           ALU.add, ALU.min, row_min[:, G % 2, s % 8:s % 8 + 1]).then_inc(m["s_bias"], 1)
                    if s % 8 == 7 and u.branch == 0:
                        dve.wait_ge(m["s_bias"], s + 1)
                        v.tensor_tensor(sink_arg[:].rearrange("p (g j) -> p j g", g=2),
                                        row_min[:, G % 2].rearrange("p (j g) -> p j g", g=2),
                                        nsink[:].rearrange("p (g j) -> p j g", g=2), ALU.subtract).then_inc(m["arg_done"], 1)
                t = s - 1
                if 0 <= t < N_ATT and t % 2 == 0:
                    dve.wait_ge(m["t_mm"], t + 1)
                    if t >= 2:
                        dve.wait_ge(m["pv_mm"], t - 1)
                    w = att(t).width
                    v.tensor_copy(pt[:, 0, 0:w], ps[:, 2, 0:w]).then_inc(m["pt_d"], 1)
                G, part = divmod(s - 8, 8)
                if G >= 0 and part in (2, 3, 4):
                    i, branch = divmod(G, 3)
                    cf, dn = coef[:, G % 2], den[:, G % 2]
                    if part == 2:
                        dve.wait_ge(m["s_exp"], 8 * G + 8)
                        if branch == 0:
                            dve.wait_ge(m["sinkexp_done"], i + 1)
                            own(v.tensor_tensor(dn, dn, sink_exp[:], ALU.add))
                            own.wait()
                        own(v.reciprocal(cf, dn))
                        own.wait()
                        if branch:
                            own(v.tensor_tensor(cf, cf, gate_of(branch)[:, i], ALU.mult))
                    elif part == 3:
                        own.wait()
                        dve.wait_ge(m["pv_mm"], 8 * G + 8)
                        if branch == 0 and i:
                            dve.wait_ge(m["ytr_mm"], i)
                        if branch and G > 1:
                            dve.wait_ge(m["ob_done"], 2 * i + branch - 1)
                        heads = ps[:, 4 + G % 2].rearrange("p (h d) -> p h d", h=8)
                        dst = o_tmp if branch else oa
                        v.tensor_tensor(dst[:].rearrange("p (h d) -> p h d", h=8), heads,
                                        cf.unsqueeze(2).to_broadcast([P, 8, HD]), ALU.mult).then_inc(m["comb_done"], 1)
                    elif branch:
                        dve.wait_ge(m["comb_done"], G + 1)
                        v.tensor_tensor(ob[:, i], ob[:, i], o_tmp[:], ALU.add).then_inc(m["ob_done"], 1)
                for half in range(2):
                    i = tail_at(s - half)
                    if i is not None:
                        dve.wait_ge(m["ytr_mm"], i + 1)
                        if i:
                            dve.wait_ge(m["yl_done"], 2 * i - 1 + half)
                        z = (ZA, ZB)[half]
                        v.tensor_tensor(y_f[:, half], ps[:, 6 + half].rearrange("p (t d) -> p t d", t=4),
                                        proj[:, z:z + 4, i * P:(i + 1) * P], ALU.mult).then_inc(m["yf_done"], 1)
                    i = tail_at(s - half - 2)
                    if i is not None:
                        dve.wait_ge(m["yh_done"], 2 * i + half + 1)
                        rows = slice(4 * half, 4 * half + 4)
                        v.tensor_tensor(y_lo[:, rows, i * P:(i + 1) * P], y_f[:, half],
                                        y_hi[:, rows, i * P:(i + 1) * P].bitcast(F32), ALU.subtract).then_inc(m["yl_done"], 1)

            def residual(it, per, o, q, t, x_of, scaled=None):
                dve.wait_ge(evac, at(it, per, o + 1))
                n = o - NORM_O[q]
                v.tensor_tensor(tile_of(x_t, it, per, n), t[:, o % 2], tile_of(x_of, it, per, n),
                                ALU.add).then_inc(nrm["x_done"], 1)
                if scaled is not None:
                    dve.wait_ge(nrm["x_done"], q * KT + n + 1)
                    v.tensor_scalar(y_out[:, scaled], x_t[:, scaled], col[:, V_FIN + scaled:V_FIN + scaled + 1], None,
                                    ALU.mult).then_inc(nrm["t_done"], 1)
                dve.wait_ge(nrm["xsq_done"], at(it, per, q * KT + n + 1))
                if n or it is not None:
                    dve.wait_ge(nrm["ss_done"], at(it, per, q * (KT + 1) + n + 1))
                v.tensor_tensor(t[:, 4], t[:, 4], t[:, 2 + o % 2], ALU.add).then_inc(nrm["ss_done"], 1)

            def norm_ms(q):
                dve.wait_ge(nrm["nst_mm"], q + 1)
                v.tensor_scalar(msq[:], ps[:, 4, 0:NI], 1.0 / D, EPS, ALU.mult, ALU.add).then_inc(nrm["ms_done"], 1)

            def norm(q, gain, t, lo, hi):
                norm_ms(q)
                dve.wait_ge(nrm["nbc_mm"], q + 1)
                for k in range(KT):
                    v.scalar_tensor_tensor(out=t[:, k], in0=x_t[:, k], scalar=col[:, gain + k:gain + k + 1], in1=ps[:, 5],
                                           op0=ALU.mult, op1=ALU.mult).then_inc(nrm["t_done"], 1)
                for k in range(KT):
                    dve.wait_ge(nrm["h_done"], q * KT + k + 1)
                    v.tensor_tensor(lo[:, k], t[:, k], hi[:, k].bitcast(F32), ALU.subtract).then_inc(nrm["l_done"], 1)

            dve.wait_ge(unit_done, U_WO)
            v.memset(tt[:, 4], 0.0).then_inc(nrm["ss_done"], 1)
            with dve.Fori(0, 2) as it:
                for k in range(4):
                    dve_convert(dve, it, 4, U_WO + k + AHEAD)
                    residual(it, 4, O_WO + k, 0, tt, x_t)
            norm(0, V_MIX, t_g, g_lo, g_hi)
            own(v.tensor_scalar(lt[:, 0], decay[:], -1.0, None, ALU.mult))
            own.wait()
            own(v.tensor_tensor(lt[:, 0], lt[:, 0], decay[:], ALU.max))
            own.wait()
            v.tensor_copy(lt[:, 4], lt[:, 0]).then_inc(m["lgt_done"], 1)
            dve.wait_ge(m["lgexp_done"], 1)
            own(v.tensor_scalar(lt[:, 2], lt[:, 1], 2.0, None, ALU.add))
            own.wait()
            own(v.reciprocal(lt[:, 2], lt[:, 2]))
            own.wait()
            own(v.tensor_tensor(lt[:, 2], lt[:, 2], lt[:, 1], ALU.mult))
            own.wait()
            own(v.tensor_tensor(lt[:, 3], lt[:, 2], lt[:, 2], ALU.mult))
            own(v.memset(lg[:], 1.0 / 19))
            own.wait()
            for n in range(17, -1, -2):
                own(v.tensor_tensor(lg[:], lg[:], lt[:, 3], ALU.mult))
                own.wait()
                own(v.tensor_scalar(lg[:], lg[:], 1.0 / n, None, ALU.add))
                own.wait()
            own(v.tensor_tensor(lg[:], lg[:], lt[:, 2], ALU.mult))
            own(v.tensor_scalar(lt[:, 1], decay[:], 0.0, None, ALU.min))
            own.wait()
            own(v.scalar_tensor_tensor(out=lg[:], in0=lg[:], scalar=-2.0, in1=lt[:, 1], op0=ALU.mult, op1=ALU.add))
            own.wait()
            own(v.tensor_scalar(lg[:, 4:8], lg[:, 4:8], -1.0, None, ALU.mult))
            own(v.memset(u_pad[:, 0:1], 0.0))
            own(v.memset(u_pad[:, S + 1:S + 2], 0.0))
            with dve.Fori(0, 2) as it:
                own.begin(it, 16)
                for t in range(4):
                    ev = conv_ev[:, t % 2]
                    tap = [col_of(col, it, 4, V_CONV + 8 * n + t) for n in range(3)]
                    dve_convert(dve, it, 12, U_CONV + 3 * t + AHEAD)
                    dve_convert(dve, it, 12, U_CONV + 3 * t + 1 + AHEAD)
                    dve.wait_ge(evac, at(it, 12, O_CONV + 3 * t + 2))
                    own.wait()
                    own(v.tensor_tensor(u_pad[:, 1:S + 1], ev[:, 0], ev[:, 1], ALU.mult))
                    own.wait()
                    own(v.tensor_scalar(conv_t[:], u_pad[:, 1:S + 1], tap[1], None, ALU.mult))
                    own.wait()
                    own(v.scalar_tensor_tensor(out=conv_t[:], in0=u_pad[:, 0:S], scalar=tap[0], in1=conv_t[:],
                                               op0=ALU.mult, op1=ALU.add))
                    own.wait()
                    own(v.scalar_tensor_tensor(out=conv_t[:], in0=u_pad[:, 2:S + 2], scalar=tap[2], in1=conv_t[:],
                                               op0=ALU.mult, op1=ALU.add))
                    dve_convert(dve, it, 12, U_CONV + 3 * t + 2 + AHEAD)
                    dve.wait_ge(evac, at(it, 12, O_CONV + 3 * t + 3))
                    own.wait()
                    v.tensor_tensor(tt[:, t % 2], conv_t[:], ev[:, 2], ALU.mult).then_inc(m["af_done"], 1)
                    dve.wait_ge(m["ah_done"], at(it, 4, t + 1))
                    v.tensor_tensor(tile_of(a_lo, it, 4, t), tt[:, t % 2], tile_of(a_hi, it, 4, t).bitcast(F32),
                                    ALU.subtract).then_inc(m["al_done"], 1)
                    dve.wait_ge(m["al_done"], at(it, 4, t + 1))
                own.end(2)
            with dve.Fori(0, 4) as it:
                own.begin(it, 2)
                for t in range(2):
                    dve_convert(dve, it, 4, U_YA + 2 * t + AHEAD)
                    dve_convert(dve, it, 4, U_YA + 2 * t + 1 + AHEAD)
                    dve.wait_ge(evac, at(it, 4, O_YA + 2 * t + 2))
                    own(v.tensor_tensor(tile_of(ya, it, 2, t), tt[:, t], tt[:, 2 + t], ALU.mult))
                own.end(4)
            dve.wait_ge(m["delta_done"], 1)
            dve.wait_ge(m["tab_in"], 32)
            own.wait()
            with dve.Fori(0, RET_HEADS) as it:
                own.begin(it, 12)

                def rotate(r):
                    for n, (x0, x1, op) in enumerate(((cos_t, sin_t, ALU.subtract), (sin_t, cos_t, ALU.add))):
                        if n:
                            own.wait()
                        own(v.tensor_tensor(rot_t[:, 0], qk_raw[:, r], x0[:], ALU.mult))
                        own(v.tensor_tensor(rot_t[:, 1], qk_raw[:, r + 1], x1[:], ALU.mult))
                        own.wait()
                        ins = v.tensor_tensor(rot_o[:, n], rot_t[:, 0], rot_t[:, 1], op)
                        if n == 0:
                            own(ins)
                        else:
                            ins.then_inc(m["rot_done"], 1)

                def rest(hi, lo, base):
                    for t in range(2):
                        dve.wait_ge(m["qkh_done"], at(it, 4, base + t + 1))
                        v.tensor_tensor(lo[:, t], rot_o[:, t], hi[:, t].bitcast(F32), ALU.subtract).then_inc(m["qkl_done"], 1)

                def v_rest(t):
                    dve.wait_ge(m["vh_done"], at(it, 4, t + 1))
                    cut = slice(t * P, (t + 1) * P)
                    v.tensor_tensor(v_lo[:, :, cut], ps[:, 4 + t].rearrange("p (j e) -> p j e", j=NI),
                                    v_hi[:, :, cut].bitcast(F32), ALU.subtract).then_inc(m["vl_done"], 1)

                def p_mult(j):
                    if j >= 2:
                        dve.wait_ge(m["pl_done"], at(it, 4, j - 1))
                    dve.wait_ge(m["rs_mm"], at(it, 4, j + 1))
                    cut = (NI - 1 - j) * P
                    v.scalar_tensor_tensor(out=p_f[:, j % 2], in0=ps[:, RS_BANK[j]], scalar=0.0625,
                                           in1=strip[:, cut:cut + S], op0=ALU.mult, op1=ALU.mult).then_inc(m["pm_done"], 1)

                def p_rest(j):
                    dve.wait_ge(m["ph_done"], at(it, 4, j + 1))
                    v.tensor_tensor(p_lo[:, j], p_f[:, j % 2], p_hi[:, j].bitcast(F32), ALU.subtract).then_inc(m["pl_done"], 1)

                for k in range(8):
                    dve_convert(dve, it, 8, U_QKV + k + AHEAD)
                    if k == 0:
                        own(v.tensor_scalar(strip[:], delta[:], 0.0, col_of(lg, it, 1, 0), ALU.max, ALU.mult))
                        own(v.tensor_scalar(strip2[:], delta[:], 0.0, col_of(lg, it, 1, 4), ALU.min, ALU.mult))
                        own.wait()
                        v.tensor_tensor(strip[:], strip[:], strip2[:], ALU.add).then_inc(m["strip_done"], 1)
                    if k in (2, 4):
                        dve.wait_ge(evac, at(it, 8, O_QKV + k))
                        rotate(k - 2)
                    if k == 3:
                        rest(q_hi, q_lo, 0)
                    if k == 5:
                        rest(k_hi, k_lo, 2)
                    if k in (5, 6):
                        v_rest(k - 5)
                dve.wait_ge(m["decay_done"], at(it, 1, 1))
                p_mult(0)
                p_mult(1)
                p_rest(0)
                v_rest(2)
                p_mult(2)
                p_rest(1)
                v_rest(3)
                p_mult(3)
                p_rest(2)
                p_rest(3)
                own.end(RET_HEADS)
            with dve.Fori(0, 2) as it:
                own.begin(it, 8)
                for k in range(12):
                    hh, n = divmod(k, 6)
                    dve_convert(dve, it, 12, U_GATE + k + AHEAD)
                    if n == 1:
                        dve.wait_ge(m["mu_mm"], at(it, 2, hh + 1))
                        for t in range(4):
                            r = tile_of(ret, it, 8, 4 * hh + t)
                            v.tensor_tensor(r, r, ps[:, 4], ALU.subtract).then_inc(m["sub_done"], 1)
                    if n == 4:
                        dve.wait_ge(m["rst_mm"], at(it, 2, hh + 1))
                        v.tensor_scalar(msq[:], ps[:, 5, 0:NI], 1.0 / 512, EPS, ALU.mult, ALU.add).then_inc(m["rms2_done"], 1)
                    if n == 5:
                        dve.wait_ge(m["rbc_mm"], at(it, 2, hh + 1))
                        dve.wait_ge(evac, at(it, 12, O_GATE + 6 * hh + 6))

                        def ret_rest(t):
                            dve.wait_ge(m["rh_done"], at(it, 8, 4 * hh + t + 1))
                            v.tensor_tensor(tile_of(ret_lo, it, 8, 4 * hh + t), (val2, val3)[t % 2][:],
                                            tile_of(ret_hi, it, 8, 4 * hh + t).bitcast(F32), ALU.subtract).then_inc(m["rl_done"], 1)

                        for t in range(4):
                            own(v.scalar_tensor_tensor(out=val[:], in0=tile_of(ret, it, 8, 4 * hh + t),
                                                       scalar=col_of(col, it, 8, V_RET + 4 * hh + t), in1=ps[:, 6],
                                                       op0=ALU.mult, op1=ALU.mult))
                            own.wait()
                            if t >= 2:
                                dve.wait_ge(m["rl_done"], at(it, 8, 4 * hh + t - 1))
                            v.tensor_tensor((val2, val3)[t % 2][:], val[:], sg[:, t], ALU.mult).then_inc(m["val_done"], 1)
                            if t:
                                ret_rest(t - 1)
                            dve.wait_ge(m["val_done"], at(it, 8, 4 * hh + t + 1))
                        ret_rest(3)
                own.end(2)
            with dve.Fori(0, 2) as it:
                own.begin(it, 4)
                for k in range(8):
                    dve_convert(dve, it, 8, U_YR + k + AHEAD)
                    if k % 2:
                        t = k // 2
                        dve.wait_ge(evac, at(it, 4, O_YR + t + 1))
                        own(v.tensor_tensor(yr_t[:, t % 2], yr_t[:, t % 2], tile_of(sig_r, it, 4, t), ALU.mult))
                        own.wait()
                        v.tensor_tensor(mg_t[:], yr_t[:, t % 2], tile_of(ya, it, 4, t), ALU.add).then_inc(m["mg_done"], 1)
                        dve.wait_ge(m["mh_done"], at(it, 4, t + 1))
                        v.tensor_tensor(tile_of(m_lo, it, 4, t), mg_t[:], tile_of(m_hi, it, 4, t).bitcast(F32),
                                        ALU.subtract).then_inc(m["ml_done"], 1)
                        dve.wait_ge(m["ml_done"], at(it, 4, t + 1))
                own.end(2)
            dve.wait_ge(m["back_in"], 16)
            v.memset(tt_o[:, 4], 0.0).then_inc(nrm["ss_done"], 1)
            with dve.Fori(0, 2) as it:
                for k in range(4):
                    dve_convert(dve, it, 4, U_O + k + AHEAD)
                    residual(it, 4, O_O + k, 1, tt_o, x1_back)
            norm(1, V_FFN, t_f, f_lo, f_hi)
            with dve.Fori(0, FT // 2) as it:
                for t in range(2):
                    dve_convert(dve, it, 4, U_FF + 2 * t + AHEAD)
                    dve_convert(dve, it, 4, U_FF + 2 * t + 1 + AHEAD)
                    dve.wait_ge(evac, at(it, 4, O_FF + 2 * t + 2))
                    v.tensor_tensor(tt[:, 4], tt[:, t], tt[:, 2 + t], ALU.mult).then_inc(m["prod_done"], 1)
                    dve.wait_ge(m["fh_done"], at(it, 2, t + 1))
                    v.tensor_tensor(tile_of(act_lo, it, 2, t), tt[:, 4], tile_of(act_hi, it, 2, t).bitcast(F32),
                                    ALU.subtract).then_inc(m["fl_done"], 1)
                    dve.wait_ge(m["fl_done"], at(it, 2, t + 1))
            dve.wait_ge(m["fl_done"], FT)
            v.memset(tt[:, 4], 0.0).then_inc(nrm["ss_done"], 1)
            for k in range(3 * KT):
                t, part = divmod(k, 3)
                if k + AHEAD < 3 * KT:
                    dve_convert(dve, None, 0, U_DOWN + k + AHEAD, KT if (k + AHEAD) % 3 < 2 else FT - 2 * KT)
                if part == 2:
                    residual(None, 0, O_DOWN + t, 2, tt, x_t, scaled=t)
            norm_ms(2)
            dve.wait_ge(nrm["rs_done"], 3)
            for n, i in enumerate(FIN_ORDER):
                dve.wait_ge(m["fin_mm"], NI + n)
                v.tensor_scalar(out_tok[:, i, 512:1024], ps[:, i], rstd[:, i:i + 1], None, ALU.mult).then_inc(m["fin_d"], 1)

        @block.tensor
        def _(pe):
            def trans(dst, src, parts=P):
                return pe.transpose(dst, src, ident[0:parts, 0:parts])

            def blk(i):
                return slice(i * P, (i + 1) * P)

            def row_on_half(g, bank, cols, src, parts=P):
                wide = src.to_broadcast([parts, HD])
                if g == 0:
                    return trans(ps[0:HD, bank, cols], wide, parts)
                return pe.matmul(ps[HD:P, bank, cols], wide, ident[0:parts, 0:parts], start=True, stop=True)

            pe.wait_ge(m["consts"], 1)
            pe.wait_ge(m["vec_in"], VEC_DMAS * 16)
            trans(ps[:, 7, 0:V_CONV], vec[0:V_CONV, :], V_CONV).then_inc(m["col_t"], 1)
            pe.wait_ge(m["onehot_in"], 32)
            pe.wait_ge(m["pool_own"], 1)
            for h in range(16):
                if h >= 3:
                    pe.wait_ge(m["line_ev"], h - 2)
                pe.matmul(ps[:, 4 + h % 3, 0:LINE], rel[:, h:h + 1].to_broadcast([33, P]), onehot[:, h // 8],
                          start=True, stop=True).then_inc(m["line_mm"], 1)
            pe.wait_ge(m["x_in"], 16)
            for k in range(KT):
                if k >= 4:
                    pe.wait_ge(m["x_ev"], k - 3)
                for i in range(NI):
                    mm = trans(ps[:, k % 4, blk(i)], x_tok[:, i, blk(k)])
                mm.then_inc(m["x_tr"], 1)
            pe.wait_ge(m["line_ev"], 16)
            pe.wait_ge(m["rms_rs"], 1)

            def rows_bc(bank):
                for i in range(NI):
                    mm = trans(ps[:, bank, blk(i)], rstd[:, i:i + 1].to_broadcast([P, P]))
                return mm

            rows_bc(5).then_inc(m["rms_bc"], 1)

            def column_sums(bank, src, n, first=0):
                for q in range(n):
                    mm = pe.matmul(ps[:, bank, q:q + 1], src[:, blk(first + q)], ones1[:], start=True, stop=True)
                return mm

            pe.wait_ge(m["ada_done"], 1)
            column_sums(4, acc, 8, 8).then_inc(m["mod_mm"], 1)
            column_sums(6, acc, 8).then_inc(m["mod_mm"], 1)
            for n in range(8):
                pe_unit(pe, None, 0, n, 0, n, h_hi, h_lo, hi_sem=m["hh_done"] if n == 0 else None,
                        lo_sem=m["hl_done"] if n == 0 else None)
                if n == 3:
                    pe.wait_ge(m["vec2_in"], VEC2_DMAS * 16)
                    trans(ps[:, 7, 0:N_VEC], vec[0:N_VEC, :], N_VEC)
                    trans(ps[:, 7, P:P + 2 * CMP_T], vec2[:], 2 * CMP_T).then_inc(m["col_t"], 1)
                if n == 6:
                    pe.wait_ge(m["adag_done"], 1)
                    column_sums(6, acc_g, 8).then_inc(m["modg_mm"], 1)
            with pe.Fori(0, 2) as it:
                for k in range(8, 12):
                    pe_unit(pe, it, 4, k, 4, k, h_hi, h_lo)

            def head_stats(t):
                pe.wait_ge(m["sq_done"], t + 1)
                for i in range(NI):
                    mm = pe.matmul(ps[:, 4, 8 * t + 2 * i:8 * t + 2 * i + 2], proj[:, 20 + t % 4, blk(i)], half_sel[:],
                                   start=True, stop=True)
                mm.then_inc(m["st_mm"], 1)

            def cmp_hidden(n, c0):
                for c in range(2):
                    for q in range(CMP_T):
                        mm = pe.matmul(ps[:, 7, c0 + 64 * c:c0 + 64 * c + 64], w1[:, q, blk(c)],
                                       xp[:, q].rearrange("p g n -> p (g n)"), start=q == 0, stop=q == CMP_T - 1)
                mm.then_inc(m["c1_mm"], 1)

            pe.wait_ge(m["w1_in"], 16)
            pe.wait_ge(m["xp_done"], 1)
            cmp_hidden(0, 0)
            for n in range(16, 24):
                pe_unit(pe, None, 0, n, 0, n, h_hi, h_lo)
                if n < 19:
                    if n > 16:
                        pe.wait_ge(m["hms_done"], n - 16)
                    else:
                        pe.wait_ge(m["mod_done"], 1)
                    for t in range(*NORM_GROUPS[n - 16]):
                        head_stats(t)
                if n == 16:
                    pe.wait_ge(m["hid_done"], 1)
                    for t in range(2):
                        mm = pe.matmul(ps[:, 7, P:P + 64], w2k[:, t].rearrange("p a d -> p (a d)"), hid[:, t],
                                       start=t == 0, stop=t == 1)
                    mm.then_inc(m["c2_mm"], 1)
                if n == 17:
                    pe.wait_ge(m["kcsq_done"], 1)
                    pe.matmul(ps[0:NC_PAD, 7, 448:450], kc_sq[:], half_sel[:], start=True, stop=True).then_inc(m["kst_mm"], 1)
                if n == 19:
                    pe.wait_ge(m["krs_done"], 1)
                    for g in range(2):
                        mm = row_on_half(g, 7, slice(480, 512), kc_rs[0:NC_PAD, g:g + 1], NC_PAD)
                    mm.then_inc(m["kbc_mm"], 1)
                for t in BCAST_AT.get(n, ()):
                    pe.wait_ge(m["rw_done"], t + 1)
                    if t >= 2:
                        pe.wait_ge(m["qk_done"], t - 1)
                    for i in range(NI):
                        mm = trans(ps[:, 5 + t % 2, blk(i)], rs_bc[:, t % 2, blk(i)])
                    mm.then_inc(m["bc_mm"], 1)
                if n == 21:
                    pe.wait_ge(m["w1_in"], 32)
                    pe.wait_ge(m["xp_done"], 2)
                    pe.wait_ge(m["kcmp_done"], 2)
                    cmp_hidden(1, 192)
                if n == 22:
                    pe.wait_ge(m["hid_done"], 3)
                    for g in range(2):
                        for t in range(2):
                            mm = pe.matmul(ps[:, 7, 320 + HD * g:384 + HD * g],
                                           hid_v[:, t, g].rearrange("p j n -> p (j n)"),
                                           w2v[:, t], start=t == 0, stop=t == 1)
                    mm.then_inc(m["c2_mm"], 1)
            pe.wait_ge(m["qk_done"], 8)
            pe.wait_ge(m["kcmp_done"], 2)
            pe.wait_ge(evac, U_GB)
            for i in range(NI):
                for j in range(4):
                    c = (i % 2) * 256 + j * 2 * NC_PAD
                    mm = pe.matmul(ps[:, 2 + i // 2, c:c + 2 * NC_PAD], proj[:, QB + j, blk(i)],
                                   kcz[:].rearrange("p g n -> p (g n)"), start=True, stop=True)
            mm.then_inc(m["cs_mm"], 1)
            pe.wait_ge(m["qk_done"], len(NORM_TILES))
            for n, t in enumerate((VA, VS, VW)):
                if n == 2:
                    pe.wait_ge(m["vbd_done"], 8)
                for i in range(NI):
                    mm = trans(ps[:, 5 + n, blk(i)], proj[:, t, blk(i)])
                mm.then_inc(m["vt_mm"], 1)
            pe_unit(pe, None, 0, U_GB, 0, O_GB, h_hi, h_lo)
            pe.wait_ge(m["hms_done"], 3)
            pe.wait_ge(evac, O_GB + 1)
            for i in range(NI):
                mm = trans(ps[:, 4, blk(i)], gb_t[:, blk(i)])
            mm.then_inc(m["gb_mm"], 1)
            pe.wait_ge(m["cexp_done"], 1)
            for g in range(2):
                for i in range(NI):
                    mm = trans(ps[:, 2 + g, blk(i)], sc[:, g, blk(i)])
            mm.then_inc(m["ctr_mm"], 1)
            pe.wait_ge(m["cpt_a"], 1)
            pe.wait_ge(m["cpt_d"], 1)
            pe.wait_ge(m["gb_add"], 1)
            pe.wait_ge(m["vt_ev"], 3)
            for i in range(NI):
                for g in range(2):
                    mm = pe.matmul(ps[:, 4 + i, 256 * g:256 * g + 256], pt[:, g, blk(i)], vbd[:, g], start=True, stop=True)
                mm.then_inc(m["co_mm"], 1)

            for s in range(STEPS):
                if s < N_ATT:
                    u = att(s)
                    if s >= 2:
                        pe.wait_ge(m["s_bias"], s - 1)
                    q = (QB if u.branch else QA) + u.j
                    keys = proj[:, (KA, KS, KW)[u.branch]] if u.g else k_group0[u.branch]
                    pe.matmul(ps[:, s % 2, 0:u.width], proj[:, q, blk(u.i)],
                              keys[:, u.first_block * P:u.first_block * P + u.width],
                              start=True, stop=True).then_inc(m["s_mm"], 1)
                t = s - 3
                if 0 <= t < N_ATT:
                    u = att(t)
                    pe.wait_ge(m["pt_a" if t % 2 else "pt_d"], t // 2 + 1)
                    if t == 0:
                        pe.wait_ge(m["co_done"], NI)
                    elif t % 8 == 0 and u.group >= 2:
                        pe.wait_ge(m["comb_done"], u.group - 1)
                    v, blocks = (VA, VS, VW)[u.branch], u.width // P
                    for b in range(blocks):
                        c = (u.first_block + b) * P + u.g * HD
                        mm = pe.matmul(ps[:, 4 + u.group % 2, u.head * HD:(u.head + 1) * HD], pt[:, t % 2, blk(b)],
                                       proj[:, v, c:c + HD], start=b == 0, stop=b == blocks - 1)
                    mm.then_inc(m["pv_mm"], 1)
                t = s - 1
                if 0 <= t < N_ATT:
                    pe.wait_ge(m["s_exp"], t + 1)
                    if t == 0:
                        pe.wait_ge(m["ctr_mm"], 1)
                    if t >= 2:
                        pe.wait_ge(m["pt_a" if t % 2 else "pt_d"], t // 2)
                    for b in range(att(t).width // P):
                        mm = trans(ps[:, 2 + t % 2, blk(b)], sc[:, t % 2, blk(b)])
                    mm.then_inc(m["t_mm"], 1)
                i = tail_at(s)
                if i is not None:
                    pe.wait_ge(m["ob_done"], 2 * i + 2)
                    pe.wait_ge(m["comb_done"], 3 * i + 3)
                    if i:
                        pe.wait_ge(m["yf_done"], 2 * i)
                    for half, o in enumerate((oa, ob[:, i])):
                        for b in range(4):
                            mm = trans(ps[:, 6 + half, blk(b)], o[:, blk(b)])
                    mm.then_inc(m["ytr_mm"], 1)

            def norm_sums(q, scratch):
                pe.wait_ge(nrm["ss_done"], q * (KT + 1) + KT + 1)
                for i in range(NI):
                    mm = pe.matmul(ps[:, 4, i:i + 1], scratch[:, 4, blk(i)], ones1[:], start=True, stop=True)
                mm.then_inc(nrm["nst_mm"], 1)

            def norm(q, scratch):
                norm_sums(q, scratch)
                pe.wait_ge(nrm["rs_done"], q + 1)
                rows_bc(5).then_inc(nrm["nbc_mm"], 1)

            pe.wait_ge(m["yl_done"], 2 * NI)
            with pe.Fori(0, 2) as it:
                for k in range(4):
                    pe_unit(pe, it, 4, U_WO + k, 4, O_WO + k, y_hi, y_lo)
            norm(0, tt)
            with pe.Fori(0, 2) as it:
                for k in range(12):
                    pe_unit(pe, it, 12, U_CONV + k, 12, O_CONV + k, g_hi, g_lo,
                            hi_sem=nrm["h_done"] if k == 0 else None, lo_sem=nrm["l_done"] if k == 0 else None)
            with pe.Fori(0, 4) as it:
                for t in range(2):
                    pe_unit(pe, it, 4, U_YA + 2 * t, 4, O_YA + 2 * t, g_hi, g_lo)
                    pe_unit(pe, it, 4, U_YA + 2 * t + 1, 4, O_YA + 2 * t + 1, a_hi, a_lo,
                            hi_sem=m["ah_done"] if t == 0 else None, lo_sem=m["al_done"] if t == 0 else None)
            with pe.Fori(0, RET_HEADS) as it:
                def v_trans(t):
                    pe.wait_ge(evac, at(it, 8, O_QKV + 5 + t))
                    for j in range(NI):
                        mm = trans(ps[:, 4 + t, blk(j)], v_t[:, t % 2, blk(j)])
                    mm.then_inc(m["vtr_mm"], 1)

                def scores(j):
                    for n, (k, q) in enumerate(((k_hi, q_hi), (k_lo, q_hi), (k_hi, q_lo))):
                        for t in range(2):
                            mm = pe.matmul(ps[:, RS_BANK[j]], k[:, t, blk(j)], q[:, t], start=n == 0 and t == 0,
                                           stop=n == 2 and t == 1)
                    mm.then_inc(m["rs_mm"], 1)

                for k in range(8):
                    pe_unit(pe, it, 8, U_QKV + k, 8, O_QKV + k, g_hi, g_lo)
                    if k >= 5:
                        v_trans(k - 5)
                pe.wait_ge(m["qkl_done"], at(it, 4, 4))
                for j in range(4):
                    if j < 2:
                        pe.wait_ge(m["vl_done"], at(it, 4, j + 1))
                    scores(j)
                v_trans(3)
                pe.wait_ge(m["pm_done"], at(it, 4, 2))
                for t in range(4):
                    if t in (1, 2):
                        pe.wait_ge(m["vl_done"], at(it, 4, t + 2))
                    for n, (w, p) in enumerate(((v_hi, p_hi), (v_lo, p_hi), (v_hi, p_lo))):
                        for j in range(NI):
                            if t == 0 and n != 1:
                                pe.wait_ge(m["ph_done" if n == 0 else "pl_done"], at(it, 4, j + 1))
                            mm = pe.matmul(ps[:, PV_BANK[t]], w[:, j, blk(t)], p[:, j], start=n == 0 and j == 0,
                                           stop=n == 2 and j == NI - 1)
                    mm.then_inc(m["rpv_mm"], 1)
            with pe.Fori(0, 2) as it:
                for k in range(12):
                    hh, n = divmod(k, 6)
                    pe_unit(pe, it, 12, U_GATE + k, 12, O_GATE + k, g_hi, g_lo)
                    if n == 0:
                        pe.wait_ge(m["hsum_done"], at(it, 2, hh + 1))
                        pe.matmul(ps[:, 4], mean512[:], head_sum[:], start=True, stop=True).then_inc(m["mu_mm"], 1)
                    if n == 3:
                        pe.wait_ge(m["hssq_done"], at(it, 2, hh + 1))
                        column_sums(5, head_ssq, NI).then_inc(m["rst_mm"], 1)
                    if n == 5:
                        pe.wait_ge(m["rrs_done"], at(it, 2, hh + 1))
                        rows_bc(6).then_inc(m["rbc_mm"], 1)
            with pe.Fori(0, 2) as it:
                for k in range(8):
                    half = k % 2
                    pe_unit(pe, it, 8, U_YR + k, 4, O_YR + k // 2, ret_hi, ret_lo, k0=8 * half, first=half == 0,
                            last=half == 1, hi_sem=m["rh_done"] if k < 2 else None, lo_sem=m["rl_done"] if k < 2 else None)
            with pe.Fori(0, 2) as it:
                for k in range(4):
                    pe_unit(pe, it, 4, U_O + k, 4, O_O + k, m_hi, m_lo,
                            hi_sem=m["mh_done"] if k == 0 else None, lo_sem=m["ml_done"] if k == 0 else None)
            norm(1, tt_o)
            with pe.Fori(0, FT // 2) as it:
                for k in range(4):
                    pe_unit(pe, it, 4, U_FF + k, 4, O_FF + k, f_hi, f_lo,
                            hi_sem=nrm["h_done"] if k == 0 else None, lo_sem=nrm["l_done"] if k == 0 else None,
                            base=KT)
            with pe.Fori(0, 2) as it:
                for k in range(12):
                    t, part = divmod(k, 3)
                    pe_unit(pe, it, 12, U_DOWN + k, 4, O_DOWN + t, act_hi, act_lo, KT if part < 2 else FT - 2 * KT,
                            8 * part, part == 0, part == 2, hi_sem=m["fh_done"] if k < 3 else None,
                            lo_sem=m["fl_done"] if k < 3 else None)
            def back(half, i):
                for k in range(4):
                    mm = trans(ps[:, 4 * (1 - half) + i, blk(k)], y_out[:, 4 * half + k, blk(i)])
                mm.then_inc(m["fin_mm"], 1)

            pe.wait_ge(nrm["t_done"], 2 * KT + 4)
            for i in FIN_ORDER[:3]:
                back(0, i)
            norm_sums(2, tt)
            pe.wait_ge(nrm["t_done"], 3 * KT)
            pe.wait_ge(evac, N_OUTS)
            for i in FIN_ORDER:
                back(1, i)
            pe.wait_ge(nrm["ms_done"], 3)
            back(0, FIN_ORDER[3])


_INS = ['x', 'c', 'w_ada', 'b_ada', 'norm_gain', 'w_in', 'b_nsa_gate', 'q_gain_a', 'k_gain_a', 'sinks', 'q_gain_b',
        'k_gain_cmp', 'k_gain_sel', 'k_gain_win', 'cmp_pos_k', 'cmp_pos_v', 'w_cmp_k1', 'w_cmp_k2', 'w_cmp_v1',
        'w_cmp_v2', 'w_out', 'rel_bias', 'g_mix_2', 'w_in_2', 'w_conv_2', 'dec_f_2', 'dec_b_2', 'g_ret_2',
        'w_a_out_2', 'w_r_out_2', 'w_o_2', 'g_ffn_2', 'w_ff_gate_2', 'w_ff_up_2', 'w_ff_down_2', 'g_final_2']
_OUTS = [((1, S, D), 'float32')]


def bias_onehot_table():
    dist = 255 - np.arange(LINE)
    near = np.maximum(dist, 0)
    far = 16 + (np.log(np.maximum(near, 1).astype(np.float32) / np.float32(16)) / np.log(8.0) * 16).astype(np.int32)
    bucket = np.where(near < 16, near, np.minimum(far, 31))
    table = np.zeros((33, 2, LINE), np.float32)
    for q, allowed in enumerate(((dist >= 0) & (dist < 128), dist >= 0)):
        for x in range(LINE):
            if allowed[x]:
                table[bucket[x], q, x] = -1.0
            else:
                table[32, q, x] = 1.0
    return table


def rope_tables():
    pos = np.arange(S, dtype=np.float32)
    freqs = np.power(np.float32(10000.0), -np.arange(0, 256, 2, dtype=np.float32) / np.float32(256))
    ang = (pos[None, :] * freqs[:, None].astype(np.float32)).astype(np.float32)
    return np.cos(ang).astype(np.float32), np.sin(ang).astype(np.float32)


def kernel(**inputs):
    import numpy as _np
    import concourse.bacc as _bacc
    from concourse import mybir as _mybir
    from concourse.bass_utils import run_bass_kernel_spmd as _run

    nc = _bacc.Bacc("TRN2", target_bir_lowering=False, num_devices=1)
    arrays, args = {}, []
    cos, sin = rope_tables()
    shape_only = [("bias_onehot", bias_onehot_table()), ("rope_cos", cos), ("rope_sin", sin)]
    for name, value in [(name, inputs[name]) for name in _INS] + shape_only:
        a = _np.ascontiguousarray(value)
        arrays[f"in_{name}_dram"] = a
        args.append(nc.dram_tensor(f"in_{name}_dram", a.shape, _mybir.dt.from_np(a.dtype), kind="ExternalInput").ap())
    for i, (shape, dtype) in enumerate(_OUTS):
        dt = _mybir.dt.from_np(_np.dtype(dtype))
        args.append(nc.dram_tensor(f"out_{i}_dram", shape, dt, kind="ExternalOutput").ap())
    hybrid_block(nc, *args)
    r = _run(nc, [arrays], core_ids=[0])
    return r.results[0]["out_0_dram"]
```
